# Optimizing a Trainium2 kernel written in Bass

```python
import jax
import jax.numpy as jnp
from jax import lax
import numpy as np

D_MODEL = 1024
BATCH = 1
SEQ = 256
DEPTH = 2

RMS_EPS = 1e-6
MIX_W = D_MODEL
A_HEADS = 4
A_HEAD_K = 128
A_HEAD_V = MIX_W // 2 // A_HEADS
A_KW = A_HEADS * A_HEAD_K
A_W = A_HEADS * A_HEAD_V
HGRN_CHUNK = 64
B_GROUPS = 4
B_W = MIX_W // 2
B_GROUP_DIM = B_W // B_GROUPS
GMLP_CHUNK = 128
EVEN_IN = 2 * A_KW + 2 * A_W + 2 * B_W
C_HEADS = 4
Q_LORA = 256
KV_LORA = 128
C_NOPE = 128
C_ROPE = 64
C_QK = C_NOPE + C_ROPE
C_V = MIX_W // 2 // C_HEADS
C_W = C_HEADS * C_V
ROPE_THETA = 10000.0
ATTN_Q_BLOCK = 128
D_HEADS = 4
D_HEAD_DIM = MIX_W // 2 // D_HEADS
D_W = D_HEADS * D_HEAD_DIM
MOBA_BLOCK = 256
MOBA_TOPK = 3
MOBA_Q_CHUNK = 64
ODD_IN = Q_LORA + KV_LORA + C_ROPE + 3 * D_W
PEER_HEADS = 8
PEER_N_KEYS = 128
PEER_N_EXPERTS = PEER_N_KEYS * PEER_N_KEYS
PEER_TOPK = 16
PEER_HALF = 128
PEER_QDIM = 2 * PEER_HALF
PEER_CHUNK = 128


def rmsnorm(x, g):
    xf = x.astype(jnp.float32)
    y = xf * lax.rsqrt(jnp.mean(xf * xf, axis=-1, keepdims=True) + RMS_EPS)
    return y.astype(x.dtype) * g

def split_cols(z, sizes):
    cuts = [int(c) for c in np.cumsum(sizes)[:-1]]
    return jnp.split(z, cuts, axis=-1)

def rope(x, positions):
    half = x.shape[-1] // 2
    inv_freq = ROPE_THETA ** (-jnp.arange(half, dtype=jnp.float32) / half)
    ang = positions.astype(jnp.float32)[..., None] * inv_freq
    cos = jnp.cos(ang)[:, :, None, :]
    sin = jnp.sin(ang)[:, :, None, :]
    x1 = x[..., :half].astype(jnp.float32)
    x2 = x[..., half:].astype(jnp.float32)
    return jnp.concatenate([x1 * cos - x2 * sin, x2 * cos + x1 * sin], axis=-1).astype(x.dtype)

def hgrn_lower_bounds(lb_logits):
    p = jax.nn.softmax(lb_logits.astype(jnp.float32), axis=0)
    return jnp.cumsum(p, axis=0)[:DEPTH]

def hgrn2_recurrence(q, k, v, log_f):
    B, S, H, dk = q.shape
    dv = v.shape[-1]
    nc = S // HGRN_CHUNK

    def chunks(t):
        return t.reshape(B, nc, HGRN_CHUNK, H, t.shape[-1]).transpose(1, 0, 3, 2, 4)

    causal = jnp.tril(jnp.ones((HGRN_CHUNK, HGRN_CHUNK), dtype=bool))[:, :, None]

    def step(state, inp):
        qi, ki, vi, gi = inp
        b = jnp.cumsum(gi.astype(jnp.float32), axis=2)
        o_inter = jnp.einsum('bhtk,bhkv->bhtv', qi * jnp.exp(b), state)
        diff = b[:, :, :, None, :] - b[:, :, None, :, :]
        decay = jnp.exp(jnp.where(causal, diff, -jnp.inf))
        scores = jnp.einsum('bhtk,bhsk,bhtsk->bhts', qi, ki, decay)
        o = o_inter + jnp.einsum('bhts,bhsv->bhtv', scores, vi)
        b_last = b[:, :, -1:, :]
        k_dec = ki * jnp.exp(b_last - b)
        state = jnp.exp(b_last[:, :, 0, :])[..., None] * state + jnp.einsum('bhsk,bhsv->bhkv', k_dec, vi)
        return state, o

    state0 = jnp.zeros((B, H, dk, dv), jnp.float32)
    _, o = lax.scan(step, state0, (chunks(q), chunks(k), chunks(v), chunks(log_f)))
    return o.transpose(1, 0, 3, 2, 4).reshape(B, S, H, dv)

def causal_attention(q, k, v, scale):
    B, H, S, dqk = q.shape
    nq = S // ATTN_Q_BLOCK
    qb = q.reshape(B, H, nq, ATTN_Q_BLOCK, dqk).transpose(2, 0, 1, 3, 4)
    k_pos = jnp.arange(S)

    def block(args):
        i, qi = args
        s = jnp.einsum('bhqd,bhkd->bhqk', qi, k).astype(jnp.float32) * scale
        q_pos = i * ATTN_Q_BLOCK + jnp.arange(ATTN_Q_BLOCK)
        s = jnp.where(k_pos[None, :] <= q_pos[:, None], s, -jnp.inf)
        p = jax.nn.softmax(s, axis=-1).astype(v.dtype)
        return jnp.einsum('bhqk,bhkd->bhqd', p, v)

    o = lax.map(block, (jnp.arange(nq), qb))
    return o.transpose(1, 2, 0, 3, 4).reshape(B, H, S, v.shape[-1])

def moba_attention(q, k, v, scale):
    B, H, S, d = q.shape
    nb = -(-S // MOBA_BLOCK)
    sp = nb * MOBA_BLOCK
    pad = ((0, 0), (0, 0), (0, sp - S), (0, 0))
    q, k, v = jnp.pad(q, pad), jnp.pad(k, pad), jnp.pad(v, pad)
    kb = k.reshape(B, H, nb, MOBA_BLOCK, d)
    vb = v.reshape(B, H, nb, MOBA_BLOCK, d)
    k_mean = jnp.mean(kb.astype(jnp.float32), axis=3)
    gate = jnp.einsum('bhsd,bhnd->bhsn', q.astype(jnp.float32), k_mean)
    q_block = jnp.arange(sp) // MOBA_BLOCK
    past = jnp.arange(nb)[None, :] < q_block[:, None]
    gate = jnp.where(past, gate, -jnp.inf)
    topk = min(MOBA_TOPK, nb)
    _, sel = lax.top_k(gate, topk)
    valid = sel < q_block[:, None]
    nqc = sp // MOBA_Q_CHUNK

    def chunks(t):
        return t.reshape(B, H, nqc, MOBA_Q_CHUNK, t.shape[-1]).transpose(2, 0, 1, 3, 4)

    b_idx = jnp.arange(B)[:, None, None, None]
    h_idx = jnp.arange(H)[None, :, None, None]

    def chunk(args):
        i, qi, si, vi_ = args
        k_sel = kb[b_idx, h_idx, si]
        v_sel = vb[b_idx, h_idx, si]
        s_sel = jnp.einsum('bhqd,bhqnkd->bhqnk', qi, k_sel).astype(jnp.float32) * scale
        s_sel = jnp.where(vi_[..., None], s_sel, -jnp.inf).reshape(B, H, MOBA_Q_CHUNK, topk * MOBA_BLOCK)
        j = (i * MOBA_Q_CHUNK) // MOBA_BLOCK
        k_own = lax.dynamic_index_in_dim(kb, j, axis=2, keepdims=False)
        v_own = lax.dynamic_index_in_dim(vb, j, axis=2, keepdims=False)
        s_own = jnp.einsum('bhqd,bhkd->bhqk', qi, k_own).astype(jnp.float32) * scale
        q_pos = i * MOBA_Q_CHUNK + jnp.arange(MOBA_Q_CHUNK)
        k_pos = j * MOBA_BLOCK + jnp.arange(MOBA_BLOCK)
        s_own = jnp.where(k_pos[None, :] <= q_pos[:, None], s_own, -jnp.inf)
        p = jax.nn.softmax(jnp.concatenate([s_sel, s_own], axis=-1), axis=-1).astype(v.dtype)
        p_sel = p[..., :topk * MOBA_BLOCK].reshape(B, H, MOBA_Q_CHUNK, topk, MOBA_BLOCK)
        p_own = p[..., topk * MOBA_BLOCK:]
        return (jnp.einsum('bhqnk,bhqnkd->bhqd', p_sel, v_sel)
                + jnp.einsum('bhqk,bhkd->bhqd', p_own, v_own))

    o = lax.map(chunk, (jnp.arange(nqc), chunks(q), chunks(sel), chunks(valid)))
    return o.transpose(1, 2, 0, 3, 4).reshape(B, H, sp, d)[:, :, :S]

def hgrn_gmlp_mixer(x, lb, norm_mix, w_in, hgrn_out_norm, gmlp_v_norm, gmlp_w_s, gmlp_b_s, w_out):
    B, S, _ = x.shape
    xn = rmsnorm(x, norm_mix)
    q, fg, inp, og, u, v = split_cols(xn @ w_in, [A_KW, A_KW, A_W, A_W, B_W, B_W])
    f = lb + (1.0 - lb) * jax.nn.sigmoid(fg.astype(jnp.float32))
    o = hgrn2_recurrence(q.reshape(B, S, A_HEADS, A_HEAD_K),
                         (1.0 - f).reshape(B, S, A_HEADS, A_HEAD_K),
                         jax.nn.silu(inp).reshape(B, S, A_HEADS, A_HEAD_V),
                         jnp.log(f).reshape(B, S, A_HEADS, A_HEAD_K))
    o = rmsnorm(o.astype(x.dtype), hgrn_out_norm.reshape(A_HEADS, A_HEAD_V))
    out_a = o.reshape(B, S, A_W) * jax.nn.silu(og)
    u = jax.nn.gelu(u)
    v = rmsnorm(jax.nn.gelu(v).reshape(B, S, B_GROUPS, B_GROUP_DIM),
                gmlp_v_norm.reshape(B_GROUPS, B_GROUP_DIM))
    nc = S // GMLP_CHUNK
    w_causal = gmlp_w_s * jnp.tril(jnp.ones((GMLP_CHUNK, GMLP_CHUNK), gmlp_w_s.dtype))
    sv = jnp.einsum('gts,bnsgd->bntgd', w_causal, v.reshape(B, nc, GMLP_CHUNK, B_GROUPS, B_GROUP_DIM))
    sv = sv + gmlp_b_s.T[:, :, None]
    out_b = u * sv.reshape(B, S, B_W)
    return jnp.concatenate([out_a, out_b], axis=-1) @ w_out

def mla_moba_mixer(x, positions, norm_mix, w_in, cq_norm, ckv_norm, w_uq, w_ukv,
                   mla_q_norm, mla_k_norm, moba_q_norm, moba_k_norm, w_out):
    B, S, _ = x.shape
    xn = rmsnorm(x, norm_mix)
    c_q, c_kv, k_pe, q_d, k_d, v_d = split_cols(xn @ w_in, [Q_LORA, KV_LORA, C_ROPE, D_W, D_W, D_W])
    q_c = (rmsnorm(c_q, cq_norm) @ w_uq).reshape(B, S, C_HEADS, C_QK)
    kv_c = (rmsnorm(c_kv, ckv_norm) @ w_ukv).reshape(B, S, C_HEADS, C_NOPE + C_V)
    k_c = jnp.concatenate([kv_c[..., :C_NOPE],
                           jnp.broadcast_to(k_pe[:, :, None, :], (B, S, C_HEADS, C_ROPE))], axis=-1)
    v_c = kv_c[..., C_NOPE:]
    q_c = rmsnorm(q_c, mla_q_norm)
    k_c = rmsnorm(k_c, mla_k_norm)
    q_c = jnp.concatenate([q_c[..., :C_NOPE], rope(q_c[..., C_NOPE:], positions)], axis=-1)
    k_c = jnp.concatenate([k_c[..., :C_NOPE], rope(k_c[..., C_NOPE:], positions)], axis=-1)
    o_c = causal_attention(q_c.transpose(0, 2, 1, 3), k_c.transpose(0, 2, 1, 3),
                           v_c.transpose(0, 2, 1, 3), C_QK ** -0.5)
    out_c = o_c.transpose(0, 2, 1, 3).reshape(B, S, C_W)
    q_d = rmsnorm(q_d.reshape(B, S, D_HEADS, D_HEAD_DIM), moba_q_norm)
    k_d = rmsnorm(k_d.reshape(B, S, D_HEADS, D_HEAD_DIM), moba_k_norm)
    v_d = v_d.reshape(B, S, D_HEADS, D_HEAD_DIM)
    o_d = moba_attention(q_d.transpose(0, 2, 1, 3), k_d.transpose(0, 2, 1, 3),
                         v_d.transpose(0, 2, 1, 3), D_HEAD_DIM ** -0.5)
    out_d = o_d.transpose(0, 2, 1, 3).reshape(B, S, D_W)
    return jnp.concatenate([out_c, out_d], axis=-1) @ w_out

def peer_ffn(x, norm_ffn, w_query, sub_keys, expert_down, expert_up):
    B, S, D = x.shape
    xn = rmsnorm(x, norm_ffn)
    nt = S // PEER_CHUNK
    xc = xn.reshape(B, nt, PEER_CHUNK, D).transpose(1, 0, 2, 3)

    def chunk(xi):
        q = (xi @ w_query).reshape(B, PEER_CHUNK, PEER_HEADS, 2, PEER_HALF)
        s = jnp.einsum('bthpd,hpnd->bthpn', q, sub_keys)
        s1, i1 = lax.top_k(s[..., 0, :], PEER_TOPK)
        s2, i2 = lax.top_k(s[..., 1, :], PEER_TOPK)
        cand = (s1[..., :, None] + s2[..., None, :]).reshape(B, PEER_CHUNK, PEER_HEADS, PEER_TOPK * PEER_TOPK)
        top_s, top_c = lax.top_k(cand, PEER_TOPK)
        idx = (jnp.take_along_axis(i1, top_c // PEER_TOPK, axis=-1) * PEER_N_KEYS
               + jnp.take_along_axis(i2, top_c % PEER_TOPK, axis=-1))
        g = jax.nn.softmax(top_s.astype(jnp.float32), axis=-1)
        u = jnp.take(expert_down, idx, axis=0)
        act = jax.nn.gelu(jnp.einsum('btd,bthkd->bthk', xi, u).astype(jnp.float32))
        v_sel = jnp.take(expert_up, idx, axis=0)
        return jnp.einsum('bthk,bthkd->btd', (g * act).astype(xi.dtype), v_sel)

    out = lax.map(chunk, xc)
    return out.transpose(1, 0, 2, 3).reshape(B, S, D)

def first_inputs(seed: int = 0) -> dict:
    key = jax.random.key(seed)
    ks = iter(jax.random.split(key, 64))

    def nrm(shape, scale):
        return jax.random.normal(next(ks), shape, jnp.float32) * scale

    def gain(n):
        return 1.0 + 0.1 * jax.random.normal(next(ks), (n,), jnp.float32)

    d = D_MODEL
    inp = {}
    inp['x'] = nrm((BATCH, SEQ, d), 1.0)
    inp['positions'] = jnp.broadcast_to(jnp.arange(SEQ, dtype=jnp.int32), (BATCH, SEQ))
    inp['lb_logits'] = nrm((DEPTH + 1, A_KW), 0.5)
    inp['l0_norm_mix'] = gain(d)
    inp['l0_w_in'] = nrm((d, EVEN_IN), d ** -0.5)
    inp['l0_hgrn_out_norm'] = gain(A_W)
    inp['l0_gmlp_v_norm'] = gain(B_W)
    inp['l0_gmlp_w_s'] = nrm((B_GROUPS, GMLP_CHUNK, GMLP_CHUNK), GMLP_CHUNK ** -0.5)
    inp['l0_gmlp_b_s'] = 1.0 + nrm((B_GROUPS, GMLP_CHUNK), 0.1)
    inp['l0_w_out'] = nrm((A_W + B_W, d), (A_W + B_W) ** -0.5)
    inp['l0_norm_ffn'] = gain(d)
    inp['l0_peer_w_query'] = nrm((d, PEER_HEADS * PEER_QDIM), d ** -0.5)
    inp['l0_peer_sub_keys'] = nrm((PEER_HEADS, 2, PEER_N_KEYS, PEER_HALF), PEER_HALF ** -0.5)
    inp['l0_peer_expert_down'] = nrm((PEER_N_EXPERTS, d), d ** -0.5)
    inp['l0_peer_expert_up'] = nrm((PEER_N_EXPERTS, d), 0.25)
    inp['l1_norm_mix'] = gain(d)
    inp['l1_w_in'] = nrm((d, ODD_IN), d ** -0.5)
    inp['l1_mla_cq_norm'] = gain(Q_LORA)
    inp['l1_mla_ckv_norm'] = gain(KV_LORA)
    inp['l1_mla_w_uq'] = nrm((Q_LORA, C_HEADS * C_QK), Q_LORA ** -0.5)
    inp['l1_mla_w_ukv'] = nrm((KV_LORA, C_HEADS * (C_NOPE + C_V)), KV_LORA ** -0.5)
    inp['l1_mla_q_norm'] = gain(C_QK)
    inp['l1_mla_k_norm'] = gain(C_QK)
    inp['l1_moba_q_norm'] = gain(D_HEAD_DIM)
    inp['l1_moba_k_norm'] = gain(D_HEAD_DIM)
    inp['l1_w_out'] = nrm((C_W + D_W, d), (C_W + D_W) ** -0.5)
    inp['l1_norm_ffn'] = gain(d)
    inp['l1_peer_w_query'] = nrm((d, PEER_HEADS * PEER_QDIM), d ** -0.5)
    inp['l1_peer_sub_keys'] = nrm((PEER_HEADS, 2, PEER_N_KEYS, PEER_HALF), PEER_HALF ** -0.5)
    inp['l1_peer_expert_down'] = nrm((PEER_N_EXPERTS, d), d ** -0.5)
    inp['l1_peer_expert_up'] = nrm((PEER_N_EXPERTS, d), 0.25)
    return inp

def first_block(x, positions, lb_logits,
              l0_norm_mix, l0_w_in, l0_hgrn_out_norm, l0_gmlp_v_norm, l0_gmlp_w_s, l0_gmlp_b_s, l0_w_out,
              l0_norm_ffn, l0_peer_w_query, l0_peer_sub_keys, l0_peer_expert_down, l0_peer_expert_up,
              l1_norm_mix, l1_w_in, l1_mla_cq_norm, l1_mla_ckv_norm, l1_mla_w_uq, l1_mla_w_ukv,
              l1_mla_q_norm, l1_mla_k_norm, l1_moba_q_norm, l1_moba_k_norm, l1_w_out,
              l1_norm_ffn, l1_peer_w_query, l1_peer_sub_keys, l1_peer_expert_down, l1_peer_expert_up):
    lbs = hgrn_lower_bounds(lb_logits)
    mixer_params = [
        (lbs[0], l0_norm_mix, l0_w_in, l0_hgrn_out_norm, l0_gmlp_v_norm, l0_gmlp_w_s, l0_gmlp_b_s, l0_w_out),
        (positions, l1_norm_mix, l1_w_in, l1_mla_cq_norm, l1_mla_ckv_norm, l1_mla_w_uq, l1_mla_w_ukv,
         l1_mla_q_norm, l1_mla_k_norm, l1_moba_q_norm, l1_moba_k_norm, l1_w_out),
    ]
    ffn_params = [
        (l0_norm_ffn, l0_peer_w_query, l0_peer_sub_keys, l0_peer_expert_down, l0_peer_expert_up),
        (l1_norm_ffn, l1_peer_w_query, l1_peer_sub_keys, l1_peer_expert_down, l1_peer_expert_up),
    ]
    for layer in range(DEPTH):
        mixer = hgrn_gmlp_mixer if layer % 2 == 0 else mla_moba_mixer
        x = x + mixer(x, *mixer_params[layer])
        x = x + peer_ffn(x, *ffn_params[layer])
    return x


GRID_W = 64
CTX_LEN = 256
N_MOD = 9
D_FF = 2816
A_HEADS_2 = 8
A_KV_HEADS = 2
A_HEAD_DIM = 64
WINDOW = 128
BLOCK = WINDOW
ROPE_BASE = 10000.0
B_HEADS = 4
B_DK = 64
B_DV = 128
B_GATE_RANK = 16
B_GATE_NORM = 16.0
B_CHUNK = 64
POOL_WINDOWS = (2, 4, 8, 16)
POOL_GROUP = D_MODEL // len(POOL_WINDOWS)
A_Q = A_HEADS_2 * A_HEAD_DIM
A_KV = A_KV_HEADS * A_HEAD_DIM
B_QK = B_HEADS * B_DK
B_V = B_HEADS * B_DV
PROJ_SIZES = (A_Q, A_KV, A_KV, B_QK, B_QK, B_V, B_V, 2 * B_GATE_RANK)
PROJ_DIM = A_Q + 2 * A_KV + 2 * B_QK + 2 * B_V + 2 * B_GATE_RANK
MIX_OUT = A_Q + B_V


def rmsnorm_2(x, g):
    x32 = x.astype(jnp.float32)
    y = x32 * lax.rsqrt(jnp.mean(x32 * x32, axis=-1, keepdims=True) + RMS_EPS)
    return y.astype(x.dtype) * g

def adaln(cond, w, b):
    mm = jax.nn.silu(cond) @ w + b
    mm = mm.reshape(mm.shape[:-1] + (N_MOD, mm.shape[-1] // N_MOD))
    return [mm[..., i, None, :] for i in range(N_MOD)]

def modulate(z, g, shift, scale):
    return rmsnorm_2(z, g) * (1.0 + scale) + shift

def swiglu(h, wi, wo):
    a, u = jnp.split(h @ wi, 2, axis=-1)
    return (jax.nn.silu(a) * u) @ wo

def _rotate(x, pos):
    n = x.shape[-1] // 2
    freqs = ROPE_BASE ** (-jnp.arange(n, dtype=jnp.float32) / n)
    ang = pos[:, None] * freqs
    cos = jnp.cos(ang)[:, None, :].astype(x.dtype)
    sin = jnp.sin(ang)[:, None, :].astype(x.dtype)
    x1, x2 = x[..., :n], x[..., n:]
    return jnp.concatenate([x1 * cos - x2 * sin, x2 * cos + x1 * sin], axis=-1)

def axial_rope(x, rows, cols):
    half = x.shape[-1] // 2
    return jnp.concatenate([_rotate(x[..., :half], rows), _rotate(x[..., half:], cols)], axis=-1)

def window_attention(q, k, v, kc, vc, sink):
    B, T, Hq, d = q.shape
    G = k.shape[2]
    R = Hq // G
    nb = T // BLOCK
    L = kc.shape[1]
    scale = d ** -0.5
    qb = q.reshape(B, nb, BLOCK, G, R, d)

    def band(a):
        ap = jnp.pad(a, ((0, 0), (BLOCK, BLOCK), (0, 0), (0, 0))).reshape(B, nb + 2, BLOCK, G, d)
        return jnp.concatenate([ap[:, :nb], ap[:, 1:nb + 1], ap[:, 2:]], axis=2)

    kb, vb = band(k), band(v)
    s_band = jnp.einsum('bnigrd,bnjgd->bgrnij', qb, kb).astype(jnp.float32) * scale
    s_ctx = jnp.einsum('bnigrd,blgd->bgrnil', qb, kc).astype(jnp.float32) * scale
    qpos = jnp.arange(nb)[:, None, None] * BLOCK + jnp.arange(BLOCK)[None, :, None]
    kpos = jnp.arange(nb)[:, None, None] * BLOCK - BLOCK + jnp.arange(3 * BLOCK)[None, None, :]
    valid = (kpos >= 0) & (kpos < T) & (jnp.abs(kpos - qpos) <= WINDOW)
    s_band = jnp.where(valid, s_band, -jnp.inf)
    sink_l = jnp.broadcast_to(sink.astype(jnp.float32).reshape(1, G, R, 1, 1, 1), s_band.shape[:-1] + (1,))
    p = jax.nn.softmax(jnp.concatenate([s_band, s_ctx, sink_l], axis=-1), axis=-1)
    nk = 3 * BLOCK
    o = (jnp.einsum('bgrnij,bnjgd->bnigrd', p[..., :nk].astype(vb.dtype), vb)
         + jnp.einsum('bgrnil,blgd->bnigrd', p[..., nk:nk + L].astype(vc.dtype), vc))
    return o.reshape(B, T, Hq * d)

def context_attention(qc, kc, vc, sink):
    B, L, Hq, d = qc.shape
    G = kc.shape[2]
    R = Hq // G
    s = jnp.einsum('blgrd,bmgd->bgrlm', qc.reshape(B, L, G, R, d), kc).astype(jnp.float32) * d ** -0.5
    sink_l = jnp.broadcast_to(sink.astype(jnp.float32).reshape(1, G, R, 1, 1), s.shape[:-1] + (1,))
    p = jax.nn.softmax(jnp.concatenate([s, sink_l], axis=-1), axis=-1)
    o = jnp.einsum('bgrlm,bmgd->blgrd', p[..., :L].astype(vc.dtype), vc)
    return o.reshape(B, L, Hq * d)

def gla_chunked(q, k, v, log_a, s0):
    B, T, H, dk = q.shape
    C = B_CHUNK
    n = T // C
    f32 = jnp.float32

    def chunks(a):
        return a.astype(f32).reshape(B, n, C, H, a.shape[-1])

    qc_ = chunks(q) * dk ** -0.5
    kc_ = chunks(k)
    vc_ = chunks(v)
    g = jnp.cumsum(chunks(log_a), axis=2)
    g_last = g[:, :, -1:]
    q_t = qc_ * jnp.exp(g)
    k_t = kc_ * jnp.exp(-g)
    k_end = kc_ * jnp.exp(g_last - g)
    lower = jnp.tril(jnp.ones((C, C), dtype=bool))
    att = jnp.where(lower, jnp.einsum('bnihd,bnjhd->bnhij', q_t, k_t), 0.0)
    o = jnp.einsum('bnhij,bnjhv->bnihv', att, vc_)
    d_state = jnp.einsum('bnjhd,bnjhv->bnhdv', k_end, vc_)
    decay = jnp.exp(g_last[:, :, 0])

    def step(S, inp):
        dec, ds = inp
        return dec[..., None] * S + ds, S

    s_final, s_prev = lax.scan(step, s0, (jnp.moveaxis(decay, 1, 0), jnp.moveaxis(d_state, 1, 0)))
    s_prev = jnp.moveaxis(s_prev, 0, 1)
    o = o + jnp.einsum('bnihd,bnhdv->bnihv', q_t, s_prev)
    return o.reshape(B, T, H, v.shape[-1]).astype(q.dtype), s_final

def bidir_gla(q, k, v, la_f, la_b, qc, kc, vc, lac_f, lac_b):
    flip = lambda a: a[:, ::-1]
    B = q.shape[0]
    zeros = jnp.zeros((B, B_HEADS, B_DK, B_DV), jnp.float32)
    oc_f, sc_f = gla_chunked(qc, kc, vc, lac_f, zeros)
    oc_b, sc_b = gla_chunked(flip(qc), flip(kc), flip(vc), flip(lac_b), zeros)
    o_f, _ = gla_chunked(q, k, v, la_f, sc_f)
    o_b, _ = gla_chunked(flip(q), flip(k), flip(v), flip(la_b), sc_b)
    return o_f + flip(o_b), oc_f + flip(oc_b)

def gla_output(o, r, gla_g):
    B, T = o.shape[:2]
    return rmsnorm_2(o, gla_g).reshape(B, T, B_V) * jax.nn.silu(r)

def mixer_ab(h, hc, rows, cols, need_ctx_out, w_in, w_a2_f, b_a_f, w_a2_b, b_a_b, sink, gla_g, w_out):
    split_points = [int(s) for s in np.cumsum(PROJ_SIZES)[:-1]]

    def project(z):
        Bz, Tz = z.shape[:2]
        qa, ka, va, qb, kb, vb, rb, zg = jnp.split(z @ w_in, split_points, axis=-1)
        la_f = jax.nn.log_sigmoid((zg[..., :B_GATE_RANK] @ w_a2_f + b_a_f).astype(jnp.float32)) / B_GATE_NORM
        la_b = jax.nn.log_sigmoid((zg[..., B_GATE_RANK:] @ w_a2_b + b_a_b).astype(jnp.float32)) / B_GATE_NORM
        return (qa.reshape(Bz, Tz, A_HEADS_2, A_HEAD_DIM),
                ka.reshape(Bz, Tz, A_KV_HEADS, A_HEAD_DIM),
                va.reshape(Bz, Tz, A_KV_HEADS, A_HEAD_DIM),
                qb.reshape(Bz, Tz, B_HEADS, B_DK),
                kb.reshape(Bz, Tz, B_HEADS, B_DK),
                vb.reshape(Bz, Tz, B_HEADS, B_DV),
                rb,
                la_f.reshape(Bz, Tz, B_HEADS, B_DK),
                la_b.reshape(Bz, Tz, B_HEADS, B_DK))

    qa, ka, va, qb, kb, vb, rb, la_f, la_b = project(h)
    cqa, cka, cva, cqb, ckb, cvb, crb, cla_f, cla_b = project(hc)
    o_a = window_attention(axial_rope(qa, rows, cols), axial_rope(ka, rows, cols), va, cka, cva, sink)
    o_b, oc_b = bidir_gla(qb, kb, vb, la_f, la_b, cqb, ckb, cvb, cla_f, cla_b)
    y = jnp.concatenate([o_a, gla_output(o_b, rb, gla_g)], axis=-1) @ w_out
    yc = None
    if need_ctx_out:
        oc_a = context_attention(cqa, cka, cva, sink)
        yc = jnp.concatenate([oc_a, gla_output(oc_b, crb, gla_g)], axis=-1) @ w_out
    return y, yc

def pool_mixer(h, w_pool, pool_scale):
    B, T, D = h.shape
    ng = len(POOL_WINDOWS)
    hg = h.astype(jnp.float32).reshape(B, T, ng, POOL_GROUP)
    prefix = jnp.pad(jnp.cumsum(hg, axis=1), ((0, 0), (1, 0), (0, 0), (0, 0)))
    t = jnp.arange(T)
    means = []
    for gi, w in enumerate(POOL_WINDOWS):
        lo = jnp.maximum(t - w // 2, 0)
        hi = jnp.minimum(t + (w - w // 2), T)
        total = prefix[:, hi, gi] - prefix[:, lo, gi]
        means.append(total / (hi - lo).astype(jnp.float32)[:, None])
    pooled = (jnp.stack(means, axis=2) - hg).astype(h.dtype)
    y = jnp.einsum('btgc,gce->btge', pooled, w_pool)
    return y.reshape(B, T, D) * pool_scale

def second_inputs(seed: int = 0) -> dict:
    key = jax.random.key(seed)
    ks = jax.random.split(key, 24)
    D = D_MODEL
    ne = (DEPTH + 1) // 2
    no = DEPTH // 2

    def nrm(k, shape, scale=1.0):
        return jax.random.normal(k, shape, jnp.float32) * scale

    return {
        "x": nrm(ks[0], (BATCH, SEQ, D)),
        "c": nrm(ks[1], (BATCH, D)),
        "ctx": nrm(ks[2], (BATCH, CTX_LEN, D)),
        "c_ctx": nrm(ks[3], (D,)),
        "w_mod": nrm(ks[4], (DEPTH, D, N_MOD * D), 0.5 * D ** -0.5),
        "b_mod": nrm(ks[5], (DEPTH, N_MOD * D), 0.01),
        "norm_g": 1.0 + nrm(ks[6], (DEPTH, 3, D), 0.05),
        "ffn1_wi": nrm(ks[7], (DEPTH, D, 2 * D_FF), D ** -0.5),
        "ffn1_wo": nrm(ks[8], (DEPTH, D_FF, D), D_FF ** -0.5),
        "ffn2_wi": nrm(ks[9], (DEPTH, D, 2 * D_FF), D ** -0.5),
        "ffn2_wo": nrm(ks[10], (DEPTH, D_FF, D), D_FF ** -0.5),
        "w_in": nrm(ks[11], (ne, D, PROJ_DIM), D ** -0.5),
        "w_a2_f": nrm(ks[12], (ne, B_GATE_RANK, B_QK), B_GATE_RANK ** -0.5),
        "b_a_f": nrm(ks[13], (ne, B_QK), 0.1),
        "w_a2_b": nrm(ks[14], (ne, B_GATE_RANK, B_QK), B_GATE_RANK ** -0.5),
        "b_a_b": nrm(ks[15], (ne, B_QK), 0.1),
        "sink": nrm(ks[16], (ne, A_HEADS_2), 1.0),
        "gla_g": 1.0 + nrm(ks[17], (ne, B_DV), 0.05),
        "w_out": nrm(ks[18], (ne, MIX_OUT, D), MIX_OUT ** -0.5),
        "w_pool": nrm(ks[19], (no, len(POOL_WINDOWS), POOL_GROUP, POOL_GROUP), POOL_GROUP ** -0.5),
        "pool_scale": 1.0 + nrm(ks[20], (no, D), 0.1),
        "final_g": 1.0 + nrm(ks[21], (D,), 0.05),
    }

def second_block(x, c, ctx, c_ctx, w_mod, b_mod, norm_g, ffn1_wi, ffn1_wo, ffn2_wi, ffn2_wo,
              w_in, w_a2_f, b_a_f, w_a2_b, b_a_b, sink, gla_g, w_out, w_pool, pool_scale, final_g):
    T = x.shape[1]
    ROWS = T // GRID_W
    rows = jnp.repeat(jnp.arange(ROWS, dtype=jnp.float32), GRID_W)
    cols = jnp.tile(jnp.arange(GRID_W, dtype=jnp.float32), ROWS)

    for l in range(DEPTH):
        even = l % 2 == 0
        ctx_out = any(j % 2 == 0 for j in range(l + 1, DEPTH))
        ctx_in = even or ctx_out
        m = adaln(c, w_mod[l], b_mod[l])
        mc = adaln(c_ctx, w_mod[l], b_mod[l]) if ctx_in else None

        x = x + 0.5 * m[2] * swiglu(modulate(x, norm_g[l, 0], m[0], m[1]), ffn1_wi[l], ffn1_wo[l])
        if ctx_in:
            ctx = ctx + 0.5 * mc[2] * swiglu(modulate(ctx, norm_g[l, 0], mc[0], mc[1]), ffn1_wi[l], ffn1_wo[l])

        h = modulate(x, norm_g[l, 1], m[3], m[4])
        if even:
            e = l // 2
            hc = modulate(ctx, norm_g[l, 1], mc[3], mc[4])
            y, yc = mixer_ab(h, hc, rows, cols, ctx_out, w_in[e], w_a2_f[e], b_a_f[e], w_a2_b[e], b_a_b[e],
                             sink[e], gla_g[e], w_out[e])
        else:
            o = l // 2
            y = pool_mixer(h, w_pool[o], pool_scale[o])
            yc = pool_mixer(modulate(ctx, norm_g[l, 1], mc[3], mc[4]), w_pool[o], pool_scale[o]) if ctx_out else None
        x = x + m[5] * y
        if ctx_out:
            ctx = ctx + mc[5] * yc

        x = x + 0.5 * m[8] * swiglu(modulate(x, norm_g[l, 2], m[6], m[7]), ffn2_wi[l], ffn2_wo[l])
        if ctx_out:
            ctx = ctx + 0.5 * mc[8] * swiglu(modulate(ctx, norm_g[l, 2], mc[6], mc[7]), ffn2_wi[l], ffn2_wo[l])

    return rmsnorm_2(x, final_g)


def setup_inputs(seed=0):
    out = dict(first_inputs(seed))
    for name, value in second_inputs(seed + 1).items():
        if name != "x":
            out[name + "_2"] = value
    return out


def reference(
    x, positions, lb_logits, l0_norm_mix, l0_w_in, l0_hgrn_out_norm, l0_gmlp_v_norm,
    l0_gmlp_w_s, l0_gmlp_b_s, l0_w_out, l0_norm_ffn, l0_peer_w_query, l0_peer_sub_keys,
    l0_peer_expert_down, l0_peer_expert_up, l1_norm_mix, l1_w_in, l1_mla_cq_norm,
    l1_mla_ckv_norm, l1_mla_w_uq, l1_mla_w_ukv, l1_mla_q_norm, l1_mla_k_norm, l1_moba_q_norm,
    l1_moba_k_norm, l1_w_out, l1_norm_ffn, l1_peer_w_query, l1_peer_sub_keys,
    l1_peer_expert_down, l1_peer_expert_up, c_2, ctx_2, c_ctx_2, w_mod_2, b_mod_2, norm_g_2,
    ffn1_wi_2, ffn1_wo_2, ffn2_wi_2, ffn2_wo_2, w_in_2, w_a2_f_2, b_a_f_2, w_a2_b_2, b_a_b_2,
    sink_2, gla_g_2, w_out_2, w_pool_2, pool_scale_2, final_g_2,
):
    x = first_block(
        x, positions, lb_logits, l0_norm_mix, l0_w_in, l0_hgrn_out_norm, l0_gmlp_v_norm,
        l0_gmlp_w_s, l0_gmlp_b_s, l0_w_out, l0_norm_ffn, l0_peer_w_query, l0_peer_sub_keys,
        l0_peer_expert_down, l0_peer_expert_up, l1_norm_mix, l1_w_in, l1_mla_cq_norm,
        l1_mla_ckv_norm, l1_mla_w_uq, l1_mla_w_ukv, l1_mla_q_norm, l1_mla_k_norm,
        l1_moba_q_norm, l1_moba_k_norm, l1_w_out, l1_norm_ffn, l1_peer_w_query,
        l1_peer_sub_keys, l1_peer_expert_down, l1_peer_expert_up,
    )
    return second_block(
        x, c_2, ctx_2, c_ctx_2, w_mod_2, b_mod_2, norm_g_2, ffn1_wi_2, ffn1_wo_2, ffn2_wi_2,
        ffn2_wo_2, w_in_2, w_a2_f_2, b_a_f_2, w_a2_b_2, b_a_b_2, sink_2, gla_g_2, w_out_2,
        w_pool_2, pool_scale_2, final_g_2,
    )


_drawn_inputs = setup_inputs


def setup_inputs(seed=0):
    import zlib

    import numpy as np

    out = dict(_drawn_inputs(seed))
    spreads = {}
    factors = {'l1_mla_cq_norm': 3.58,
     'l1_mla_q_norm': 3.876,
     'l1_mla_k_norm': 3.538,
     'l1_moba_q_norm': 4.386,
     'l1_moba_k_norm': 3.733,
     'b_mod_2': 5.022,
     'norm_g_2': 2.901,
     'w_a2_f_2': 3.355,
     'b_a_f_2': 8.0,
     'w_a2_b_2': 4.105,
     'b_a_b_2': 8.0,
     'sink_2': 64.0,
     'gla_g_2': 8.0,
     'pool_scale_2': 2.729}
    for name, (base, spread) in spreads.items():
        noise = np.random.default_rng([zlib.crc32(name.encode()), seed]).standard_normal(out[name].shape)
        drawn = base * np.exp(spread * noise) if base else spread * noise
        out[name] = jnp.asarray(drawn.astype(out[name].dtype))
    for name, factor in factors.items():
        out[name] = (out[name] * factor).astype(out[name].dtype)
    return out
```

```python
from contextlib import ExitStack, contextmanager

import numpy as np

import concourse.bass as bass
from concourse import mybir

F32 = mybir.dt.float32
I32 = mybir.dt.int32
U32 = mybir.dt.uint32
ALU = mybir.AluOpType
ACT = mybir.ActivationFunctionType
AX_X = mybir.AxisListType.X

P = 128
D = 1024
DC = D // P
T = 256
TT = T // P
EPS = 1e-6
NEG = -1.0e30
LOWEST = -3.0e38

PH, NK, PK = 8, 128, 16
HP = 2 * PH
PG = 2
TOKS = 4

AH, HC = 4, 32
NB = T // HC
CH, NOPE, ROPE = 4, 128, 64
QK = NOPE + ROPE
FF = 2816
FT = FF // P
NMOD = 9
MT = NMOD * D // P
BC = 64
NBC = T // BC
WH, WD, WG = 8, 64, 2

COLS = [
    ("l0_norm_mix", 8), ("l0_hgrn_out_norm", 4), ("l0_norm_ffn", 8), ("l1_norm_mix", 8),
    ("l1_mla_cq_norm", 2), ("l1_mla_ckv_norm", 1), ("l1_norm_ffn", 8), ("c_2", 8), ("c_ctx_2", 8),
    ("b_mod_2", 2 * MT), ("norm_g_2", 48), ("b_a_f_2", 2), ("b_a_b_2", 2), ("gla_g_2", 1),
    ("pool_scale_2", 8), ("final_g_2", 8), ("lb_logits", 12),
]
COL_AT, NCOL = {}, 0
for _name, _n in COLS:
    COL_AT[_name] = (NCOL, NCOL + _n)
    NCOL += _n
ROWS = [
    ("l0_gmlp_v_norm", 512), ("l1_mla_q_norm", QK), ("l1_mla_k_norm", QK), ("l1_moba_q_norm", 128),
    ("l1_moba_k_norm", 128), ("sink_2", 8), ("l0_gmlp_b_s", 512), ("inv_freq", 32),
]
ROW_AT, NROW = {}, 0
for _name, _n in ROWS:
    ROW_AT[_name] = (NROW, NROW + _n)
    NROW += _n

STAGE_SEM = 170


class Stage:

    def __init__(self, nc, ctx, name):
        self.nc, self.ctx, self.name, self.n_sems = nc, ctx, name, 0

    def sb(self, name, shape, dt=F32):
        return self.ctx.enter_context(self.nc.sbuf_tensor(f"{self.name}_{name}", shape, dt))

    def ps(self, name, shape):
        return self.ctx.enter_context(self.nc.psum_tensor(f"{self.name}_{name}", shape, F32))

    def sem(self, name):
        self.n_sems += 1
        return self.ctx.enter_context(
            self.nc.semaphore(f"{self.name}_{name}", STAGE_SEM + self.n_sems - 1))


@contextmanager
def stage(nc, name):
    with ExitStack() as ctx:
        st = Stage(nc, ctx, name)
        yield st
    nc.all_engine_barrier(sems_to_clear=range(STAGE_SEM, STAGE_SEM + st.n_sems))


class Chain:

    def __init__(self, eng, sem):
        self.eng, self.sem, self.n = eng, sem, 0

    def __call__(self, instruction):
        self.n += 1
        instruction.then_inc(self.sem, 1)
        self.eng.wait_ge(self.sem, self.n)


class Store:
    pass


def setup(nc, keep, dram, K):
    def sb(name, shape, dt=F32):
        return keep.enter_context(nc.sbuf_tensor(name, shape, dt))

    K.x = sb("x_stream", [P, DC, T])
    K.xn = sb("x_normed", [P, DC, T])
    K.cols = sb("cols", [P, NCOL])
    K.rows = sb("rows", [P, NROW])
    K.ones = sb("ones", [P, P])
    K.ident = sb("ident", [P, P])
    K.iota = sb("iota", [P, P])
    K.eps = sb("eps", [P, 1])
    K.lb = sb("lower_bound", [P, AH])
    K.nlb = sb("one_less_lower_bound", [P, AH])
    K.col = lambda name: K.cols[:, COL_AT[name][0]:COL_AT[name][1]]
    K.row = lambda name: K.rows[:, ROW_AT[name][0]:ROW_AT[name][1]]

    with stage(nc, "setup") as st:
        cols_in, rows_in, x_in = st.sem("cols_in"), st.sem("rows_in"), st.sem("x_in")
        filled, v_step, exped = st.sem("filled"), st.sem("v_step"), st.sem("exped")
        cleared, shifted = st.sem("cleared"), st.sem("shifted")
        e = st.sb("e", [P, 3, AH])
        mx = st.sb("mx", [P, AH])
        mx2 = st.sb("mx2", [P, AH])
        block = st.ctx.enter_context(nc.Block())

        @block.sync
        def _(sp):
            sp.dma_start(K.cols[:], dram["cols"]).then_inc(cols_in, 16)
            sp.dma_start(K.rows[:], dram["rows"].partition_broadcast(P)).then_inc(rows_in, 16)
            sp.dma_start(K.x[:], dram["x"]).then_inc(x_in, 16)
            sp.wait_ge(rows_in, 16)
            sp.wait_ge(x_in, 16)

        @block.gpsimd
        def _(pool):
            pool.memset(K.ones[:], 1.0)
            pool.memset(K.eps[:], EPS)
            pool.memset(K.ident[:], 0.0).then_inc(cleared, 1)
            pool.iota(K.iota[:], pattern=[[1, P]], base=0, channel_multiplier=0,
                      allow_small_or_imprecise_dtypes=True)
            pool.wait_ge(cleared, 1)
            pool.affine_select(out=K.ident[:], in_=K.ident[:], compare_op=ALU.not_equal, fill=1.0,
                               base=0, pattern=[[-1, P]], channel_multiplier=1).then_inc(filled, 1)

        @block.vector
        def _(dve):
            chain = Chain(dve, v_step)
            dve.wait_ge(cols_in, 16)
            lg = K.col("lb_logits").rearrange("p (r h) -> p r h", r=3)
            chain(dve.tensor_tensor(mx[:], lg[:, 0], lg[:, 1], ALU.max))
            chain(dve.tensor_tensor(mx2[:], mx[:], lg[:, 2], ALU.max))
            dve.tensor_tensor(e[:], lg, mx2[:].unsqueeze(1).to_broadcast([P, 3, AH]),
                              ALU.subtract).then_inc(shifted, 1)
            dve.wait_ge(exped, 1)
            chain(dve.tensor_tensor(mx[:], e[:, 0], e[:, 1], ALU.add))
            chain(dve.tensor_tensor(mx2[:], mx[:], e[:, 2], ALU.add))
            chain(dve.reciprocal(mx[:], mx2[:]))
            chain(dve.tensor_tensor(K.lb[:], e[:, 0], mx[:], ALU.mult))
            chain(dve.tensor_scalar(K.nlb[:], K.lb[:], -1.0, 1.0, ALU.mult, ALU.add))

        @block.scalar
        def _(act):
            act.wait_ge(shifted, 1)
            act.activation(e[:], e[:], ACT.Exp).then_inc(exped, 1)


def normalize(nc, K, name, src, dst, gain, shift=None, width=D):
    chunks, tokens = src.shape[1], src.shape[2]
    with stage(nc, name) as st:
        squared, summed, rooted, v_step = (st.sem(x) for x in ("squared", "summed", "rooted", "v_step"))
        sq = st.sb("sq", [P, chunks, tokens])
        root = st.sb("root", [P, tokens])
        rstd = st.sb("rstd", [P, tokens])
        total = st.ps("total", [P, 512])
        block = st.ctx.enter_context(nc.Block())

        @block.scalar
        def _(act):
            for c in range(chunks):
                act.activation(sq[:, c], src[:, c], ACT.Square).then_inc(squared, 1)
            act.wait_ge(summed, 1)
            act.activation(root[:], total[:, 0:tokens], ACT.Sqrt, bias=K.eps[:], scale=1.0 / width)\
                .then_inc(rooted, 1)

        @block.tensor
        def _(pe):
            for c in range(chunks):
                pe.wait_ge(squared, c + 1)
                mm = pe.matmul(total[:, 0:tokens], K.ones[:], sq[:, c], start=c == 0, stop=c == chunks - 1)
            mm.then_inc(summed, 1)

        @block.vector
        def _(dve):
            chain = Chain(dve, v_step)
            dve.wait_ge(rooted, 1)
            chain(dve.reciprocal(rstd[:], root[:]))
            for c in range(chunks):
                ins = dve.scalar_tensor_tensor(out=dst[:, c], in0=src[:, c], scalar=gain[:, c:c + 1],
                                               in1=rstd[:], op0=ALU.mult, op1=ALU.mult)
            chain(ins)
            if shift is not None:
                for c in range(chunks):
                    dve.tensor_scalar(dst[:, c], dst[:, c], shift[:, c:c + 1], None, ALU.add)


class Proj:

    def __init__(self, w, c0, width, x, form, out, func=ACT.Copy):
        self.w, self.c0, self.width, self.x, self.form, self.out, self.func = w, c0, width, x, form, out, func


def project(nc, name, blocks, slots=3):
    with stage(nc, name) as st:
        loaded = [st.sem(f"loaded{s}") for s in range(slots)]
        product, evacuated = st.sem("product"), st.sem("evacuated")
        chunks = max(len(b.x) for b in blocks)
        width = max(b.width for b in blocks)
        w = st.sb("w", [P, slots, chunks, width])
        acc = st.ps("acc", [P, 2, 2 * 512])
        block = st.ctx.enter_context(nc.Block())

        @block.sync
        def _(sp):
            for n, b in enumerate(blocks):
                if n >= slots:
                    sp.wait_ge(product, n - slots + 1)
                k = b.x[0].shape[0]
                src = b.w[:, b.c0:b.c0 + b.width].rearrange("(c p) n -> p c n", p=k)
                sp.dma_start(w[0:k, n % slots, 0:len(b.x), 0:b.width], src).then_inc(loaded[n % slots], 16)

        @block.tensor
        def _(pe):
            for n, b in enumerate(blocks):
                pe.wait_ge(loaded[n % slots], 16 * (n // slots + 1))
                if n >= 2:
                    pe.wait_ge(evacuated, n - 1)
                k = b.x[0].shape[0]
                if b.form == "f":
                    for j in range(-(-b.width // P)):
                        m = min(P, b.width - j * P)
                        for c, x in enumerate(b.x):
                            mm = pe.matmul(acc[0:m, n % 2, j * T:(j + 1) * T],
                                           w[0:k, n % slots, c, j * P:j * P + m], x,
                                           start=c == 0, stop=c == len(b.x) - 1)
                else:
                    for j in range(TT):
                        for c, x in enumerate(b.x):
                            mm = pe.matmul(acc[:, n % 2, j * 512:j * 512 + b.width], x[:, j * P:(j + 1) * P],
                                           w[0:k, n % slots, c, 0:b.width],
                                           start=c == 0, stop=c == len(b.x) - 1)
                mm.then_inc(product, 1)

        @block.scalar
        def _(act):
            for n, b in enumerate(blocks):
                act.wait_ge(product, n + 1)
                if b.form == "f":
                    m = min(P, b.width)
                    src = acc[0:m, n % 2, 0:-(-b.width // P) * T].rearrange("p (j t) -> p j t", t=T)
                else:
                    src = acc[:, n % 2, :].rearrange("p (j n) -> p j n", n=512)[:, :, 0:b.width]
                act.activation(b.out, src, b.func).then_inc(evacuated, 1)


def chunked(x):
    return [x[:, c] for c in range(x.shape[1])]


def project_residual(nc, K, name, w, x, gate=None):
    slots, width, chunks = 3, 256, x.shape[1]
    blocks = D // width
    with stage(nc, name) as st:
        loaded = [st.sem(f"loaded{s}") for s in range(slots)]
        product, added = st.sem("product"), st.sem("added")
        ws = st.sb("w", [P, slots, chunks, width])
        acc = st.ps("acc", [P, 2, 512])
        block = st.ctx.enter_context(nc.Block())

        @block.sync
        def _(sp):
            for n in range(blocks):
                if n >= slots:
                    sp.wait_ge(product, n - slots + 1)
                sp.dma_start(ws[:, n % slots], w[:, n * width:(n + 1) * width]
                             .rearrange("(c p) n -> p c n", p=P)).then_inc(loaded[n % slots], 16)

        @block.tensor
        def _(pe):
            for n in range(blocks):
                pe.wait_ge(loaded[n % slots], 16 * (n // slots + 1))
                if n >= 2:
                    pe.wait_ge(added, 2 * (n - 1))
                for j in range(2):
                    for c in range(chunks):
                        mm = pe.matmul(acc[:, n % 2, j * T:(j + 1) * T], ws[:, n % slots, c, j * P:(j + 1) * P],
                                       x[:, c], start=c == 0, stop=c == chunks - 1)
                mm.then_inc(product, 1)

        @block.vector
        def _(dve):
            for n in range(blocks):
                dve.wait_ge(product, n + 1)
                for j in range(2):
                    c = 2 * n + j
                    scale = 1.0 if gate is None else gate[:, c:c + 1]
                    dve.scalar_tensor_tensor(out=K.x[:, c], in0=acc[:, n % 2, j * T:(j + 1) * T], scalar=scale,
                                             in1=K.x[:, c], op0=ALU.mult, op1=ALU.add).then_inc(added, 1)


def hgrn_gmlp(nc, K, dram):
    with ExitStack() as keep:
        def sb(name, shape, dt=F32):
            return keep.enter_context(nc.sbuf_tensor(name, shape, dt))

        q, f, og = sb("hg_q", [P, AH, T]), sb("hg_f", [P, AH, T]), sb("hg_og", [P, AH, T])
        v, u, gv = sb("hg_v", [P, TT, 512]), sb("hg_u", [P, 4, T]), sb("hg_gv", [P, TT, 512])
        mix = sb("hg_mix", [P, DC, T])
        normalize(nc, K, "l0_norm", K.x, K.xn, K.col("l0_norm_mix"))
        w, x = dram["l0_w_in"], chunked(K.xn)
        project(nc, "l0_in", [
            Proj(w, 0, 512, x, "f", q[:]),
            Proj(w, 512, 512, x, "f", f[:], ACT.Sigmoid),
            Proj(w, 1024, 512, x, "t", v[:], ACT.Silu),
            Proj(w, 1536, 512, x, "f", og[:], ACT.Silu),
            Proj(w, 2048, 512, x, "f", u[:], ACT.Gelu_apprx_tanh),
            Proj(w, 2560, 512, x, "t", gv[:], ACT.Gelu_apprx_tanh),
        ])
        hgrn(nc, K, q, f, v, og, mix)
        gmlp(nc, K, dram, u, gv, mix)
        project_residual(nc, K, "l0_out", dram["l0_w_out"], mix)


def hgrn(nc, K, q, f, v, og, mix):
    with stage(nc, "hgrn") as st:
        v_step, masked, ready, product = (st.sem(x) for x in ("v_step", "masked", "ready", "product"))
        scored, turned, copied, state_add = (st.sem(x) for x in ("scored", "turned", "copied", "state_add"))
        state, added, out_sum, squared, rooted = (
            st.sem(x) for x in ("state", "added", "out_sum", "squared", "rooted"))
        moved = st.sem("moved")
        kk = st.sb("k", [P, AH, T])
        cum = st.sb("cum", [P, AH, T])
        inner = st.sb("inner", [P, AH, T])
        first = st.sb("first", [P, AH, T])
        qd = st.sb("qd", [P, AH, T])
        decayed = st.sb("decayed", [P, AH, T])
        pair = st.sb("pair", [P, 2, AH, T])
        onehot = st.sb("onehot", [P, HC, HC])
        score = st.sb("score", [HC, AH, T])
        own = st.sb("own", [P, P // HC])
        own2 = st.sb("own2", [P, P // HC])
        diag = st.sb("diag", [P, AH * TT, P // HC, HC])
        kt = st.sb("kt", [P, AH * TT, P])
        states = st.sb("states", [P, NB, AH, P])
        startm = st.sb("startm", [P, HC])
        sq = st.sb("sq", [P, AH, T])
        root = st.sb("root", [P, AH, T])
        a_ps = st.ps("a", [P, AH, T])
        t_ps = st.ps("t", [P, AH, T])
        d_ps = st.ps("d", [P, 2, 512])
        o_ps = st.ps("o", [P, AH, T])
        at_ps = d_ps[:, 0, 0:AH * TT * HC].rearrange("p (n t) -> p n t", t=HC)
        block = st.ctx.enter_context(nc.Block())
        chunk = lambda a: a.rearrange("p h (b t) -> p (h b) t", t=HC)

        @block.gpsimd
        def _(pool):
            pool.memset(onehot[:], 0.0).then_inc(masked, 1)
            pool.memset(own[:], 1.0).then_inc(masked, 1)
            pool.memset(startm[:], 0.0).then_inc(masked, 1)
            pool.wait_ge(masked, 3)
            pool.affine_select(out=onehot[:], in_=onehot[:], compare_op=ALU.not_equal, fill=1.0, base=0,
                               pattern=[[1, HC], [-1, HC]], channel_multiplier=0).then_inc(masked, 1)
            pool.affine_select(out=own2[:], in_=own[:], compare_op=ALU.is_ge, fill=0.0, base=0,
                               pattern=[[-HC, P // HC]], channel_multiplier=1).then_inc(masked, 1)
            pool.affine_select(out=startm[:], in_=startm[:], compare_op=ALU.not_equal, fill=1.0, base=0,
                               pattern=[[1, HC]], channel_multiplier=0).then_inc(masked, 1)
            pool.wait_ge(masked, 6)
            pool.affine_select(out=own[:], in_=own2[:], compare_op=ALU.is_ge, fill=0.0, base=HC - 1,
                               pattern=[[HC, P // HC]], channel_multiplier=-1).then_inc(masked, 1)

        @block.vector
        def _(dve):
            chain = Chain(dve, v_step)
            for h in range(AH):
                ins = dve.tensor_scalar(f[:, h], f[:, h], K.nlb[:, h:h + 1], K.lb[:, h:h + 1], ALU.mult, ALU.add)
            chain(ins)
            dve.tensor_scalar(kk[:], f[:], -1.0, 1.0, ALU.mult, ALU.add)
            dve.wait_ge(masked, 7)
            starts = startm[:].unsqueeze(1).to_broadcast([P, AH * NB, HC])
            chain(dve.tensor_tensor(chunk(first[:]), chunk(f[:]), starts, ALU.mult))
            chain(dve.tensor_tensor(inner[:], f[:], first[:], ALU.subtract))
            chain(dve.tensor_tensor_scan(cum[:].rearrange("p h t -> p (h t)"),
                                         inner[:].rearrange("p h t -> p (h t)"),
                                         first[:].rearrange("p h t -> p (h t)"), 0.0, ALU.mult, ALU.add))
            dve.tensor_tensor(qd[:], q[:], cum[:], ALU.mult)
            dc, kc, qc, fc = chunk(decayed[:]), chunk(kk[:]), chunk(q[:]), chunk(f[:])
            for i in range(HC):
                if i:
                    chain(dve.tensor_tensor(dc[:, :, 0:i], dc[:, :, 0:i],
                                            fc[:, :, i:i + 1].to_broadcast([P, AH * NB, i]), ALU.mult))
                chain(dve.tensor_copy(dc[:, :, i:i + 1], kc[:, :, i:i + 1]))
                if i >= 2:
                    dve.wait_ge(product, i - 1)
                dve.tensor_tensor(chunk(pair[:, i % 2])[:, :, 0:i + 1], dc[:, :, 0:i + 1],
                                  qc[:, :, i:i + 1].to_broadcast([P, AH * NB, i + 1]), ALU.mult)\
                    .then_inc(ready, 1)
            chain(dve.memset(states[:, 0], 0.0))
            for b in range(NB - 1):
                dve.wait_ge(state_add, b + 1)
                for h in range(AH):
                    t = b * HC + HC - 1
                    ins = dve.scalar_tensor_tensor(out=states[:, b + 1, h], in0=states[:, b, h],
                                                   scalar=cum[:, h, t:t + 1],
                                                   in1=d_ps[:, b % 2, h * P:(h + 1) * P],
                                                   op0=ALU.mult, op1=ALU.add)
                ins.then_inc(state, 1)
                dve.wait_ge(state, b + 1)
            dve.wait_ge(turned, 2)
            dve.tensor_tensor(
                diag[:], at_ps.unsqueeze(2).to_broadcast([P, AH * TT, P // HC, HC]),
                own[:].unsqueeze(1).unsqueeze(3).to_broadcast([P, AH * TT, P // HC, HC]), ALU.mult)\
                .then_inc(added, 1)
            dve.wait_ge(rooted, 1)
            chain(dve.reciprocal(sq[:], root[:]))
            chain(dve.tensor_tensor(root[:], o_ps[:], sq[:], ALU.mult))
            for h in range(AH):
                g = K.col("l0_hgrn_out_norm")[:, h:h + 1]
                dve.scalar_tensor_tensor(out=mix[:, h], in0=root[:, h], scalar=g, in1=og[:, h],
                                         op0=ALU.mult, op1=ALU.mult)

        @block.tensor
        def _(pe):
            pe.wait_ge(masked, 7)
            for i in range(HC):
                pe.wait_ge(ready, i + 1)
                for half in range(2):
                    hs = slice(half * 2, half * 2 + 2)
                    mm = pe.matmul(chunk(a_ps[0:HC, hs])[:, :, 0:i + 1], onehot[:, i, :],
                                   chunk(pair[:, i % 2, hs])[:, :, 0:i + 1],
                                   start=i == 0, stop=i == HC - 1, skip_group_check=True)
                mm.then_inc(product, 1)
            for h in range(AH):
                for t in range(TT):
                    mm = pe.transpose(t_ps[:, h, t * P:(t + 1) * P], decayed[:, h, t * P:(t + 1) * P], K.ident[:])
            mm.then_inc(turned, 1)
            pe.wait_ge(copied, 1)
            for b in range(NB - 1):
                t, at = b * HC // P, b * HC % P
                if b >= 2:
                    pe.wait_ge(state, b - 1)
                for h in range(AH):
                    mm = pe.matmul(d_ps[:, b % 2, h * P:(h + 1) * P], kt[at:at + HC, h * TT + t, :],
                                   v[at:at + HC, t, h * P:(h + 1) * P], start=True, stop=True)
                mm.then_inc(state_add, 1)
            pe.wait_ge(scored, 1)
            pe.wait_ge(state, NB - 1)
            for h in range(AH):
                for t in range(TT):
                    mm = pe.transpose(at_ps[:, h * TT + t, :], score[:, h, t * P:(t + 1) * P], K.ident[0:HC, 0:HC])
            mm.then_inc(turned, 1)
            pe.wait_ge(added, 1)
            for h in range(AH):
                for t in range(TT):
                    pe.matmul(o_ps[:, h, t * P:(t + 1) * P], v[:, t, h * P:(h + 1) * P],
                              diag[:, h * TT + t].rearrange("p j t -> p (j t)"),
                              start=h % 2 == 0 and t == 0, stop=False, skip_group_check=True)
            for h in range(AH):
                for b in range(1, NB):
                    mm = pe.matmul(o_ps[:, h, b * HC:(b + 1) * HC], states[:, b, h], qd[:, h, b * HC:(b + 1) * HC],
                                   start=False, stop=True, skip_group_check=True)
            mm.then_inc(out_sum, 1)
            pe.wait_ge(squared, 1)
            for half in range(2):
                hs = slice(half * 2, half * 2 + 2)
                mm = pe.matmul(a_ps[:, hs], K.ones[:], sq[:, hs], start=True, stop=True)
            mm.then_inc(out_sum, 1)

        @block.scalar
        def _(act):
            act.wait_ge(turned, 1)
            act.activation(kt[:].rearrange("p (h t) k -> p h (t k)", t=TT), t_ps[:], ACT.Copy).then_inc(copied, 1)
            act.wait_ge(product, HC)
            act.activation(score[:], a_ps[0:HC], ACT.Copy).then_inc(scored, 1)
            act.wait_ge(out_sum, 1)
            act.activation(sq[:], o_ps[:], ACT.Square).then_inc(squared, 1)
            act.wait_ge(out_sum, 2)
            act.activation(root[:], a_ps[:], ACT.Sqrt, bias=K.eps[:], scale=1.0 / P).then_inc(rooted, 1)


def gmlp(nc, K, dram, u, gv, mix):
    groups = 4
    with stage(nc, "gmlp") as st:
        w_in, kept, squared, rooted = (st.sem(x) for x in ("w_in", "kept", "squared", "rooted"))
        v_step, normed, mixed = (st.sem(x) for x in ("v_step", "normed", "mixed"))
        summed = st.sem("summed")
        w = st.sb("w", [P, groups, P])
        wc = st.sb("wc", [P, groups, P])
        sq = st.sb("sq", [P, TT * groups, P])
        ss = st.sb("ss", [P, TT * groups])
        root = st.sb("root", [P, TT * groups])
        rstd = st.sb("rstd", [P, TT * groups])
        acc = st.ps("acc", [P, groups, T])
        block = st.ctx.enter_context(nc.Block())
        g4 = gv[:].rearrange("p n (g d) -> p (n g) d", g=groups)

        @block.sync
        def _(sp):
            sp.dma_start(w[:], dram["w_s"]).then_inc(w_in, 16)

        @block.gpsimd
        def _(pool):
            pool.wait_ge(w_in, 16)
            pool.affine_select(out=wc[:], in_=w[:], compare_op=ALU.is_ge, fill=0.0, base=0,
                               pattern=[[0, groups], [1, P]], channel_multiplier=-1).then_inc(kept, 1)

        @block.scalar
        def _(act):
            act.activation(sq[:], g4, ACT.Square).then_inc(squared, 1)
            act.wait_ge(summed, 1)
            act.activation(root[:], ss[:], ACT.Sqrt, bias=K.eps[:], scale=1.0 / P).then_inc(rooted, 1)

        @block.vector
        def _(dve):
            chain = Chain(dve, v_step)
            dve.wait_ge(squared, 1)
            dve.tensor_reduce(ss[:], sq[:], AX_X, ALU.add).then_inc(summed, 1)
            dve.wait_ge(rooted, 1)
            chain(dve.reciprocal(rstd[:], root[:]))
            chain(dve.tensor_tensor(g4, g4, rstd[:].unsqueeze(2).to_broadcast([P, TT * groups, P]), ALU.mult))
            dve.tensor_tensor(gv[:], gv[:], K.row("l0_gmlp_v_norm").unsqueeze(1).to_broadcast([P, TT, 512]),
                              ALU.mult).then_inc(normed, 1)
            dve.wait_ge(mixed, 1)
            dve.tensor_tensor(mix[:, 4:8], acc[:], u[:], ALU.mult)

        @block.tensor
        def _(pe):
            pe.wait_ge(kept, 1)
            pe.wait_ge(normed, 1)
            bias = K.row("l0_gmlp_b_s")
            for g in range(groups):
                for n in range(TT):
                    out = acc[:, g, n * P:(n + 1) * P]
                    pe.matmul(out, gv[:, n, g * P:(g + 1) * P], wc[:, g, :], start=True, stop=False)
                    mm = pe.matmul(out, K.ones[0:1, :], bias[0:1, g * P:(g + 1) * P], start=False, stop=True)
            mm.then_inc(mixed, 1)


def peer(nc, K, dram, layer):
    name = f"peer{layer}"
    normalize(nc, K, f"{name}_norm", K.x, K.xn, K.col(f"l{layer}_norm_ffn"))
    with ExitStack() as keep:
        def sb(n, shape, dt=F32):
            return keep.enter_context(nc.sbuf_tensor(f"{name}_{n}", shape, dt))

        s = sb("scores", [P, TT, HP, NK])
        q = sb("q", [P, HP, T])
        w, x = dram[f"l{layer}_peer_w_query"], chunked(K.xn)
        with ExitStack() as early:
            keys = early.enter_context(nc.sbuf_tensor(f"{name}_keys", [P, HP, NK], F32))
            project(nc, f"{name}_q", [Proj(w, n * 512, 512, x, "f", q[:, 4 * n:4 * n + 4]) for n in range(4)])
            peer_scores(nc, K, name, dram[f"l{layer}_sub_keys"], keys, q, s)
        peer_experts(nc, K, name, dram[f"l{layer}_down"], dram[f"l{layer}_up"], s, q)


def peer_scores(nc, K, name, keys_in, keys, q, s):
    with stage(nc, f"{name}_s") as st:
        loaded, product, copied = (st.sem(x) for x in ("loaded", "product", "copied"))
        acc = st.ps("acc", [P, 4, 4, NK])
        block = st.ctx.enter_context(nc.Block())

        @block.sync
        def _(sp):
            sp.dma_start(keys[:], keys_in).then_inc(loaded, 16)

        @block.tensor
        def _(pe):
            pe.wait_ge(loaded, 16)
            for n in range(TT * 4):
                t, b = divmod(n, 4)
                if n >= 4:
                    pe.wait_ge(copied, n - 3)
                for j in range(4):
                    hp = 4 * b + j
                    mm = pe.matmul(acc[:, n % 4, j], q[:, hp, t * P:(t + 1) * P], keys[:, hp], start=True, stop=True)
                mm.then_inc(product, 1)

        @block.scalar
        def _(act):
            for n in range(TT * 4):
                t, b = divmod(n, 4)
                act.wait_ge(product, n + 1)
                act.activation(s[:, t, 4 * b:4 * b + 4], acc[:, n % 4], ACT.Copy).then_inc(copied, 1)


def peer_experts(nc, K, name, down, up, s, work):
    groups = NK // PG
    with stage(nc, f"{name}_e") as st:
        loaded = [st.sem(f"loaded{i}") for i in range(2)]
        product, gelued, v_step = st.sem("product"), st.sem("gelued"), st.sem("v_step")
        shifted, exped, chosen, turned, copied = (
            st.sem(x) for x in ("shifted", "exped", "chosen", "turned", "copied"))
        hot, routed, weighted = (st.sem(x) for x in ("hot", "routed", "weighted"))
        out_sum = st.sem("out_sum")
        ring = st.sb("ring", [P, 2, PG * D])
        h = st.sb("h", [P, NK, T])
        val = st.sb("val", [P, HP, PK])
        idx = st.sb("idx", [P, HP, PK], U32)
        idxf = st.sb("idxf", [P, HP, PK])
        top = st.sb("top", [P, TT, PH, PK])
        pos = st.sb("pos", [P, PH, PK], U32)
        half = st.sb("half", [P, PH, PK], U32)
        halff = st.sb("halff", [P, PH, PK])
        den = st.sb("den", [P, TT * PH])
        rden = st.sb("rden", [P, TT * PH])
        s0, s1 = (s[:, t].rearrange("p a n -> p (a n)") for t in range(TT))
        pick = s0[:, 0:2 * T].rearrange("p (n t e) -> p n t e", n=2, t=TT)
        by_choice = s0[:, 2 * T:5 * T].rearrange("p (n t) -> p n t", n=3)
        a_hot = s1[:, 0:2 * TOKS * P].rearrange("p (k a e) -> p k a e", k=2, a=TOKS)
        b_hot = s1[:, 2 * TOKS * P:4 * TOKS * P].rearrange("p (k a e) -> p k a e", k=2, a=TOKS)
        s_ps = st.ps("s", [P, 2, PG, T])
        o_ps = st.ps("o", [P, DC, T])
        g_ps = o_ps[:, 0:4, :].rearrange("p (b c) t -> p b (c t)", b=2)
        t_ps = o_ps[:, 4:7, :]
        cand = work[:].rearrange("p a t -> p (a t)")[:, 0:PH * PK * PK].rearrange("p (h c) -> p h c", h=PH)
        match = work[:].rearrange("p a t -> p (a t)")[:, PH * PK * PK:2 * PH * PK * PK]\
            .rearrange("p (h j a) -> p h j a", h=PH, a=PK)
        block = st.ctx.enter_context(nc.Block())

        def top16(dve, chain, src, rows, values, indices):
            for lo in (0, 8):
                for r in range(rows):
                    ins = dve.max(values[:, r, lo:lo + 8], src[:, r])
                chain(ins)
                for r in range(rows):
                    ins = dve.max_index(indices[:, r, lo:lo + 8], values[:, r, lo:lo + 8], src[:, r])
                chain(ins)
                if lo == 0:
                    for r in range(rows):
                        ins = dve.match_replace(src[:, r], values[:, r, 0:8], src[:, r], LOWEST)
                    chain(ins)

        @block.sync
        def _(sp):
            for g in range(2):
                sp.dma_start(ring[:, g], down[g]).then_inc(loaded[g], 16)
            with sp.Fori(1, groups // 2) as i:
                for k in range(2):
                    sp.wait_ge(product, i * 2 + k - 1)
                    sp.dma_start(ring[:, k], down[i * 2 + k]).then_inc(loaded[k], 16)
            for k in range(2):
                sp.wait_ge(product, groups + k - 1)
                sp.dma_start(ring[:, k], up[:, k * PG:(k + 1) * PG].rearrange("p a d -> p (a d)"))\
                    .then_inc(loaded[k], 16)
            with sp.Fori(1, groups // 2) as i:
                for k in range(2):
                    sp.wait_ge(out_sum, i * 2 + k - 1)
                    sp.dma_start(ring[:, k], up[:, bass.ds((i * 2 + k) * PG, PG)]
                                 .rearrange("p a d -> p (a d)")).then_inc(loaded[k], 16)

        @block.tensor
        def _(pe):
            def group(i, k, value):
                pe.wait_ge(loaded[k], value)
                w = ring[:, k].rearrange("p (a c e) -> p a c e", a=PG, c=DC)
                for a in range(PG):
                    for c in range(DC):
                        mm = pe.matmul(s_ps[:, k, a], w[:, a, c], K.xn[:, c], start=c == 0, stop=c == DC - 1)
                mm.then_inc(product, 1)

            group(0, 0, 16)
            group(0, 1, 16)
            with pe.Fori(1, groups // 2) as i:
                for k in range(2):
                    pe.wait_ge(gelued, i * 2 + k - 1)
                    group(i, k, i * 16 + 16)
            pe.wait_ge(chosen, 1)
            for n in range(2):
                for t in range(TT):
                    pe.transpose(t_ps[:, n, t * P:(t + 1) * P], pick[:, n, t], K.ident[:])
            for t in range(TT):
                mm = pe.transpose(t_ps[:, 2, t * P:(t + 1) * P],
                                  top[:, t].rearrange("p h j -> p (h j)"), K.ident[:])
            mm.then_inc(turned, 1)
            def route(i, k):
                pe.wait_ge(hot, i * 2 + k + 1)
                for a in range(TOKS):
                    mm = pe.matmul(g_ps[:, k, a * P:(a + 1) * P], a_hot[:, k, a], b_hot[:, k, a],
                                   start=True, stop=True)
                mm.then_inc(routed, 1)

            for k in range(2):
                route(0, k)
            with pe.Fori(1, T // (2 * TOKS)) as i:
                for k in range(2):
                    pe.wait_ge(weighted, i * 2 + k - 1)
                    route(i, k)
            pe.wait_ge(weighted, T // TOKS)

            def out_tile(k, a, tile, first):
                w = ring[:, k].rearrange("p (a c d) -> p a c d", a=PG, c=DC)
                for c in range(DC):
                    mm = pe.matmul(o_ps[:, c], w[:, a, c], h[:, tile], start=first and c % 2 == 0, stop=False,
                                   skip_group_check=True)
                return mm

            for k in range(2):
                pe.wait_ge(loaded[k], 16 * (groups // 2 + 1))
                for a in range(PG):
                    mm = out_tile(k, a, k * PG + a, k == 0 and a == 0)
                mm.then_inc(out_sum, 1)
            with pe.Fori(1, groups // 2) as i:
                for k in range(2):
                    pe.wait_ge(loaded[k], i * 16 + 16 * (groups // 2 + 1))
                    for a in range(PG):
                        mm = out_tile(k, a, (i * 2 + k) * PG + a, False)
                    mm.then_inc(out_sum, 1)

        @block.scalar
        def _(act):
            with act.Fori(0, groups // 2) as i:
                for k in range(2):
                    act.wait_ge(product, i * 2 + k + 1)
                    act.activation(h[:, bass.ds((i * 2 + k) * PG, PG), :], s_ps[:, k], ACT.Gelu_apprx_tanh)\
                        .then_inc(gelued, 1)
            act.wait_ge(shifted, 1)
            act.activation(top[:], top[:], ACT.Exp).then_inc(exped, 1)

        @block.vector
        def _(dve):
            chain = Chain(dve, v_step)
            iota16 = K.iota[:, 0:PK].unsqueeze(1).unsqueeze(1).to_broadcast([P, PH, PK, PK])
            for t in range(TT):
                top16(dve, chain, s[:, t], HP, val, idx)
                chain(dve.tensor_copy(idxf[:], idx[:]))
                v2 = val[:].rearrange("p (h s) k -> p h s k", s=2)
                chain(dve.tensor_tensor(
                    cand.rearrange("p h (a b) -> p h a b", a=PK),
                    v2[:, :, 0].unsqueeze(3).to_broadcast([P, PH, PK, PK]),
                    v2[:, :, 1].unsqueeze(2).to_broadcast([P, PH, PK, PK]), ALU.add))
                top16(dve, chain, cand, PH, top[:, t], pos)
                for n in range(2):
                    if n == 0:
                        chain(dve.tensor_scalar(half[:], pos[:], 4, None, ALU.logical_shift_right))
                    else:
                        chain(dve.tensor_scalar(half[:], pos[:], PK - 1, None, ALU.bitwise_and))
                    chain(dve.tensor_copy(halff[:], half[:]))
                    chain(dve.tensor_tensor(match, halff[:].unsqueeze(3).to_broadcast([P, PH, PK, PK]), iota16,
                                            ALU.is_equal))
                    i2 = idxf[:].rearrange("p (h s) k -> p h s k", s=2)[:, :, n]
                    chain(dve.tensor_tensor(match, match, i2.unsqueeze(2).to_broadcast([P, PH, PK, PK]), ALU.mult))
                    chain(dve.tensor_reduce(pick[:, n, t].rearrange("p (h j) -> p h j", h=PH), match, AX_X, ALU.add))
            tops = top[:].rearrange("p t h j -> p (t h) j")
            chain(dve.tensor_copy(den[:].unsqueeze(2), tops[:, :, 0:1]))
            dve.tensor_tensor(tops, tops, den[:].unsqueeze(2).to_broadcast([P, TT * PH, PK]), ALU.subtract)\
                .then_inc(shifted, 1)
            dve.wait_ge(exped, 1)
            chain(dve.tensor_reduce(den[:], tops, AX_X, ALU.add))
            chain(dve.reciprocal(rden[:], den[:]))
            dve.tensor_tensor(tops, tops, rden[:].unsqueeze(2).to_broadcast([P, TT * PH, PK]), ALU.mult)\
                .then_inc(chosen, 1)
            dve.wait_ge(turned, 1)
            dve.tensor_copy(by_choice, t_ps).then_inc(copied, 1)
            dve.wait_ge(copied, 1)

            def hots(i, k):
                for a in range(TOKS):
                    t = (i * 2 + k) * TOKS + a
                    ins = dve.tensor_scalar(a_hot[:, k, a], K.iota[:], by_choice[:, 0, bass.ds(t, 1)],
                                            by_choice[:, 2, bass.ds(t, 1)], ALU.is_equal, ALU.mult)
                    ins = dve.tensor_scalar(b_hot[:, k, a], K.iota[:], by_choice[:, 1, bass.ds(t, 1)], None,
                                            ALU.is_equal)
                ins.then_inc(hot, 1)

            def weigh(i, k):
                hh = h[:, :, bass.ds((i * 2 + k) * TOKS, TOKS)]
                g = g_ps[:, k].rearrange("p (a e) -> p e a", a=TOKS)
                dve.tensor_tensor(hh, g, hh, ALU.mult).then_inc(weighted, 1)

            for k in range(2):
                hots(0, k)
            with dve.Fori(1, T // (2 * TOKS)) as i:
                for k in range(2):
                    dve.wait_ge(routed, i * 2 + k - 1)
                    weigh(i - 1, k)
                    hots(i, k)
            for k in range(2):
                dve.wait_ge(routed, T // TOKS - 1 + k)
                weigh(T // (2 * TOKS) - 1, k)
            dve.wait_ge(out_sum, groups)
            for c in range(0, DC, 2):
                dve.tensor_tensor(K.x[:, c:c + 2], o_ps[:, c:c + 2], K.x[:, c:c + 2], ALU.add)


class Head:

    def __init__(self, qk, v, out, sink=None):
        self.qk, self.v, self.out, self.sink = qk, v, out, sink


def attend(nc, K, name, heads, keys, chunks_of, mask, scale):
    units = [(h, t) for h in heads for t in range(TT)]
    with stage(nc, name) as st:
        scored, masked, shifted, exped, normed = (
            st.sem(x) for x in ("scored", "masked", "shifted", "exped", "normed"))
        turned, copied, product, stored, v_step = (
            st.sem(x) for x in ("turned", "copied", "product", "stored", "v_step"))
        nch = keys // P
        m = st.sb("m", [P, 2, keys])
        p = st.sb("p", [P, 2, keys])
        pn = st.sb("pn", [P, 2, keys])
        pt = st.sb("pt", [P, 2, nch, P])
        small = st.sb("small", [P, 2, 6])
        s_ps = st.ps("s", [P, 2, 512])
        t_ps = st.ps("t", [P, 2, 512])
        o_ps = st.ps("o", [P, 2, 512])
        block = st.ctx.enter_context(nc.Block())

        def width(h):
            return h.out.shape[0]

        @block.tensor
        def _(pe):
            def score(n):
                h, t = units[n]
                if n >= 2:
                    pe.wait_ge(masked, n - 1)
                for i, (q, k) in enumerate(h.qk):
                    mm = pe.matmul(s_ps[:, n % 2, 0:keys], q[:, t * P:(t + 1) * P], k,
                                   start=i == 0, stop=i == len(h.qk) - 1)
                mm.then_inc(scored, 1)

            def turn(n):
                t = units[n][1]
                pe.wait_ge(normed, n + 1)
                if n >= 2:
                    pe.wait_ge(copied, n - 1)
                for c in chunks_of[t]:
                    mm = pe.transpose(t_ps[:, n % 2, c * P:(c + 1) * P], pn[:, n % 2, c * P:(c + 1) * P], K.ident[:])
                mm.then_inc(turned, 1)

            def combine(n):
                h, t = units[n]
                pe.wait_ge(copied, n + 1)
                if n >= 2:
                    pe.wait_ge(stored, n - 1)
                at = h.out.base_partition() if callable(h.out.base_partition) else h.out.base_partition
                cs = chunks_of[t]
                for c in cs:
                    mm = pe.matmul(o_ps[at:at + width(h), n % 2, 0:P], h.v(c), pt[:, n % 2, c],
                                   start=c == cs[0], stop=c == cs[-1])
                mm.then_inc(product, 1)

            for n in range(len(units) + 2):
                if n < len(units):
                    score(n)
                if 1 <= n <= len(units):
                    turn(n - 1)
                if n >= 2:
                    combine(n - 2)

        @block.vector
        def _(dve):
            chain = Chain(dve, v_step)

            def maximum(n):
                h, t = units[n]
                z = small[:, n % 2]
                dve.wait_ge(scored, n + 1)
                if n >= 2:
                    dve.wait_ge(exped, n - 1)
                dve.scalar_tensor_tensor(out=m[:, n % 2], in0=s_ps[:, n % 2, 0:keys], scalar=scale,
                                         in1=mask[:, t], op0=ALU.mult, op1=ALU.add).then_inc(masked, 1)
                dve.wait_ge(masked, n + 1)
                chain(dve.tensor_reduce(z[:, 0:1], m[:, n % 2], AX_X, ALU.max))
                bound = z[:, 0:1] if h.sink is None else h.sink
                dve.tensor_scalar(z[:, 1:2], z[:, 0:1], bound, -1.0, ALU.max, ALU.mult).then_inc(shifted, 1)

            def norm(n):
                h, t = units[n]
                z = small[:, n % 2]
                dve.wait_ge(exped, n + 1)
                total = z[:, 2:3]
                if h.sink is not None:
                    chain(dve.tensor_tensor(z[:, 4:5], z[:, 2:3], z[:, 3:4], ALU.add))
                    total = z[:, 4:5]
                chain(dve.reciprocal(z[:, 5:6], total))
                if n >= 2:
                    dve.wait_ge(turned, n - 1)
                dve.tensor_scalar(pn[:, n % 2], p[:, n % 2], z[:, 5:6], None, ALU.mult).then_inc(normed, 1)

            for n in range(len(units) + 1):
                if n < len(units):
                    maximum(n)
                if n >= 1:
                    norm(n - 1)

        @block.scalar
        def _(act):
            def exps(n):
                h, t = units[n]
                z = small[:, n % 2]
                act.wait_ge(shifted, n + 1)
                if n >= 2:
                    act.wait_ge(normed, n - 1)
                ins = act.activation(p[:, n % 2], m[:, n % 2], ACT.Exp, bias=z[:, 1:2], accum_out=z[:, 2:3])
                if h.sink is not None:
                    ins = act.activation(z[:, 3:4], h.sink, ACT.Exp, bias=z[:, 1:2])
                ins.then_inc(exped, 1)

            def copies(n):
                h, t = units[n]
                cs = chunks_of[t]
                act.wait_ge(turned, n + 1)
                if n >= 2:
                    act.wait_ge(product, n - 1)
                act.activation(pt[:, n % 2, cs[0]:cs[-1] + 1].rearrange("p c q -> p (c q)"),
                               t_ps[:, n % 2, cs[0] * P:(cs[-1] + 1) * P], ACT.Copy).then_inc(copied, 1)

            def store(n):
                h, t = units[n]
                at = h.out.base_partition() if callable(h.out.base_partition) else h.out.base_partition
                act.wait_ge(product, n + 1)
                act.activation(h.out[:, t * P:(t + 1) * P], o_ps[at:at + width(h), n % 2, 0:P], ACT.Copy)\
                    .then_inc(stored, 1)

            for n in range(len(units) + 2):
                if n < len(units):
                    exps(n)
                if 1 <= n <= len(units):
                    copies(n - 1)
                if n >= 2:
                    store(n - 2)


class Tok:

    def __init__(self, x, gain=None, rope=(), half=0):
        self.x, self.gain, self.rope, self.half = x, gain, rope, half


def token_norm_rope(nc, K, name, items, turns):
    with stage(nc, name) as st:
        squared, summed, rooted, v_step = (st.sem(x) for x in ("squared", "summed", "rooted", "v_step"))
        done, turned, copied = (st.sem(x) for x in ("done", "turned", "copied"))
        normed = [x for x in items if x.gain is not None]
        most = max([x.x.shape[2] * x.x.shape[3] for x in normed], default=1)
        widest = max([x.x.shape[2] * x.half for x in items], default=1) or 1
        sq = st.sb("sq", [P, TT * most])
        ss = st.sb("ss", [P, 32])
        root = st.sb("root", [P, 32])
        rstd = st.sb("rstd", [P, 32])
        tmp = [st.sb(f"tmp{i}", [P, TT * widest]) for i in range(4)]
        t_ps = st.ps("t", [P, 2, 512])
        block = st.ctx.enter_context(nc.Block())

        @block.scalar
        def _(act):
            for n, it in enumerate(normed):
                heads, width = it.x.shape[2], it.x.shape[3]
                v = sq[:, 0:TT * heads * width].rearrange("p (t h d) -> p t h d", t=TT, h=heads)
                if n:
                    act.wait_ge(summed, n)
                act.activation(v, it.x, ACT.Square).then_inc(squared, 1)
                act.wait_ge(summed, n + 1)
                act.activation(root[:, 0:TT * heads], ss[:, 0:TT * heads], ACT.Sqrt, bias=K.eps[:],
                               scale=1.0 / width).then_inc(rooted, 1)
            for n, (src, dst) in enumerate(turns):
                act.wait_ge(turned, n + 1)
                act.activation(dst, t_ps[0:dst.shape[0], n % 2, 0:T], ACT.Copy).then_inc(copied, 1)

        @block.vector
        def _(dve):
            chain = Chain(dve, v_step)
            for n, it in enumerate(normed):
                heads, width = it.x.shape[2], it.x.shape[3]
                shape = [P, TT, heads, width]
                v = sq[:, 0:TT * heads * width].rearrange("p (n d) -> p n d", d=width)
                dve.wait_ge(squared, n + 1)
                dve.tensor_reduce(ss[:, 0:TT * heads], v, AX_X, ALU.add).then_inc(summed, 1)
                dve.wait_ge(rooted, n + 1)
                chain(dve.reciprocal(rstd[:, 0:TT * heads], root[:, 0:TT * heads]))
                r = rstd[:, 0:TT * heads].rearrange("p (t h) -> p t h", t=TT)
                for t in range(TT):
                    ins = dve.tensor_tensor(it.x[:, t], it.x[:, t],
                                            r[:, t].unsqueeze(2).to_broadcast([P, heads, width]), ALU.mult)
                chain(ins)
                for t in range(TT):
                    ins = dve.tensor_tensor(it.x[:, t], it.x[:, t],
                                            it.gain.unsqueeze(1).to_broadcast([P, heads, width]), ALU.mult)
                chain(ins)
            for it in items:
                heads, half = it.x.shape[2], it.half
                for at, cos, sin in it.rope:
                    x1, x2 = it.x[:, :, :, at:at + half], it.x[:, :, :, at + half:at + 2 * half]
                    a, b, c, d = (x[:, 0:TT * heads * half].rearrange("p (t h e) -> p t h e", t=TT, h=heads)
                                  for x in tmp)
                    for t in range(TT):
                        cs = cos[:, t].unsqueeze(1).to_broadcast([P, heads, half])
                        sn = sin[:, t].unsqueeze(1).to_broadcast([P, heads, half])
                        dve.tensor_tensor(a[:, t], x1[:, t], cs, ALU.mult)
                        dve.tensor_tensor(b[:, t], x2[:, t], sn, ALU.mult)
                        dve.tensor_tensor(c[:, t], x2[:, t], cs, ALU.mult)
                        ins = dve.tensor_tensor(d[:, t], x1[:, t], sn, ALU.mult)
                    chain(ins)
                    for t in range(TT):
                        dve.tensor_tensor(x1[:, t], a[:, t], b[:, t], ALU.subtract)
                        ins = dve.tensor_tensor(x2[:, t], c[:, t], d[:, t], ALU.add)
                    chain(ins)
            dve.engine_nop().then_inc(done, 1)

        @block.tensor
        def _(pe):
            pe.wait_ge(done, 1)
            for n, (src, dst) in enumerate(turns):
                if n >= 2:
                    pe.wait_ge(copied, n - 1)
                for t in range(TT):
                    mm = pe.transpose(t_ps[0:dst.shape[0], n % 2, t * P:(t + 1) * P], src[:, t], K.ident[:])
                mm.then_inc(turned, 1)


def angles(nc, K, dram, cos, sin):
    with stage(nc, "angles") as st:
        pos_in, v_step, reduced, sined = (st.sem(x) for x in ("pos_in", "v_step", "reduced", "sined"))
        pos = st.sb("pos", [P, TT], I32)
        posf = st.sb("posf", [P, TT])
        ang = st.sb("ang", [P, TT, 32])
        turn = st.sb("turn", [P, TT, 32])
        whole = st.sb("whole", [P, TT, 32], I32)
        wholef = st.sb("wholef", [P, TT, 32])
        tmp = st.sb("tmp", [P, TT, 32])
        rest = st.sb("rest", [P, 2, TT, 32])
        block = st.ctx.enter_context(nc.Block())
        c1 = 6.28125
        c2 = float(np.float32(np.floor((2 * np.pi - c1) * 2.0 ** 19) / 2.0 ** 19))
        c3 = float(np.float32(2 * np.pi - c1 - c2))

        @block.sync
        def _(sp):
            sp.dma_start(pos[:], dram["positions"]).then_inc(pos_in, 16)

        @block.vector
        def _(dve):
            chain = Chain(dve, v_step)
            dve.wait_ge(pos_in, 16)
            chain(dve.tensor_copy(posf[:], pos[:]))
            for t in range(TT):
                ins = dve.tensor_scalar(ang[:, t], K.row("inv_freq"), posf[:, t:t + 1], None, ALU.mult)
            chain(ins)
            for n, ahead in ((0, float(np.pi / 2)), (1, 0.0)):
                chain(dve.tensor_scalar(turn[:], ang[:], ahead, float(1 / (2 * np.pi)), ALU.add, ALU.mult))
                chain(dve.tensor_copy(whole[:], turn[:]))
                chain(dve.tensor_copy(wholef[:], whole[:]))
                chain(dve.scalar_tensor_tensor(out=tmp[:], in0=wholef[:], scalar=-c1, in1=ang[:],
                                               op0=ALU.mult, op1=ALU.add))
                chain(dve.scalar_tensor_tensor(out=turn[:], in0=wholef[:], scalar=-c2, in1=tmp[:],
                                               op0=ALU.mult, op1=ALU.add))
                chain(dve.scalar_tensor_tensor(out=tmp[:], in0=wholef[:], scalar=-c3, in1=turn[:],
                                               op0=ALU.mult, op1=ALU.add))
                chain(dve.tensor_scalar(turn[:], tmp[:], ahead, float(np.float32(3.1415925)), ALU.add, ALU.min))
                chain(dve.tensor_scalar(rest[:, n], turn[:], -float(np.float32(3.1415925)), None, ALU.max))
            dve.engine_nop().then_inc(reduced, 1)

        @block.scalar
        def _(act):
            act.wait_ge(reduced, 1)
            act.activation(cos, rest[:, 0], ACT.Sin)
            act.activation(sin, rest[:, 1], ACT.Sin).then_inc(sined, 1)


def mla_moba(nc, K, dram):
    with ExitStack() as keep:
        def sb(name, shape, dt=F32):
            return keep.enter_context(nc.sbuf_tensor(f"mla_{name}", shape, dt))

        cq, ckv, kpe = sb("cq", [P, 2, T]), sb("ckv", [P, 1, T]), sb("kpe", [P, TT, ROPE])
        qd, kd, vd = sb("qd", [P, TT, 512]), sb("kd", [P, TT, 512]), sb("vd", [P, TT, 512])
        cqn, ckvn = sb("cqn", [P, 2, T]), sb("ckvn", [P, 1, T])
        qc, kc = sb("qc", [P, TT, CH, QK]), sb("kc", [P, TT, CH, QK])
        kv = sb("kv", [P, TT, CH, 2 * P])
        cos, sin = sb("cos", [P, TT, 32]), sb("sin", [P, TT, 32])
        qt, kt = sb("qt", [P, 8, T]), sb("kt", [P, 8, T])
        qpt, kpt = sb("qpt", [ROPE, CH, T]), sb("kpt", [ROPE, CH, T])
        mix = sb("mix", [P, DC, T])
        causal = sb("causal", [P, TT, T])
        normalize(nc, K, "l1_norm", K.x, K.xn, K.col("l1_norm_mix"))
        w, x = dram["l1_w_in"], chunked(K.xn)
        project(nc, "l1_in", [
            Proj(w, 0, 256, x, "f", cq[:]),
            Proj(w, 256, 128, x, "f", ckv[:]),
            Proj(w, 384, ROPE, x, "t", kpe[:]),
            Proj(w, 448, 512, x, "t", qd[:]),
            Proj(w, 960, 512, x, "t", kd[:]),
            Proj(w, 1472, 512, x, "t", vd[:]),
        ])
        angles(nc, K, dram, cos[:], sin[:])
        normalize(nc, K, "cq_norm", cq, cqn, K.col("l1_mla_cq_norm"), width=256)
        normalize(nc, K, "ckv_norm", ckv, ckvn, K.col("l1_mla_ckv_norm"), width=128)
        qcf, kvf = (a[:].rearrange("p t h d -> p t (h d)") for a in (qc, kv))
        project(nc, "uq", [
            Proj(dram["l1_mla_w_uq"], 0, 384, chunked(cqn), "t", qcf[:, :, 0:384]),
            Proj(dram["l1_mla_w_uq"], 384, 384, chunked(cqn), "t", qcf[:, :, 384:768]),
            Proj(dram["l1_mla_w_ukv"], 0, 512, chunked(ckvn), "t", kvf[:, :, 0:512]),
            Proj(dram["l1_mla_w_ukv"], 512, 512, chunked(ckvn), "t", kvf[:, :, 512:1024]),
        ])
        with stage(nc, "mla_keys") as st:
            cleared, half = st.sem("cleared"), st.sem("half")
            block = st.ctx.enter_context(nc.Block())

            @block.vector
            def _(dve):
                for t in range(TT):
                    dve.tensor_copy(kc[:, t, :, 0:NOPE], kv[:, t, :, 0:NOPE])
                    dve.tensor_copy(kc[:, t, :, NOPE:QK], kpe[:, t].unsqueeze(1).to_broadcast([P, CH, ROPE]))

            @block.gpsimd
            def _(pool):
                pool.memset(causal[:], 0.0).then_inc(cleared, 1)
                pool.wait_ge(cleared, 1)
                pool.affine_select(out=causal[:], in_=causal[:], compare_op=ALU.is_ge, fill=NEG, base=0,
                                   pattern=[[P, TT], [-1, T]], channel_multiplier=1)

        qd4, kd4, vd4 = (a[:].rearrange("p t (h d) -> p t h d", h=4) for a in (qd, kd, vd))
        rope = ((NOPE, cos, sin),)
        token_norm_rope(nc, K, "mla_qk", [
            Tok(qc[:], K.row("l1_mla_q_norm"), rope, ROPE // 2), Tok(kc[:], K.row("l1_mla_k_norm"), rope, ROPE // 2),
            Tok(qd4, K.row("l1_moba_q_norm")), Tok(kd4, K.row("l1_moba_k_norm")),
        ], [(qc[:, :, h, 0:NOPE], qt[:, h]) for h in range(4)] + [(kc[:, :, h, 0:NOPE], kt[:, h]) for h in range(4)]
          + [(qc[:, :, h, NOPE:QK], qpt[:, h]) for h in range(4)] + [(kc[:, :, h, NOPE:QK], kpt[:, h]) for h in range(4)]
          + [(qd4[:, :, h], qt[:, 4 + h]) for h in range(4)] + [(kd4[:, :, h], kt[:, 4 + h]) for h in range(4)])

        def value(a, h, lo):
            return lambda c: a[:, c, h, lo:lo + P]

        seen = [[0], [0, 1]]
        attend(nc, K, "mla", [Head([(qt[:, h], kt[:, h]), (qpt[:, h], kpt[:, h])], value(kv, h, NOPE), mix[:, h])
                              for h in range(4)], T, seen, causal, float(QK) ** -0.5)
        attend(nc, K, "moba", [Head([(qt[:, 4 + h], kt[:, 4 + h])], value(vd4, h, 0), mix[:, 4 + h])
                               for h in range(4)], T, seen, causal, float(P) ** -0.5)
        project_residual(nc, K, "l1_out", dram["l1_w_out"], mix)


def modulation(nc, K, dram, layer, M):
    name, slots, per = f"mod{layer}", 4, 2
    blocks = MT // per
    with stage(nc, name) as st:
        loaded = [st.sem(f"loaded{s}") for s in range(slots)]
        silued, product, copied, v_step = (st.sem(x) for x in ("silued", "product", "copied", "v_step"))
        w = st.sb("w", [P, slots, DC, per * P])
        cond = st.sb("cond", [P, DC, 2])
        acc = st.ps("acc", [P, slots, 512])
        block = st.ctx.enter_context(nc.Block())

        @block.sync
        def _(sp):
            for s in range(slots):
                sp.dma_start(w[:, s].rearrange("p c n -> p (c n)"), dram["w_mod"][layer, s]).then_inc(loaded[s], 16)
            with sp.Fori(1, blocks // slots) as i:
                for s in range(slots):
                    sp.wait_ge(product, i * slots + s - (slots - 1))
                    sp.dma_start(w[:, s].rearrange("p c n -> p (c n)"), dram["w_mod"][layer, i * slots + s])\
                        .then_inc(loaded[s], 16)

        @block.scalar
        def _(act):
            act.activation(cond[:, :, 0], K.col("c_2"), ACT.Silu).then_inc(silued, 1)
            act.activation(cond[:, :, 1], K.col("c_ctx_2"), ACT.Silu).then_inc(silued, 1)

        @block.tensor
        def _(pe):
            def one(s):
                for j in range(per):
                    for c in range(DC):
                        mm = pe.matmul(acc[:, s, 2 * j:2 * j + 2], w[:, s, c, j * P:(j + 1) * P], cond[:, c],
                                       start=c == 0, stop=c == DC - 1)
                mm.then_inc(product, 1)

            pe.wait_ge(silued, 2)
            for s in range(slots):
                pe.wait_ge(loaded[s], 16)
                one(s)
            with pe.Fori(1, blocks // slots) as i:
                for s in range(slots):
                    pe.wait_ge(loaded[s], i * 16 + 16)
                    pe.wait_ge(copied, i * slots + s - (slots - 1))
                    one(s)

        @block.vector
        def _(dve):
            chain = Chain(dve, v_step)
            with dve.Fori(0, blocks // slots) as i:
                for s in range(slots):
                    dve.wait_ge(product, i * slots + s + 1)
                    dve.tensor_copy(M.m[:, bass.ds((i * slots + s) * per, per), :],
                                    acc[:, s, 0:2 * per].rearrange("p (j s) -> p j s", s=2)).then_inc(copied, 1)
            dve.wait_ge(copied, blocks)
            bias = K.col("b_mod_2")[:, layer * MT:(layer + 1) * MT]
            chain(dve.tensor_tensor(M.m[:], M.m[:], bias.unsqueeze(2).to_broadcast([P, MT, 2]), ALU.add))
            for k in range(3):
                g = K.col("norm_g_2")[:, (layer * 3 + k) * DC:(layer * 3 + k + 1) * DC]
                for s in range(2):
                    scale = M.m[:, (3 * k + 1) * DC:(3 * k + 2) * DC, s]
                    dve.scalar_tensor_tensor(out=M.gain[:, k, s], in0=scale, scalar=1.0, in1=g,
                                             op0=ALU.add, op1=ALU.mult)
            for n, k in enumerate((2, 8)):
                for s in range(2):
                    dve.tensor_scalar(M.half[:, n, s], M.m[:, k * DC:(k + 1) * DC, s], 0.5, None, ALU.mult)
            dve.tensor_tensor(M.pool[:], M.m[:, 5 * DC:6 * DC, 0], K.col("pool_scale_2"), ALU.mult)


def swiglu(nc, K, name, wi, wo, h, streams):
    tokens = h.shape[2]
    banks = tokens // T
    with stage(nc, name) as st:
        w1 = [st.sem(f"w1_loaded{s}") for s in range(2)]
        w2 = [st.sem(f"w2_loaded{s}") for s in range(2)]
        product, silued, gated, out_sum = (st.sem(x) for x in ("product", "silued", "gated", "out_sum"))
        wa = st.sb("wi", [P, 2, DC, 2, P])
        wb = st.sb("wo", [P, 2, D])
        g = st.sb("g", [P, FT, tokens])
        sl = st.sb("silu", [P, 2, tokens])
        acc = st.ps("acc", [P, 8, 512])
        au = [acc[:, 2 * banks * k:2 * banks * (k + 1)] for k in range(2)]
        half = lambda k, j: acc[:, 2 * k + j, 0:tokens]
        block = st.ctx.enter_context(nc.Block())

        @block.sync
        def _(sp):
            for k in range(2):
                sp.dma_start(wa[:, k].rearrange("p c j n -> p (c j n)"), wi[k]).then_inc(w1[k], 16)
            with sp.Fori(1, FT // 2) as i:
                for k in range(2):
                    sp.wait_ge(product, i * 2 + k - 1)
                    sp.dma_start(wa[:, k].rearrange("p c j n -> p (c j n)"), wi[i * 2 + k]).then_inc(w1[k], 16)
            for k in range(2):
                sp.dma_start(wb[:, k], wo[k]).then_inc(w2[k], 16)
            with sp.Fori(1, FT // 2) as i:
                for k in range(2):
                    sp.wait_ge(out_sum, i * 2 + k - 1)
                    sp.dma_start(wb[:, k], wo[i * 2 + k]).then_inc(w2[k], 16)

        @block.tensor
        def _(pe):
            def up(k, value):
                pe.wait_ge(w1[k], value)
                for j in range(2):
                    for c in range(DC):
                        mm = pe.matmul(half(k, j), wa[:, k, c, j], h[:, c], start=c == 0, stop=c == DC - 1)
                mm.then_inc(product, 1)

            for k in range(2):
                up(k, 16)
            with pe.Fori(1, FT // 2) as i:
                for k in range(2):
                    pe.wait_ge(gated, i * 2 + k - 1)
                    up(k, i * 16 + 16)

            def down(k, tile, value, first):
                pe.wait_ge(w2[k], value)
                for c in range(DC):
                    at = c * tokens
                    out = acc[:, at // 512, at % 512:at % 512 + tokens]
                    mm = pe.matmul(out, wb[:, k, c * P:(c + 1) * P], g[:, tile], start=first and at % 512 == 0,
                                   stop=False, skip_group_check=True)
                mm.then_inc(out_sum, 1)

            pe.wait_ge(gated, FT)
            for k in range(2):
                down(k, k, 16, k == 0)
            with pe.Fori(1, FT // 2) as i:
                for k in range(2):
                    down(k, i * 2 + k, i * 16 + 16, False)

        @block.scalar
        def _(act):
            def silu(i, k):
                act.wait_ge(product, i * 2 + k + 1)
                act.activation(sl[:, k], half(k, 0), ACT.Silu).then_inc(silued, 1)

            for k in range(2):
                silu(0, k)
            with act.Fori(1, FT // 2) as i:
                for k in range(2):
                    act.wait_ge(gated, i * 2 + k - 1)
                    silu(i, k)

        @block.vector
        def _(dve):
            with dve.Fori(0, FT // 2) as i:
                for k in range(2):
                    dve.wait_ge(silued, i * 2 + k + 1)
                    dve.tensor_tensor(g[:, bass.ds(i * 2 + k, 1), :].squeeze(1), half(k, 1), sl[:, k], ALU.mult)\
                        .then_inc(gated, 1)
            dve.wait_ge(out_sum, FT)
            for c in range(DC):
                for n, (x, gate) in enumerate(streams):
                    at = c * tokens + n * T
                    dve.scalar_tensor_tensor(out=x[:, c], in0=acc[:, at // 512, at % 512:at % 512 + T],
                                             scalar=gate[:, c:c + 1], in1=x[:, c], op0=ALU.mult, op1=ALU.add)


def window_gla(nc, K, dram, M, ctx):
    with ExitStack() as keep:
        def sb(name, shape, dt=F32):
            return keep.enter_context(nc.sbuf_tensor(f"wg_{name}", shape, dt))

        h, hc = K.xn, sb("hc", [P, DC, T])
        mix = sb("mix", [P, DC, T])
        normalize(nc, K, "wg_norm", K.x, h, M.gain[:, 1, 0], M.m[:, 3 * DC:4 * DC, 0])
        normalize(nc, K, "wg_cnorm", ctx, hc, M.gain[:, 1, 1], M.m[:, 3 * DC:4 * DC, 1])
        w, x, xc = dram["w_in"], chunked(h), chunked(hc)
        gq, gk, gv = sb("gq", [P, 2, T]), sb("gk", [P, 2, 2, T]), sb("gv", [P, 2, TT, 512])
        gr, zg = sb("gr", [P, 4, T]), sb("zg", [16, 2, 2, T])
        with ExitStack() as early:
            def eb(name, shape, dt=F32):
                return early.enter_context(nc.sbuf_tensor(f"wg_{name}", shape, dt))

            q = eb("q", [P, TT, 512])
            kv = eb("kv", [P, 2, TT, 256])
            qt, kt = eb("qt", [P, 4, T]), eb("kt", [P, WG, 2 * T])
            table, mask = eb("table", [P, TT, 4, 16]), eb("mask", [P, TT, 2 * T])
            full = eb("full", [P, TT, 2 * T])
            blocks = [
                Proj(w, 0, 512, x, "t", q[:]), Proj(w, 512, 256, x, "t", kv[:, 0]), Proj(w, 512, 256, xc, "t", kv[:, 1]),
                Proj(w, 768, 256, x, "f", gq[:]), Proj(w, 1024, 256, x, "f", gk[:, 0]),
                Proj(w, 1024, 256, xc, "f", gk[:, 1]), Proj(w, 1280, 512, x, "t", gv[:, 0]),
                Proj(w, 1280, 512, xc, "t", gv[:, 1]),
            ]
            blocks += [Proj(w, 2304 + 16 * d, 16, y, "f", zg[:, d, s:s + 1]) for d in range(2) for s, y in ((0, x), (1, xc))]
            blocks += [Proj(w, 1792, 512, x, "f", gr[:], ACT.Silu)]
            project(nc, "wg_in", blocks)
            with stage(nc, "wg_mask") as st:
                table_in, step = st.sem("table_in"), st.sem("step")
                block = st.ctx.enter_context(nc.Block())

                @block.sync
                def _(sp):
                    sp.dma_start(table[:], dram["rope_table"]).then_inc(table_in, 16)
                    sp.wait_ge(table_in, 16)

                @block.gpsimd
                def _(pool):
                    pool.memset(full[:], 0.0).then_inc(step, 1)
                    pool.memset(mask[:, :, T:2 * T], 0.0)
                    pool.wait_ge(step, 1)
                    pool.affine_select(out=full[:, :, 0:T], in_=full[:, :, 0:T], compare_op=ALU.is_ge, fill=NEG,
                                       base=P, pattern=[[P, TT], [-1, T]], channel_multiplier=1).then_inc(step, 1)
                    pool.wait_ge(step, 2)
                    pool.affine_select(out=mask[:, :, 0:T], in_=full[:, :, 0:T], compare_op=ALU.is_ge, fill=NEG,
                                       base=P, pattern=[[-P, TT], [1, T]], channel_multiplier=-1)

            q4 = q[:].rearrange("p t (h d) -> p t h d", h=WH)
            k4 = kv[:, 0, :, 0:128].rearrange("p t (h d) -> p t h d", h=WG)
            rope = ((0, table[:, :, 0], table[:, :, 1]), (32, table[:, :, 2], table[:, :, 3]))
            turns = [(q[:, :, P * i:P * (i + 1)], qt[:, i]) for i in range(4)]
            for g in range(WG):
                for at in (0, WD):
                    turns.append((k4[:, :, g], kt[at:at + WD, g, 0:T]))
                    turns.append((kv[:, 1, :, g * WD:(g + 1) * WD], kt[at:at + WD, g, T:2 * T]))
            token_norm_rope(nc, K, "wg_rope", [Tok(q4, None, rope, 16), Tok(k4, None, rope, 16)], turns)
            heads = []
            for i in range(WH):
                at, g = WD * (i % 2), i // (WH // WG)

                def v(c, g=g):
                    return kv[:, c // TT, c % TT, 128 + g * WD:128 + (g + 1) * WD]

                heads.append(Head([(qt[at:at + WD, i // 2], kt[at:at + WD, g])], v, mix[at:at + WD, i // 2],
                                  K.row("sink_2")[:, i:i + 1]))
            attend(nc, K, "window", heads, 2 * T, [[0, 1, 2, 3]] * 2, mask, WD ** -0.5)
        la = sb("la", [P, 2, 2, 2, T])
        log_decays(nc, K, dram, zg, la)
        gla(nc, K, gq, gk, gv, gr, la, mix)
        project_residual(nc, K, "wg_out", dram["w_out"], mix, M.m[:, 5 * DC:6 * DC, 0])


def log_decays(nc, K, dram, zg, la):
    with stage(nc, "decays") as st:
        loaded, product, biased, absed, exped, logged, v_step = (
            st.sem(x) for x in ("loaded", "product", "biased", "absed", "exped", "logged", "v_step"))
        w = st.sb("w", [16, 2, 256])
        z = st.sb("z", [P, 4, 2 * T])
        neg = st.sb("neg", [P, 4, 2 * T])
        ab = st.sb("ab", [P, 4, 2 * T])
        acc = st.ps("acc", [P, 4, 2 * T])
        block = st.ctx.enter_context(nc.Block())

        @block.sync
        def _(sp):
            sp.dma_start(w[:], dram["w_a2"]).then_inc(loaded, 16)

        @block.tensor
        def _(pe):
            pe.wait_ge(loaded, 16)
            for n in range(4):
                d, s = divmod(n, 2)
                for f in range(2):
                    mm = pe.matmul(acc[:, n, f * T:(f + 1) * T], w[:, d, f * P:(f + 1) * P], zg[:, d, s],
                                   start=True, stop=True)
            mm.then_inc(product, 1)

        @block.scalar
        def _(act):
            act.wait_ge(product, 1)
            for n in range(4):
                b = K.col("b_a_f_2" if n < 2 else "b_a_b_2")
                for f in range(2):
                    ins = act.activation(z[:, n, f * T:(f + 1) * T], acc[:, n, f * T:(f + 1) * T], ACT.Identity,
                                         bias=b[:, f:f + 1])
            ins.then_inc(biased, 1)
            act.wait_ge(absed, 1)
            act.activation(neg[:], ab[:], ACT.Exp, scale=-1.0).then_inc(exped, 1)
            act.wait_ge(exped, 1)
            act.activation(ab[:], neg[:], ACT.Ln, bias=K.ones[:, 0:1]).then_inc(logged, 1)

        @block.vector
        def _(dve):
            chain = Chain(dve, v_step)
            dve.wait_ge(biased, 1)
            dve.scalar_tensor_tensor(out=ab[:], in0=z[:], scalar=-1.0, in1=z[:], op0=ALU.mult, op1=ALU.max)\
                .then_inc(absed, 1)
            dve.wait_ge(logged, 1)
            chain(dve.scalar_tensor_tensor(out=neg[:], in0=z[:], scalar=0.0, in1=ab[:], op0=ALU.min,
                                           op1=ALU.subtract))
            dve.tensor_scalar(la[:].rearrange("p d s f t -> p (d s) (f t)"), neg[:], 1.0 / 16.0, None, ALU.mult)


def gla(nc, K, q, k, v, gr, la, mix):
    with stage(nc, "gla") as st:
        made, v_step, decayed, exped = (st.sem(x) for x in ("made", "v_step", "decayed", "exped"))
        keyed, turned, copied, summed = (st.sem(x) for x in ("keyed", "turned", "copied", "summed"))
        scored, selected, stated, out_sum = (st.sem(x) for x in ("scored", "selected", "stated", "out_sum"))
        squared, normed, rooted = (st.sem(x) for x in ("squared", "normed", "rooted"))
        upto = st.sb("upto", [P, 2, P])
        pairs = st.sb("pairs", [P, 2, P], I32)
        carry_on = st.sb("carry_on", [P, 4 * T + BC])
        g = st.sb("g", [P, 2, 2, T])
        e = st.sb("e", [P, 3, 2, 2, T])
        qg, kg, ke = st.sb("qg", [P, 2, T]), st.sb("kg", [P, 2, T]), st.sb("ke", [P, 2, 2, T])
        dec = st.sb("dec", [P, 4, NBC])
        ket = st.sb("ket", [P, 2, 2, TT, P])
        att = st.sb("att", [P, 2, 2, TT, P])
        carry = st.sb("carry", [P, 2, P])
        states = st.sb("states", [P, NBC, 2, P])
        sq, root = st.sb("sq", [P, 2, 2, T]), st.sb("root", [P, 2, 2, T])
        t_ps = st.ps("t", [P, 2, 512])
        d_ps = st.ps("d", [P, 4, 512])
        o_ps = st.ps("o", [P, 2, 2, T])
        block = st.ctx.enter_context(nc.Block())
        sixteenth = lambda a: a.rearrange("p s f (n t) -> p (s f n) t", t=BC)
        flat = lambda a: a.rearrange("p s f t -> p (s f t)")
        add_of = lambda s, n, f: d_ps[:, 2 * s + n % 2, ((n // 2) * 2 + f) * P:((n // 2) * 2 + f + 1) * P]

        @block.gpsimd
        def _(pool):
            pool.memset(upto[:], 1.0).then_inc(made, 1)
            pool.memset(carry_on[:], 1.0).then_inc(made, 1)
            pool.wait_ge(made, 2)
            pool.memset(carry_on[:].rearrange("p (n t) -> p n t", t=BC)[:, :, 0:1], 0.0).then_inc(made, 1)
            pool.affine_select(out=upto[:, 0], in_=upto[:, 0], compare_op=ALU.is_ge, fill=0.0, base=0,
                               pattern=[[1, P]], channel_multiplier=-1).then_inc(made, 1)
            pool.affine_select(out=upto[:, 1], in_=upto[:, 1], compare_op=ALU.is_ge, fill=0.0, base=0,
                               pattern=[[-1, P]], channel_multiplier=1).then_inc(made, 1)
            pool.wait_ge(made, 5)
            pool.memset(upto[0:BC, 0, BC:P], 0.0).then_inc(made, 1)
            pool.memset(upto[BC:P, 1, 0:BC], 0.0).then_inc(made, 1)

        @block.vector
        def _(dve):
            chain = Chain(dve, v_step)
            dve.wait_ge(made, 7)
            chain(dve.tensor_copy(pairs[:], upto[:]))
            for d in range(2):
                last = BC - 1 if d == 0 else 0
                if d == 0:
                    chain(dve.tensor_tensor_scan(flat(g[:]), carry_on[:, 0:4 * T], flat(la[:, d]), 0.0,
                                                 ALU.mult, ALU.add))
                else:
                    chain(dve.tensor_tensor_scan(flat(g[:])[:, ::-1], carry_on[:, 1:4 * T + 1][:, ::-1],
                                                 flat(la[:, d])[:, ::-1], 0.0, ALU.mult, ALU.add))
                gl = sixteenth(g[:])[:, :, last:last + 1]
                dve.tensor_tensor(sixteenth(e[:, 2]), gl.to_broadcast([P, 16, BC]), sixteenth(g[:]), ALU.subtract)\
                    .then_inc(decayed, 1)
                if d == 1:
                    dve.wait_ge(out_sum, 1)
                dve.memset(att[:], 0.0)
                dve.wait_ge(exped, d + 1)
                dve.scalar_tensor_tensor(out=qg[:], in0=q[:], scalar=float(BC) ** -0.5, in1=e[:, 0, 0],
                                         op0=ALU.mult, op1=ALU.mult)
                dve.tensor_tensor(kg[:], k[:, 0], e[:, 1, 0], ALU.mult)
                dve.tensor_tensor(ke[:], k[:], e[:, 2], ALU.mult).then_inc(keyed, 1)
                dve.wait_ge(scored, d + 1)
                dve.copy_predicated(att[:].rearrange("p a b t i -> p (a b t) i"),
                                    pairs[:, d].unsqueeze(1).to_broadcast([P, 8, P]),
                                    t_ps[:].rearrange("p a (b i) -> p (a b) i", i=P)).then_inc(selected, 1)
                chain(dve.memset(carry[:], 0.0))
                order = list(range(NBC)) if d == 0 else list(range(NBC))[::-1]
                for s in (1, 0):
                    for i, n in enumerate(order):
                        if s == 0 and i == 0:
                            chain(dve.tensor_copy(states[:, n], carry[:]))
                        if s == 0 and i == NBC - 1:
                            break
                        src = carry if s == 1 else states[:, n]
                        dst = carry if s == 1 else states[:, order[i + 1]]
                        for f in range(2):
                            ins = dve.scalar_tensor_tensor(out=dst[:, f], in0=src[:, f],
                                                           scalar=dec[:, 2 * s + f, n:n + 1],
                                                           in1=add_of(s, n, f), op0=ALU.mult, op1=ALU.add)
                        chain(ins)
                dve.engine_nop().then_inc(stated, 1)
            dve.wait_ge(rooted, 1)
            chain(dve.reciprocal(sq[:], root[:]))
            chain(dve.tensor_tensor(root[:], o_ps[:], sq[:], ALU.mult))
            for h in range(4):
                dve.scalar_tensor_tensor(out=mix[:, 4 + h], in0=root[:, h % 2, h // 2], scalar=K.col("gla_g_2"),
                                         in1=gr[:, h], op0=ALU.mult, op1=ALU.mult)

        @block.scalar
        def _(act):
            for d in range(2):
                last = BC - 1 if d == 0 else 0
                act.wait_ge(decayed, d + 1)
                if d:
                    act.wait_ge(stated, d)
                act.activation(dec[:], g[:].rearrange("p s f (n t) -> p (s f) n t", t=BC)[:, :, :, last],
                               ACT.Exp)
                act.activation(e[:, 0, 0], g[:, 0], ACT.Exp)
                act.activation(e[:, 1, 0], g[:, 0], ACT.Exp, scale=-1.0)
                act.activation(e[:, 2], e[:, 2], ACT.Exp).then_inc(exped, 1)
                act.wait_ge(turned, d + 1)
                if d:
                    act.wait_ge(summed, d)
                act.activation(ket[:].rearrange("p s f t e -> p s (f t e)"), t_ps[:], ACT.Copy).then_inc(copied, 1)
            act.wait_ge(out_sum, 2)
            act.activation(sq[:], o_ps[:], ACT.Square).then_inc(squared, 1)
            act.wait_ge(normed, 1)
            act.activation(root[:].rearrange("p a b t -> p a (b t)"), t_ps[:], ACT.Sqrt, bias=K.eps[:],
                           scale=1.0 / P).then_inc(rooted, 1)

        @block.tensor
        def _(pe):
            for d in range(2):
                pe.wait_ge(keyed, d + 1)
                if d:
                    pe.wait_ge(selected, d)
                for s in range(2):
                    for f in range(2):
                        for t in range(TT):
                            mm = pe.transpose(t_ps[:, s, (2 * f + t) * P:(2 * f + t + 1) * P],
                                              ke[:, s, f, t * P:(t + 1) * P], K.ident[:])
                mm.then_inc(turned, 1)
                pe.wait_ge(copied, d + 1)
                if d:
                    pe.wait_ge(stated, d)
                for par in range(2):
                    for s in range(2):
                        for n in range(par, NBC, 2):
                            rows = slice(BC * par, BC * par + BC)
                            for h in range(4):
                                f, at = h // 2, BC * (h % 2)
                                mm = pe.matmul(add_of(s, n, f)[at:at + BC], ket[rows, s, f, n // 2, at:at + BC],
                                               v[rows, s, n // 2, h * P:(h + 1) * P], start=True, stop=True)
                mm.then_inc(summed, 1)
                for par in range(2):
                    rows = slice(BC * par, BC * par + BC)
                    for f in range(2):
                        for t in range(TT):
                            mm = pe.matmul(t_ps[:, par, (2 * f + t) * P:(2 * f + t + 1) * P],
                                           kg[rows, f, t * P:(t + 1) * P], qg[rows, f, t * P:(t + 1) * P],
                                           start=True, stop=True)
                mm.then_inc(scored, 1)
                pe.wait_ge(selected, d + 1)
                for par in range(2):
                    for f in range(2):
                        for t in range(TT):
                            h = 2 * f + par
                            pe.matmul(o_ps[:, par, f, t * P:(t + 1) * P], v[:, 0, t, h * P:(h + 1) * P],
                                      att[:, par, f, t], start=d == 0 and f == 0 and t == 0, stop=False,
                                      skip_group_check=True)
                pe.wait_ge(stated, d + 1)
                for par in range(2):
                    rows = slice(BC * par, BC * par + BC)
                    for f in range(2):
                        for n in range(NBC):
                            mm = pe.matmul(o_ps[:, par, f, n * BC:(n + 1) * BC], states[rows, n, f],
                                           qg[rows, f, n * BC:(n + 1) * BC], start=False, stop=d == 1,
                                           skip_group_check=True)
                mm.then_inc(out_sum, 1)
            pe.wait_ge(squared, 1)
            for a in range(2):
                mm = pe.matmul(t_ps[:, a], K.ones[:], sq[:, a].rearrange("p b t -> p (b t)"), start=True, stop=True)
            mm.then_inc(normed, 1)


def pool_mix(nc, K, dram, M):
    normalize(nc, K, "pool_norm", K.x, K.xn, M.gain[:, 1, 0], M.m[:, 3 * DC:4 * DC, 0])
    pad = 16
    wide = T + 2 * pad
    with stage(nc, "pool") as st:
        w_in, inv_in, v_step, product, ready = (st.sem(x) for x in ("w_in", "inv_in", "v_step", "product", "ready"))
        w = st.sb("w", [P, 4, 2, T])
        inv = st.sb("inv", [P, 4, T])
        a, b = st.sb("a", [P, DC, wide]), st.sb("b", [P, DC, wide])
        pooled = st.sb("pooled", [P, DC, T])
        acc = st.ps("acc", [P, DC, T])
        block = st.ctx.enter_context(nc.Block())

        @block.sync
        def _(sp):
            sp.dma_start(w[:], dram["w_pool"].rearrange("g (c p) e -> p g c e", p=P)).then_inc(w_in, 16)
            sp.dma_start(inv[:], dram["pool_inv"].partition_broadcast(P)).then_inc(inv_in, 16)

        @block.vector
        def _(dve):
            chain = Chain(dve, v_step)
            h = K.xn
            chain(dve.memset(a[:], 0.0))
            chain(dve.memset(b[:], 0.0))
            chain(dve.tensor_copy(a[:, :, pad:pad + T], h[:]))
            dve.wait_ge(inv_in, 16)
            src, dst = a, b
            for g, (back, ahead) in enumerate(((1, 0), (1, 1), (2, 2), (4, 4))):
                lo, hi = 8, wide - 8
                chain(dve.tensor_tensor(dst[:, 2 * g:, lo:hi], src[:, 2 * g:, lo - back:hi - back],
                                        src[:, 2 * g:, lo + ahead:hi + ahead], ALU.add))
                cs = slice(2 * g, 2 * g + 2)
                chain(dve.tensor_tensor(pooled[:, cs], dst[:, cs, pad:pad + T],
                                        inv[:, g:g + 1].to_broadcast([P, 2, T]), ALU.mult))
                src, dst = dst, src
            dve.tensor_tensor(pooled[:], pooled[:], h[:], ALU.subtract).then_inc(ready, 1)
            dve.wait_ge(product, 1)
            for c in range(DC):
                dve.scalar_tensor_tensor(out=K.x[:, c], in0=acc[:, c], scalar=M.pool[:, c:c + 1], in1=K.x[:, c],
                                         op0=ALU.mult, op1=ALU.add)

        @block.tensor
        def _(pe):
            pe.wait_ge(w_in, 16)
            pe.wait_ge(ready, 1)
            for g in range(4):
                for j in range(2):
                    for c in range(2):
                        mm = pe.matmul(acc[:, 2 * g + j], w[:, g, c, j * P:(j + 1) * P], pooled[:, 2 * g + c],
                                       start=c == 0, stop=c == 1)
            mm.then_inc(product, 1)


def second_block(nc, K, dram, out):
    with ExitStack() as keep:
        def sb(name, shape, dt=F32):
            return keep.enter_context(nc.sbuf_tensor(f"b2_{name}", shape, dt))

        M = Store()
        M.m, M.gain = sb("m", [P, MT, 2]), sb("gain", [P, 3, 2, DC])
        M.half, M.pool = sb("half", [P, 2, 2, DC]), sb("pool", [P, DC])
        for layer in range(2):
            modulation(nc, K, dram, layer, M)
            shift = lambda k, s: M.m[:, 3 * k * DC:(3 * k + 1) * DC, s]
            if layer == 0:
                with ExitStack() as with_ctx:
                    ctx = with_ctx.enter_context(nc.sbuf_tensor("ctx_stream", [P, DC, T], F32))
                    with ExitStack() as both:
                        h2 = both.enter_context(nc.sbuf_tensor("h_both", [P, DC, 2 * T], F32))
                        load_ctx(nc, dram, ctx)
                        normalize(nc, K, "f1_norm", K.x, h2[:, :, 0:T], M.gain[:, 0, 0], shift(0, 0))
                        normalize(nc, K, "f1_cnorm", ctx, h2[:, :, T:2 * T], M.gain[:, 0, 1], shift(0, 1))
                        swiglu(nc, K, "ffn1_0", dram["ffn1_wi"][layer], dram["ffn1_wo"][layer], h2,
                               [(K.x, M.half[:, 0, 0]), (ctx, M.half[:, 0, 1])])
                    window_gla(nc, K, dram, M, ctx)
            else:
                normalize(nc, K, "f1_norm1", K.x, K.xn, M.gain[:, 0, 0], shift(0, 0))
                swiglu(nc, K, "ffn1_1", dram["ffn1_wi"][layer], dram["ffn1_wo"][layer], K.xn, [(K.x, M.half[:, 0, 0])])
                pool_mix(nc, K, dram, M)
            normalize(nc, K, f"f2_norm{layer}", K.x, K.xn, M.gain[:, 2, 0], shift(2, 0))
            swiglu(nc, K, f"ffn2_{layer}", dram["ffn2_wi"][layer], dram["ffn2_wo"][layer], K.xn,
                   [(K.x, M.half[:, 1, 0])])
    normalize(nc, K, "final_norm", K.x, K.xn, K.col("final_g_2"))
    store(nc, K.xn, out)


def load_ctx(nc, dram, ctx):
    with stage(nc, "load_ctx") as st:
        loaded = st.sem("loaded")
        block = st.ctx.enter_context(nc.Block())

        @block.sync
        def _(sp):
            sp.dma_start(ctx[:], dram["ctx"]).then_inc(loaded, 16)
            sp.wait_ge(loaded, 16)


def store(nc, src, out):
    with stage(nc, "store") as st:
        stored = st.sem("stored")
        block = st.ctx.enter_context(nc.Block())

        @block.sync
        def _(sp):
            sp.dma_start(out, src[:]).then_inc(stored, 16)
            sp.wait_ge(stored, 16)


def program(nc, dram, out):
    with ExitStack() as keep:
        K = Store()
        setup(nc, keep, dram, K)
        hgrn_gmlp(nc, K, dram)
        peer(nc, K, dram, 0)
        mla_moba(nc, K, dram)
        peer(nc, K, dram, 1)
        second_block(nc, K, dram, out)


def by_column(a):
    return np.asarray(a).reshape(-1, P).T


def layouts(a):
    feature_major = lambda x: np.ascontiguousarray(x[0].T.reshape(DC, P, T).transpose(1, 0, 2))
    half = np.arange(ROPE // 2, dtype=np.float32) / (ROPE // 2)
    inv_freq = np.float32(10000.0) ** (-half)
    rows = [inv_freq if name == "inv_freq" else np.asarray(a[name]).reshape(-1) for name, _ in ROWS]
    freqs = np.float32(10000.0) ** (-np.arange(16, dtype=np.float32) / np.float32(16))
    t = np.arange(T, dtype=np.float32)
    at = [(np.floor(t / 64)[:, None] * freqs).astype(np.float32), ((t % 64)[:, None] * freqs).astype(np.float32)]
    table = np.stack([f(x) for x in at for f in (np.cos, np.sin)], 1).astype(np.float32)
    counts = [np.minimum(t + w // 2, T) - np.maximum(t - w // 2, 0) for w in (2, 4, 8, 16)]
    out = {
        "x": feature_major(a["x"]),
        "ctx": feature_major(a["ctx_2"]),
        "cols": np.concatenate([by_column(a[name]) for name, _ in COLS], 1),
        "rows": np.concatenate(rows),
        "positions": a["positions"].reshape(TT, P).T,
        "l0_w_in": a["l0_w_in"], "l0_w_out": a["l0_w_out"], "l1_w_in": a["l1_w_in"], "l1_w_out": a["l1_w_out"],
        "w_s": a["l0_gmlp_w_s"].transpose(2, 0, 1),
        "l1_mla_w_uq": a["l1_mla_w_uq"], "l1_mla_w_ukv": a["l1_mla_w_ukv"],
        "w_mod": a["w_mod_2"].reshape(2, DC, P, MT // 2, 2 * P).transpose(0, 3, 2, 1, 4)
        .reshape(2, MT // 2, P, DC * 2 * P),
        "w_in": a["w_in_2"][0], "w_out": a["w_out_2"][0],
        "w_a2": np.stack([a["w_a2_f_2"][0], a["w_a2_b_2"][0]], 1),
        "rope_table": table.reshape(TT, P, 4, 16).transpose(1, 0, 2, 3),
        "w_pool": a["w_pool_2"][0],
        "pool_inv": np.stack([np.float32(1) / c for c in counts]).astype(np.float32),
    }
    for n in ("ffn1", "ffn2"):
        out[f"{n}_wi"] = a[f"{n}_wi_2"].reshape(2, DC, P, 2, FT, P).transpose(0, 4, 2, 1, 3, 5)\
            .reshape(2, FT, P, DC * 2 * P)
        out[f"{n}_wo"] = a[f"{n}_wo_2"].reshape(2, FT, P, D)
    for n in ("l0", "l1"):
        out[f"{n}_peer_w_query"] = a[f"{n}_peer_w_query"]
        out[f"{n}_sub_keys"] = a[f"{n}_peer_sub_keys"].transpose(3, 0, 1, 2).reshape(P, HP, NK)
        out[f"{n}_down"] = a[f"{n}_peer_expert_down"].reshape(NK, NK // PG, PG, DC, P).transpose(1, 4, 2, 3, 0)\
            .reshape(NK // PG, P, PG * DC * NK)
        out[f"{n}_up"] = a[f"{n}_peer_expert_up"].reshape(NK, NK, D)
    return {name: np.ascontiguousarray(x) for name, x in out.items()}


def kernel(**inputs):
    import concourse.bacc as bacc
    from concourse.bass_utils import run_bass_kernel_spmd as run

    arrays = layouts({name: np.asarray(x) for name, x in inputs.items()})
    nc = bacc.Bacc("TRN2", target_bir_lowering=False, num_devices=1)
    dram = {name: nc.dram_tensor(f"in_{name}", x.shape, mybir.dt.from_np(x.dtype), kind="ExternalInput").ap()
            for name, x in arrays.items()}
    out = nc.dram_tensor("out", [P, DC, T], F32, kind="ExternalOutput").ap()
    program(nc, dram, out)
    result = run(nc, [{f"in_{name}": x for name, x in arrays.items()}], core_ids=[0])
    y = np.asarray(result.results[0]["out"])
    return np.ascontiguousarray(y.transpose(1, 0, 2).reshape(D, T).T)[None]
```

```python
from contextlib import ExitStack, contextmanager

import numpy as np

import concourse.bass as bass
from concourse import mybir

F32 = mybir.dt.float32
I32 = mybir.dt.int32
U32 = mybir.dt.uint32
F32R = mybir.dt.float32r
ALU = mybir.AluOpType
ACT = mybir.ActivationFunctionType
AX_X = mybir.AxisListType.X

P = 128
D = 1024
DC = D // P
T = 256
TT = T // P
EPS = 1e-6
NEG = -1.0e30
LOWEST = -3.0e38

PH, NK, PK = 8, 128, 16
HP = 2 * PH
TOKS = 4

AH, HC = 4, 32
NB = T // HC
CH, NOPE, ROPE = 4, 128, 64
QK = NOPE + ROPE
FF = 2816
FT = FF // P
NMOD = 9
MT = NMOD * D // P
BC = 64
NBC = T // BC
WH, WD, WG = 8, 64, 2

COLS = [
    ("l0_norm_mix", 8), ("l0_hgrn_out_norm", 4), ("l0_norm_ffn", 8), ("l1_norm_mix", 8),
    ("l1_mla_cq_norm", 2), ("l1_mla_ckv_norm", 1), ("l1_norm_ffn", 8), ("c_2", 8), ("c_ctx_2", 8),
    ("b_mod_2", 2 * MT), ("norm_g_2", 48), ("b_a_f_2", 2), ("b_a_b_2", 2), ("gla_g_2", 1),
    ("pool_scale_2", 8), ("final_g_2", 8), ("lb_logits", 12),
]
COL_AT, NCOL = {}, 0
for _name, _n in COLS:
    COL_AT[_name] = (NCOL, NCOL + _n)
    NCOL += _n
ROWS = [
    ("l0_gmlp_v_norm", 512), ("l1_mla_q_norm", QK), ("l1_mla_k_norm", QK), ("l1_moba_q_norm", 128),
    ("l1_moba_k_norm", 128), ("sink_2", 8), ("l0_gmlp_b_s", 512), ("inv_freq", 32),
]
ROW_AT, NROW = {}, 0
for _name, _n in ROWS:
    ROW_AT[_name] = (NROW, NROW + _n)
    NROW += _n

UNIT = 1024
STAGE_SEM = 170


class Stage:

    def __init__(self, nc, ctx, name):
        self.nc, self.ctx, self.name, self.n_sems = nc, ctx, name, 0

    def sb(self, name, shape, dt=F32):
        return self.ctx.enter_context(self.nc.sbuf_tensor(f"{self.name}_{name}", shape, dt))

    def ps(self, name, shape):
        return self.ctx.enter_context(self.nc.psum_tensor(f"{self.name}_{name}", shape, F32))

    def sem(self, name):
        self.n_sems += 1
        return self.ctx.enter_context(
            self.nc.semaphore(f"{self.name}_{name}", STAGE_SEM + self.n_sems - 1))


@contextmanager
def stage(nc, name):
    with ExitStack() as ctx:
        st = Stage(nc, ctx, name)
        yield st
    nc.all_engine_barrier(sems_to_clear=range(STAGE_SEM, STAGE_SEM + st.n_sems))


class Chain:

    def __init__(self, eng, sem):
        self.eng, self.sem, self.n = eng, sem, 0

    def __call__(self, instruction):
        self.n += 1
        instruction.then_inc(self.sem, 1)
        self.eng.wait_ge(self.sem, self.n)


class Store:
    pass


def setup(nc, keep, dram, K):
    def sb(name, shape, dt=F32):
        return keep.enter_context(nc.sbuf_tensor(name, shape, dt))

    K.x = sb("x_stream", [P, DC, T])
    K.xp = sb("x_normed", [P, 2, DC, T], F32R)
    K.cols = sb("cols", [P, NCOL])
    K.ones = sb("ones", [P, P])
    K.ident = sb("ident", [P, P])
    K.iota = sb("iota", [P, P])
    K.eps = sb("eps", [P, 1])
    K.lb = sb("lower_bound", [P, AH])
    K.nlb = sb("one_less_lower_bound", [P, AH])
    K.mod = [sb(f"mod{n}", [P, MT, 2 - n]) for n in range(2)]
    K.col = lambda name: K.cols[:, COL_AT[name][0]:COL_AT[name][1]]
    K.row = lambda name: K.rows[:, ROW_AT[name][0]:ROW_AT[name][1]]

    with stage(nc, "setup") as st:
        cols_in, x_in = st.sem("cols_in"), st.sem("x_in")
        filled, v_step, exped = st.sem("filled"), st.sem("v_step"), st.sem("exped")
        cleared, shifted = st.sem("cleared"), st.sem("shifted")
        e = st.sb("e", [P, 3, AH])
        mx = st.sb("mx", [P, AH])
        mx2 = st.sb("mx2", [P, AH])
        block = st.ctx.enter_context(nc.Block())

        @block.sync
        def _(sp):
            sp.dma_start(K.cols[:], dram["cols"]).then_inc(cols_in, 16)
            sp.dma_start(K.x[:], dram["x"]).then_inc(x_in, 16)
            sp.wait_ge(x_in, 16)

        @block.gpsimd
        def _(pool):
            pool.memset(K.ones[:], 1.0)
            pool.memset(K.eps[:], EPS)
            pool.memset(K.ident[:], 0.0).then_inc(cleared, 1)
            pool.iota(K.iota[:], pattern=[[1, P]], base=0, channel_multiplier=0,
                      allow_small_or_imprecise_dtypes=True)
            pool.wait_ge(cleared, 1)
            pool.affine_select(out=K.ident[:], in_=K.ident[:], compare_op=ALU.not_equal, fill=1.0,
                               base=0, pattern=[[-1, P]], channel_multiplier=1).then_inc(filled, 1)

        @block.vector
        def _(dve):
            chain = Chain(dve, v_step)
            dve.wait_ge(cols_in, 16)
            lg = K.col("lb_logits").rearrange("p (r h) -> p r h", r=3)
            chain(dve.tensor_tensor(mx[:], lg[:, 0], lg[:, 1], ALU.max))
            chain(dve.tensor_tensor(mx2[:], mx[:], lg[:, 2], ALU.max))
            dve.tensor_tensor(e[:], lg, mx2[:].unsqueeze(1).to_broadcast([P, 3, AH]),
                              ALU.subtract).then_inc(shifted, 1)
            dve.wait_ge(exped, 1)
            chain(dve.tensor_tensor(mx[:], e[:, 0], e[:, 1], ALU.add))
            chain(dve.tensor_tensor(mx2[:], mx[:], e[:, 2], ALU.add))
            chain(dve.reciprocal(mx[:], mx2[:]))
            chain(dve.tensor_tensor(K.lb[:], e[:, 0], mx[:], ALU.mult))
            chain(dve.tensor_scalar(K.nlb[:], K.lb[:], -1.0, 1.0, ALU.mult, ALU.add))

        @block.scalar
        def _(act):
            act.wait_ge(shifted, 1)
            act.activation(e[:], e[:], ACT.Exp).then_inc(exped, 1)



def cut_hi(act, hi, v):
    return act.activation(hi, v, ACT.Copy)


def cut_lo(eng, lo, v, hi):
    return eng.tensor_tensor(lo, v, hi.bitcast(F32), ALU.subtract)


def multiply(pe, out, w_hi, w_lo, x_hi, x_lo, start, stop, lax=False):
    pe.matmul(out, w_hi, x_hi, start=start, stop=False, skip_group_check=lax)
    pe.matmul(out, w_hi, x_lo, start=False, stop=False, skip_group_check=lax)
    return pe.matmul(out, w_lo, x_hi, start=False, stop=stop, skip_group_check=lax)


class Norm:

    def __init__(self, st, K, tag, src, gain, shift=None, width=D, pair=None, raw=None, total=None):
        self.K, self.src, self.gain, self.shift, self.width = K, src, gain, shift, width
        self.pair, self.raw = pair, raw
        self.chunks, self.tokens = src.shape[1], src.shape[2]
        self.squared_a, self.squared_v, self.summed, self.rooted, self.inverted, self.scaled, self.cut, self.done = (
            st.sem(f"{tag}_{x}") for x in
            ("squared_a", "squared_v", "summed", "rooted", "inverted", "scaled", "cut", "done"))
        self.sq = st.sb(f"{tag}_sq", [P, self.chunks, self.tokens])
        self.root = st.sb(f"{tag}_root", [P, self.tokens])
        self.primed = st.sb(f"{tag}_primed", [P, 1])
        self.rstd = st.sb(f"{tag}_rstd", [P, self.tokens])
        self.total = st.ps(f"{tag}_total", [P, 512])[:, 0:self.tokens] if total is None else total

    def tensor(self, pe):
        for c in range(self.chunks):
            pe.wait_ge(self.squared_v if c % 2 else self.squared_a, c // 2 + 1)
            mm = pe.matmul(self.total, self.K.ones[:], self.sq[:, c], start=c == 0, stop=c == self.chunks - 1)
        mm.then_inc(self.summed, 1)

    def scalar_squares(self, act):
        for c in range(0, self.chunks, 2):
            act.activation(self.sq[:, c], self.src[:, c], ACT.Square).then_inc(self.squared_a, 1)
        act.activation(self.primed[:], self.K.eps[:], ACT.Sqrt)

    def vector_squares(self, dve):
        for c in range(1, self.chunks, 2):
            dve.tensor_tensor(self.sq[:, c], self.src[:, c], self.src[:, c], ALU.mult).then_inc(self.squared_v, 1)

    def scalar(self, act):
        act.wait_ge(self.summed, 1)
        act.activation(self.root[:], self.total, ACT.Sqrt, bias=self.K.eps[:], scale=1.0 / self.width)\
            .then_inc(self.rooted, 1)
        for c in range(self.chunks if self.pair is not None else 0):
            act.wait_ge(self.scaled, c + 1)
            if self.shift is None:
                ins = cut_hi(act, self.pair[:, 0, c], self.sq[:, c])
            else:
                ins = act.activation(self.pair[:, 0, c], self.sq[:, c], ACT.Identity, bias=self.shift[:, c:c + 1])
            ins.then_inc(self.cut, 1)

    def vector(self, dve):
        dve.wait_ge(self.rooted, 1)
        dve.reciprocal(self.rstd[:], self.root[:]).then_inc(self.inverted, 1)
        dve.wait_ge(self.inverted, 1)
        lag = 2
        for n in range(self.chunks + lag):
            if n < self.chunks:
                dve.scalar_tensor_tensor(out=self.sq[:, n], in0=self.src[:, n], scalar=self.gain[:, n:n + 1],
                                         in1=self.rstd[:], op0=ALU.mult, op1=ALU.mult).then_inc(self.scaled, 1)
            c = n - lag
            if c < 0:
                continue
            shift = 0.0 if self.shift is None else self.shift[:, c:c + 1]
            if self.pair is not None:
                dve.wait_ge(self.cut, c + 1)
                ins = dve.scalar_tensor_tensor(out=self.pair[:, 1, c], in0=self.sq[:, c], scalar=shift,
                                               in1=self.pair[:, 0, c].bitcast(F32), op0=ALU.add, op1=ALU.subtract)
            else:
                dve.wait_ge(self.scaled, c + 1)
                ins = dve.tensor_scalar(self.raw[:, c], self.sq[:, c], shift, None, ALU.add)
            ins.then_inc(self.done, 1)


class Cut:

    def __init__(self, st, tag, v, pair):
        self.v, self.pair, self.chunks = v, pair, v.shape[1]
        self.cut, self.done = st.sem(f"{tag}_cut"), st.sem(f"{tag}_done")

    def tensor(self, pe):
        pass

    def scalar_squares(self, act):
        pass

    def vector_squares(self, dve):
        pass

    def scalar(self, act):
        for c in range(self.chunks):
            cut_hi(act, self.pair[:, 0, c], self.v[:, c]).then_inc(self.cut, 1)

    def vector(self, dve):
        for c in range(self.chunks):
            dve.wait_ge(self.cut, c + 1)
            cut_lo(dve, self.pair[:, 1, c], self.v[:, c], self.pair[:, 0, c]).then_inc(self.done, 1)


class Proj:

    def __init__(self, w, c0, width, x, form, out, func=ACT.Copy, gate=None, src=0):
        self.w, self.c0, self.width, self.x, self.form, self.out = w, c0, width, x, form, out
        self.func, self.gate, self.src = func, gate, src


def project(nc, name, blocks, sources=lambda st: (), loads=()):
    raws, pairs = 6, 3
    early = 2
    units, last_of = [], []
    for b, blk in enumerate(blocks):
        chunks = blk.x.shape[2]
        step = max(1, min(chunks, UNIT // blk.width))
        units += [(b, c, min(c + step, chunks)) for c in range(0, chunks, step)]
        last_of.append(len(units) - 1)
    with stage(nc, name) as st:
        loaded = [st.sem(f"loaded{s}") for s in range(raws)]
        cut, ready, product, evacuated, hi_out = (
            st.sem(x) for x in ("cut", "ready", "product", "evacuated", "hi_out"))
        others = st.sem("others")
        raw = st.sb("raw", [P, raws, UNIT])
        hi = st.sb("hi", [P, pairs, UNIT], F32R)
        lo = st.sb("lo", [P, pairs, UNIT], F32R)
        acc = st.ps("acc", [P, 2, 2 * 512])
        src = sources(st)
        block = st.ctx.enter_context(nc.Block())

        def view(buf, n):
            b, c0, c1 = units[n]
            blk = blocks[b]
            k, size = blk.x.shape[0], (c1 - c0) * blk.width
            return buf[0:k, 0:size], buf[0:k, 0:size].rearrange("p (c n) -> p c n", n=blk.width)

        @block.sync
        def _(sp):
            for n, (b, c0, c1) in enumerate(units):
                blk = blocks[b]
                k = blk.x.shape[0]
                if n >= raws:
                    sp.wait_ge(ready, n - raws + 1)
                sp.dma_start(view(raw[:, n % raws], n)[1],
                             blk.w[c0 * k:c1 * k, blk.c0:blk.c0 + blk.width].rearrange("(c p) n -> p c n", p=k))\
                    .then_inc(loaded[n % raws], 16)
            for n, (dst, source) in enumerate(loads):
                sp.dma_start(dst, source).then_inc(others, 16)
                sp.wait_ge(others, 16 * (n + 1))

        @block.tensor
        def _(pe):
            for s in src:
                s.tensor(pe)
            waited = [0] * len(src)
            for n, (b, c0, c1) in enumerate(units):
                blk = blocks[b]
                pe.wait_ge(ready, n + 1)
                if c0 == 0 and b >= 2:
                    pe.wait_ge(evacuated, b - 1)
                wh, wl = view(hi[:, n % pairs], n)[1], view(lo[:, n % pairs], n)[1]
                for c in range(c0, c1):
                    end = c == blk.x.shape[2] - 1
                    if src and waited[blk.src] < c + 1:
                        pe.wait_ge(src[blk.src].done, c + 1)
                        waited[blk.src] = c + 1
                    xh, xl = blk.x[:, 0, c], blk.x[:, 1, c]
                    if blk.form == "t":
                        for j in range(TT):
                            js = slice(j * P, (j + 1) * P)
                            mm = multiply(pe, acc[:, b % 2, j * 512:j * 512 + blk.width], xh[:, js], xl[:, js],
                                          wh[:, c - c0], wl[:, c - c0], c == 0, end)
                    else:
                        for j in range(-(-blk.width // P)):
                            m = min(P, blk.width - j * P)
                            js = slice(j * P, j * P + m)
                            mm = multiply(pe, acc[0:m, b % 2, j * T:(j + 1) * T], wh[:, c - c0, js],
                                          wl[:, c - c0, js], xh, xl, c == 0 and j % 2 == 0, end, lax=True)
                mm.then_inc(product, 1)

        def tiles(b):
            blk = blocks[b]
            m = min(P, blk.width)
            return acc[0:m, b % 2, 0:-(-blk.width // P) * T].rearrange("p (j t) -> p j t", t=T)

        @block.scalar
        def _(act):
            def evacuate(b):
                blk = blocks[b]
                if blk.form == "+":
                    return
                act.wait_ge(product, last_of[b] + 1)
                if blk.form == "t":
                    s = acc[:, b % 2, :].rearrange("p (j n) -> p j n", n=512)[:, :, 0:blk.width]
                    act.activation(blk.out, s, blk.func).then_inc(evacuated, 1)
                elif blk.form == "f":
                    act.activation(blk.out, tiles(b), blk.func).then_inc(evacuated, 1)
                else:
                    cut_hi(act, blk.out[:, 0], tiles(b)).then_inc(hi_out, 1)

            for s in src:
                s.scalar_squares(act)
            b = 0
            for n in range(len(units)):
                if n == early:
                    for s in src:
                        s.scalar(act)
                act.wait_ge(loaded[n % raws], 16 * (n // raws + 1))
                if n >= pairs:
                    act.wait_ge(product, n - pairs + 1)
                cut_hi(act, view(hi[:, n % pairs], n)[0], view(raw[:, n % raws], n)[0]).then_inc(cut, 1)
                while b < len(blocks) and last_of[b] + pairs <= n:
                    evacuate(b)
                    b += 1
            for b in range(b, len(blocks)):
                evacuate(b)

        @block.vector
        def _(dve):
            def evacuate(b):
                blk = blocks[b]
                if blk.form == "+":
                    dve.wait_ge(product, last_of[b] + 1)
                    for j in range(blk.width // P):
                        scale = 1.0 if blk.gate is None else blk.gate[:, j:j + 1]
                        ins = dve.scalar_tensor_tensor(out=blk.out[:, j], in0=tiles(b)[:, j], scalar=scale,
                                                       in1=blk.out[:, j], op0=ALU.mult, op1=ALU.add)
                    ins.then_inc(evacuated, 1)
                elif blk.form == "p":
                    dve.wait_ge(hi_out, b + 1)
                    cut_lo(dve, blk.out[:, 1], tiles(b), blk.out[:, 0]).then_inc(evacuated, 1)

            for s in src:
                s.vector_squares(dve)
            b = 0
            for n in range(len(units)):
                if n == early:
                    for s in src:
                        s.vector(dve)
                dve.wait_ge(cut, n + 1)
                cut_lo(dve, view(lo[:, n % pairs], n)[0], view(raw[:, n % raws], n)[0],
                       view(hi[:, n % pairs], n)[0]).then_inc(ready, 1)
                while b < len(blocks) and last_of[b] + pairs <= n:
                    evacuate(b)
                    b += 1
            for b in range(b, len(blocks)):
                evacuate(b)


def project_residual(nc, K, name, w, x, gate=None):
    blocks = [Proj(w, n * 512, 512, K.xp[:], "+", K.x[:, 4 * n:4 * n + 4],
                   gate=None if gate is None else gate[:, 4 * n:4 * n + 4]) for n in range(2)]
    project(nc, name, blocks, lambda st: [Cut(st, "x", x, K.xp)])


def hgrn_gmlp(nc, K, dram):
    with ExitStack() as keep:
        def sb(name, shape, dt=F32):
            return keep.enter_context(nc.sbuf_tensor(name, shape, dt))

        q, f, og = sb("hg_q", [P, AH, T]), sb("hg_f", [P, AH, T]), sb("hg_og", [P, AH, T])
        v, u, gv = sb("hg_v", [P, TT, 512]), sb("hg_u", [P, 4, T]), sb("hg_gv", [P, TT, 512])
        mix = sb("hg_mix", [P, DC, T])
        K.rows = sb("hg_rows", [P, NROW])
        w, x = dram["l0_w_in"], K.xp[:]
        project(nc, "l0_in", [
            Proj(w, 0, 512, x, "f", q[:]),
            Proj(w, 512, 512, x, "f", f[:], ACT.Sigmoid),
            Proj(w, 1024, 512, x, "t", v[:], ACT.Silu),
            Proj(w, 1536, 512, x, "f", og[:], ACT.Silu),
            Proj(w, 2048, 512, x, "f", u[:], ACT.Gelu_apprx_tanh),
            Proj(w, 2560, 512, x, "t", gv[:], ACT.Gelu_apprx_tanh),
        ], lambda st: [Norm(st, K, "n", K.x, K.col("l0_norm_mix"), pair=K.xp)],
            [(K.rows[:], dram["rows"].partition_broadcast(P))])
        hgrn(nc, K, q, f, v, og, mix)
        gmlp(nc, K, dram, u, gv, mix)
        project_residual(nc, K, "l0_out", dram["l0_w_out"], mix)


def hgrn(nc, K, q, f, v, og, mix):
    with stage(nc, "hgrn") as st:
        v_step, masked, ready, product = (st.sem(x) for x in ("v_step", "masked", "ready", "product"))
        scored, turned, copied, state_add = (st.sem(x) for x in ("scored", "turned", "copied", "state_add"))
        state, added, out_sum, squared, rooted = (
            st.sem(x) for x in ("state", "added", "out_sum", "squared", "rooted"))
        decay, ready_p = st.sem("decay"), st.sem("ready_p")
        SPLIT = AH * NB // 2
        cum = st.sb("cum", [P, AH, T])
        inner = st.sb("inner", [P, AH, T])
        first = st.sb("first", [P, AH, T])
        qd = st.sb("qd", [P, AH, T])
        decays = st.sb("decays", [P, 2, AH, T])
        decayed = decays[:, (HC - 1) % 2]
        pair = st.sb("pair", [P, 2, AH, T])
        onehot = st.sb("onehot", [P, HC, HC])
        score = st.sb("score", [HC, AH, T])
        own = st.sb("own", [P, P // HC])
        own2 = st.sb("own2", [P, P // HC])
        diag = st.sb("diag", [P, AH * TT, P // HC, HC])
        kt = st.sb("kt", [P, AH * TT, P])
        states = st.sb("states", [P, NB, AH, P])
        startm = st.sb("startm", [P, HC])
        sq = st.sb("sq", [P, AH, T])
        root = st.sb("root", [P, AH, T])
        a_ps = st.ps("a", [P, AH, T])
        t_ps = st.ps("t", [P, AH, T])
        d_ps = st.ps("d", [P, 2, 512])
        o_ps = st.ps("o", [P, AH, T])
        at_ps = d_ps[:, 0, 0:AH * TT * HC].rearrange("p (n t) -> p n t", t=HC)
        block = st.ctx.enter_context(nc.Block())
        chunk = lambda a: a.rearrange("p h (b t) -> p (h b) t", t=HC)

        @block.gpsimd
        def _(pool):
            pool.memset(onehot[:], 0.0).then_inc(masked, 1)
            pool.memset(own[:], 1.0).then_inc(masked, 1)
            pool.memset(startm[:], 0.0).then_inc(masked, 1)
            pool.wait_ge(masked, 3)
            pool.affine_select(out=onehot[:], in_=onehot[:], compare_op=ALU.not_equal, fill=1.0, base=0,
                               pattern=[[1, HC], [-1, HC]], channel_multiplier=0).then_inc(masked, 1)
            pool.affine_select(out=own2[:], in_=own[:], compare_op=ALU.is_ge, fill=0.0, base=0,
                               pattern=[[-HC, P // HC]], channel_multiplier=1).then_inc(masked, 1)
            pool.affine_select(out=startm[:], in_=startm[:], compare_op=ALU.not_equal, fill=1.0, base=0,
                               pattern=[[1, HC]], channel_multiplier=0).then_inc(masked, 1)
            pool.wait_ge(masked, 6)
            pool.affine_select(out=own[:], in_=own2[:], compare_op=ALU.is_ge, fill=0.0, base=HC - 1,
                               pattern=[[HC, P // HC]], channel_multiplier=-1).then_inc(masked, 1)
            qc = chunk(q[:])
            for i in range(HC):
                pool.wait_ge(decay, i + 1)
                if i >= 2:
                    pool.wait_ge(product, i - 1)
                pool.tensor_tensor(chunk(pair[:, i % 2])[:, 0:SPLIT, 0:i + 1],
                                   chunk(decays[:, i % 2])[:, 0:SPLIT, 0:i + 1],
                                   qc[:, 0:SPLIT, i:i + 1].to_broadcast([P, SPLIT, i + 1]), ALU.mult)\
                    .then_inc(ready_p, 1)

        @block.vector
        def _(dve):
            chain = Chain(dve, v_step)
            for h in range(AH):
                ins = dve.tensor_scalar(f[:, h], f[:, h], K.nlb[:, h:h + 1], K.lb[:, h:h + 1], ALU.mult, ALU.add)
            chain(ins)
            for n in range(2):
                ins = dve.tensor_scalar(decays[:, n], f[:], -1.0, 1.0, ALU.mult, ALU.add)
            chain(ins)
            dve.wait_ge(masked, 7)
            starts = startm[:].unsqueeze(1).to_broadcast([P, AH * NB, HC])
            chain(dve.tensor_tensor(chunk(first[:]), chunk(f[:]), starts, ALU.mult))
            chain(dve.tensor_tensor(inner[:], f[:], first[:], ALU.subtract))
            chain(dve.tensor_tensor_scan(cum[:].rearrange("p h t -> p (h t)"),
                                         inner[:].rearrange("p h t -> p (h t)"),
                                         first[:].rearrange("p h t -> p (h t)"), 0.0, ALU.mult, ALU.add))
            dve.tensor_tensor(qd[:], q[:], cum[:], ALU.mult)
            qc, fc = chunk(q[:]), chunk(f[:])
            dve.engine_nop().then_inc(decay, 1)
            for i in range(HC):
                src, dst = chunk(decays[:, (i + 1) % 2]), chunk(decays[:, i % 2])
                if i:
                    if i >= 2:
                        dve.wait_ge(ready_p, i - 1)
                    dve.tensor_tensor(dst[:, :, 0:i], src[:, :, 0:i],
                                      fc[:, :, i:i + 1].to_broadcast([P, AH * NB, i]), ALU.mult).then_inc(decay, 1)
                    dve.wait_ge(decay, i + 1)
                if i >= 2:
                    dve.wait_ge(product, i - 1)
                dve.tensor_tensor(chunk(pair[:, i % 2])[:, SPLIT:, 0:i + 1], dst[:, SPLIT:, 0:i + 1],
                                  qc[:, SPLIT:, i:i + 1].to_broadcast([P, AH * NB - SPLIT, i + 1]), ALU.mult)\
                    .then_inc(ready, 1)
            chain(dve.memset(states[:, 0], 0.0))
            for b in range(NB - 1):
                dve.wait_ge(state_add, b + 1)
                for h in range(AH):
                    t = b * HC + HC - 1
                    ins = dve.scalar_tensor_tensor(out=states[:, b + 1, h], in0=states[:, b, h],
                                                   scalar=cum[:, h, t:t + 1],
                                                   in1=d_ps[:, b % 2, h * P:(h + 1) * P],
                                                   op0=ALU.mult, op1=ALU.add)
                ins.then_inc(state, 1)
                dve.wait_ge(state, b + 1)
            dve.wait_ge(turned, 2)
            dve.tensor_tensor(
                diag[:], at_ps.unsqueeze(2).to_broadcast([P, AH * TT, P // HC, HC]),
                own[:].unsqueeze(1).unsqueeze(3).to_broadcast([P, AH * TT, P // HC, HC]), ALU.mult)\
                .then_inc(added, 1)
            dve.wait_ge(rooted, 1)
            chain(dve.reciprocal(sq[:], root[:]))
            chain(dve.tensor_tensor(root[:], o_ps[:], sq[:], ALU.mult))
            for h in range(AH):
                g = K.col("l0_hgrn_out_norm")[:, h:h + 1]
                dve.scalar_tensor_tensor(out=mix[:, h], in0=root[:, h], scalar=g, in1=og[:, h],
                                         op0=ALU.mult, op1=ALU.mult)

        @block.tensor
        def _(pe):
            pe.wait_ge(masked, 7)
            for i in range(HC):
                pe.wait_ge(ready, i + 1)
                pe.wait_ge(ready_p, i + 1)
                for half in range(2):
                    hs = slice(half * 2, half * 2 + 2)
                    mm = pe.matmul(chunk(a_ps[0:HC, hs])[:, :, 0:i + 1], onehot[:, i, :],
                                   chunk(pair[:, i % 2, hs])[:, :, 0:i + 1],
                                   start=i == 0, stop=i == HC - 1, skip_group_check=True)
                mm.then_inc(product, 1)
            for h in range(AH):
                for t in range(TT):
                    mm = pe.transpose(t_ps[:, h, t * P:(t + 1) * P], decayed[:, h, t * P:(t + 1) * P], K.ident[:])
            mm.then_inc(turned, 1)
            pe.wait_ge(copied, 1)
            for b in range(NB - 1):
                t, at = b * HC // P, b * HC % P
                if b >= 2:
                    pe.wait_ge(state, b - 1)
                for h in range(AH):
                    mm = pe.matmul(d_ps[:, b % 2, h * P:(h + 1) * P], kt[at:at + HC, h * TT + t, :],
                                   v[at:at + HC, t, h * P:(h + 1) * P], start=True, stop=True)
                mm.then_inc(state_add, 1)
            pe.wait_ge(scored, 1)
            pe.wait_ge(state, NB - 1)
            for h in range(AH):
                for t in range(TT):
                    mm = pe.transpose(at_ps[:, h * TT + t, :], score[:, h, t * P:(t + 1) * P], K.ident[0:HC, 0:HC])
            mm.then_inc(turned, 1)
            pe.wait_ge(added, 1)
            for h in range(AH):
                for t in range(TT):
                    pe.matmul(o_ps[:, h, t * P:(t + 1) * P], v[:, t, h * P:(h + 1) * P],
                              diag[:, h * TT + t].rearrange("p j t -> p (j t)"),
                              start=h % 2 == 0 and t == 0, stop=False, skip_group_check=True)
            for h in range(AH):
                for b in range(1, NB):
                    mm = pe.matmul(o_ps[:, h, b * HC:(b + 1) * HC], states[:, b, h], qd[:, h, b * HC:(b + 1) * HC],
                                   start=False, stop=True, skip_group_check=True)
            mm.then_inc(out_sum, 1)
            pe.wait_ge(squared, 1)
            for half in range(2):
                hs = slice(half * 2, half * 2 + 2)
                mm = pe.matmul(a_ps[:, hs], K.ones[:], sq[:, hs], start=True, stop=True)
            mm.then_inc(out_sum, 1)

        @block.scalar
        def _(act):
            act.wait_ge(turned, 1)
            act.activation(kt[:].rearrange("p (h t) k -> p h (t k)", t=TT), t_ps[:], ACT.Copy).then_inc(copied, 1)
            act.wait_ge(product, HC)
            act.activation(score[:], a_ps[0:HC], ACT.Copy).then_inc(scored, 1)
            act.wait_ge(out_sum, 1)
            act.activation(sq[:], o_ps[:], ACT.Square).then_inc(squared, 1)
            act.wait_ge(out_sum, 2)
            act.activation(root[:], a_ps[:], ACT.Sqrt, bias=K.eps[:], scale=1.0 / P).then_inc(rooted, 1)


def gmlp(nc, K, dram, u, gv, mix):
    groups = 4
    with stage(nc, "gmlp") as st:
        w_in, kept, squared, rooted = (st.sem(x) for x in ("w_in", "kept", "squared", "rooted"))
        v_step, normed, mixed = (st.sem(x) for x in ("v_step", "normed", "mixed"))
        summed = st.sem("summed")
        w = st.sb("w", [P, groups, P])
        wc = st.sb("wc", [P, groups, P])
        sq = st.sb("sq", [P, TT * groups, P])
        ss = st.sb("ss", [P, TT * groups])
        root = st.sb("root", [P, TT * groups])
        rstd = st.sb("rstd", [P, TT * groups])
        acc = st.ps("acc", [P, groups, T])
        block = st.ctx.enter_context(nc.Block())
        g4 = gv[:].rearrange("p n (g d) -> p (n g) d", g=groups)

        @block.sync
        def _(sp):
            sp.dma_start(w[:], dram["w_s"]).then_inc(w_in, 16)

        @block.gpsimd
        def _(pool):
            pool.wait_ge(w_in, 16)
            pool.affine_select(out=wc[:], in_=w[:], compare_op=ALU.is_ge, fill=0.0, base=0,
                               pattern=[[0, groups], [1, P]], channel_multiplier=-1).then_inc(kept, 1)

        @block.scalar
        def _(act):
            act.activation(sq[:], g4, ACT.Square).then_inc(squared, 1)
            act.wait_ge(summed, 1)
            act.activation(root[:], ss[:], ACT.Sqrt, bias=K.eps[:], scale=1.0 / P).then_inc(rooted, 1)

        @block.vector
        def _(dve):
            chain = Chain(dve, v_step)
            dve.wait_ge(squared, 1)
            dve.tensor_reduce(ss[:], sq[:], AX_X, ALU.add).then_inc(summed, 1)
            dve.wait_ge(rooted, 1)
            chain(dve.reciprocal(rstd[:], root[:]))
            chain(dve.tensor_tensor(g4, g4, rstd[:].unsqueeze(2).to_broadcast([P, TT * groups, P]), ALU.mult))
            dve.tensor_tensor(gv[:], gv[:], K.row("l0_gmlp_v_norm").unsqueeze(1).to_broadcast([P, TT, 512]),
                              ALU.mult).then_inc(normed, 1)
            dve.wait_ge(mixed, 1)
            dve.tensor_tensor(mix[:, 4:8], acc[:], u[:], ALU.mult)

        @block.tensor
        def _(pe):
            pe.wait_ge(kept, 1)
            pe.wait_ge(normed, 1)
            bias = K.row("l0_gmlp_b_s")
            for g in range(groups):
                for n in range(TT):
                    out = acc[:, g, n * P:(n + 1) * P]
                    pe.matmul(out, gv[:, n, g * P:(g + 1) * P], wc[:, g, :], start=True, stop=False)
                    mm = pe.matmul(out, K.ones[0:1, :], bias[0:1, g * P:(g + 1) * P], start=False, stop=True)
            mm.then_inc(mixed, 1)


def peer(nc, K, dram, layer):
    name = f"peer{layer}"
    with nc.sbuf_tensor(f"{name}_q", [P, 2, HP, T], F32R) as q, \
            nc.sbuf_tensor(f"{name}_keys", [P, HP, NK], F32) as keys:
        project(nc, f"{name}_q", [
            Proj(dram[f"l{layer}_peer_w_query"], n * 512, 512, K.xp[:], "p", q[:, :, 4 * n:4 * n + 4])
            for n in range(4)],
            lambda st: [Norm(st, K, "n", K.x, K.col(f"l{layer}_norm_ffn"), pair=K.xp)],
            [(keys[:], dram[f"l{layer}_sub_keys"])])
        peer_scores(nc, K, name, keys, q, dram["scores"][layer])
    peer_experts(nc, K, name, layer, dram)


def peer_scores(nc, K, name, keys, q, out):
    with stage(nc, f"{name}_s") as st:
        product, copied = st.sem("product"), st.sem("copied")
        stored = [st.sem(f"stored{i}") for i in range(2 * TT)]
        keys_pair = st.sb("keys_pair", [P, 2, HP, NK], F32R)
        s = st.sb("s", [P, TT, HP, NK])
        acc = st.ps("acc", [P, 4, 4, NK])
        by_four = lambda a: a.rearrange("p (b j) n -> p b (j n)", j=4)
        cut = Cut(st, "keys", by_four(keys[:]), keys_pair[:].rearrange("p s (b j) n -> p s b (j n)", j=4))
        block = st.ctx.enter_context(nc.Block())

        @block.sync
        def _(sp):
            for i, done in enumerate(stored):
                t, part = i // 2, slice(HP // 2 * (i % 2), HP // 2 * (i % 2 + 1))
                sp.wait_ge(copied, 2 * (i + 1))
                sp.dma_start(out[:, t, part], s[:, t, part]).then_inc(done, 16)
            for done in stored:
                sp.wait_ge(done, 16)

        @block.tensor
        def _(pe):
            for n in range(TT * 4):
                t, b = divmod(n, 4)
                if t == 0:
                    pe.wait_ge(cut.done, b + 1)
                if n >= 4:
                    pe.wait_ge(copied, n - 3)
                for j in range(4):
                    hp, ts = 4 * b + j, slice(t * P, (t + 1) * P)
                    mm = multiply(pe, acc[:, n % 4, j], q[:, 0, hp, ts], q[:, 1, hp, ts], keys_pair[:, 0, hp],
                                  keys_pair[:, 1, hp], True, True)
                mm.then_inc(product, 1)

        @block.scalar
        def _(act):
            cut.scalar(act)
            for n in range(TT * 4):
                t, b = divmod(n, 4)
                act.wait_ge(product, n + 1)
                act.activation(s[:, t, 4 * b:4 * b + 4], acc[:, n % 4], ACT.Copy).then_inc(copied, 1)

        @block.vector
        def _(dve):
            cut.vector(dve)


def peer_experts(nc, K, name, layer, dram):
    down, up, w_mod = dram[f"l{layer}_down"], dram[f"l{layer}_up"], dram["w_mod"][layer]
    RAWS = 4
    BODIES = NK // RAWS
    NC = 2 - layer
    mod = K.mod[layer]
    A_FROM, A_PER = 11, 2
    A_MOD = A_PER * (BODIES - A_FROM)
    SILU_AT, EXP_AT = 7, 16
    C_MOD = MT - A_MOD
    CTX_MOD = 5 * DC
    ACT_TOKS = 3
    TAIL = 88
    with stage(nc, f"{name}_e") as st:
        down_in = [st.sem(f"down_in{i}") for i in range(RAWS)]
        up_in = [st.sem(f"up_in{i}") for i in range(RAWS)]
        mod_in = [st.sem(f"mod_in{i}") for i in range(A_PER)]
        s_in = [st.sem(f"s_in{t}") for t in range(TT)]
        cond_in, silued, mod_sum, mod_done = (st.sem(x) for x in ("cond_in", "silued", "mod_sum", "mod_done"))
        hi_down, lo_down, product, gelued = (st.sem(x) for x in ("hi_down", "lo_down", "product", "gelued"))
        v_step, shifted, exped, chosen, turned, copied = (
            st.sem(x) for x in ("v_step", "shifted", "exped", "chosen", "turned", "copied"))
        hot_a, hot_b, hot, routed, moved, weighted = (
            st.sem(x) for x in ("hot_a", "hot_b", "hot", "routed", "moved", "weighted"))
        hi_up, lo_up, hi_h, lo_h, out_sum = (st.sem(x) for x in ("hi_up", "lo_up", "hi_h", "lo_h", "out_sum"))
        raw = st.sb("raw", [P, RAWS, D])
        hi = st.sb("hi", [P, 2, D], F32R)
        lo = st.sb("lo", [P, 2, D], F32R)
        h = st.sb("h", [P, NK, T])
        wm = st.sb("wm", [P, A_PER, D])
        cond = st.sb("cond", [P, 2, D])
        sums = st.sb("sums", [P, A_PER, NC])
        choice = st.sb("choice", [P, 3, T])
        den = st.sb("den", [P, TT * PH])
        rden = st.sb("rden", [P, TT * PH])
        tail = h[:, TAIL:].rearrange("p a t -> p (a t)")
        at = 0

        def part(size):
            nonlocal at
            at += size
            return tail[:, at - size:at]

        s = part(TT * HP * NK).rearrange("p (t a n) -> p t a n", t=TT, a=HP)
        cand = part(PH * PK * PK).rearrange("p (h c) -> p h c", h=PH)
        match = part(PH * PK * PK).rearrange("p (h j a) -> p h j a", h=PH, a=PK)
        val = part(HP * PK).rearrange("p (a k) -> p a k", k=PK)
        idx = part(HP * PK).bitcast(U32).rearrange("p (a k) -> p a k", k=PK)
        idxf = part(HP * PK).rearrange("p (a k) -> p a k", k=PK)
        pos, half = (part(PH * PK).bitcast(U32).rearrange("p (h k) -> p h k", k=PK) for _ in range(2))
        halff = part(PH * PK).rearrange("p (h k) -> p h k", k=PK)
        pick = choice[:, 0:2].rearrange("p n (t e) -> p n t e", t=TT)
        top = choice[:, 2].rearrange("p (t h j) -> p t h j", t=TT, h=PH)
        hots = wm[:].rearrange("p n (k a e) -> p n k a e", k=2, a=TOKS)
        a_hot, b_hot = hots[:, 0], hots[:, 1]
        g_sb = cond[:, 1].rearrange("p (k a e) -> p k a e", k=2, a=TOKS)
        h_hi, h_lo = K.xp[:, 0, 0:2], K.xp[:, 1, 0:2]
        s_ps = st.ps("s", [P, 2, 512])
        waste = st.ps("waste", [P, D])
        o_ps = st.ps("o", [P, DC, T])
        g_ps = o_ps[:, 0:4, :].rearrange("p (b c) t -> p b (c t)", b=2)
        t_ps = o_ps[:, 4:7, :]
        block = st.ctx.enter_context(nc.Block())

        def top16(dve, chain, src, rows, values, indices):
            for first in (0, 8):
                for r in range(rows):
                    ins = dve.max(values[:, r, first:first + 8], src[:, r])
                chain(ins)
                for r in range(rows):
                    ins = dve.max_index(indices[:, r, first:first + 8], values[:, r, first:first + 8], src[:, r])
                chain(ins)
                if first == 0:
                    for r in range(rows):
                        ins = dve.match_replace(src[:, r], values[:, r, 0:8], src[:, r], LOWEST)
                    chain(ins)

        @block.sync
        def _(sp):
            def load_mod(n, k):
                sp.dma_start(wm[:, k], w_mod[n]).then_inc(mod_in[k], 16)

            def down_body(i):
                for k in range(RAWS):
                    sp.wait_ge(lo_down, i * RAWS + k - (RAWS - 1))
                    sp.dma_start(raw[:, k], down[i * RAWS + k]).then_inc(down_in[k], 16)

            for k in range(RAWS):
                sp.dma_start(raw[:, k], down[k]).then_inc(down_in[k], 16)
            for t in range(TT):
                sp.dma_start(s[:, t], dram["scores"][layer][:, t]).then_inc(s_in[t], 16)
            with sp.Fori(1, SILU_AT - 3) as i:
                down_body(i)
            sp.dma_start(cond[:, 0:NC], dram["cond"][0:NC].partition_broadcast(P)).then_inc(cond_in, 16)
            with sp.Fori(SILU_AT - 3, A_FROM) as i:
                down_body(i)
            for k in range(A_PER):
                load_mod(k, k)
            with sp.Fori(A_FROM, A_FROM + 1) as i:
                down_body(i)
            with sp.Fori(A_FROM + 1, BODIES) as i:
                down_body(i)
                for k in range(A_PER):
                    sp.wait_ge(mod_done, i - A_FROM)
                    load_mod((i - A_FROM) * A_PER + k, k)
            for k in range(RAWS):
                sp.wait_ge(lo_down, NK - (RAWS - 1) + k)
                sp.dma_start(raw[:, k], up[:, k]).then_inc(up_in[k], 16)
            def up_body(i, with_mod):
                for k in range(RAWS):
                    sp.wait_ge(lo_up, i * RAWS + k - (RAWS - 1))
                    sp.dma_start(raw[:, k], up[:, bass.ds(i * RAWS + k, 1)].rearrange("p a d -> p (a d)"))\
                        .then_inc(up_in[k], 16)
                    if k == 0 and with_mod:
                        sp.wait_ge(mod_done, i + (A_MOD // A_PER - 1))
                        load_mod(i + (A_MOD - 1), 0)

            with sp.Fori(1, C_MOD + 1) as i:
                up_body(i, True)
            with sp.Fori(C_MOD + 1, BODIES) as i:
                up_body(i, False)

        @block.tensor
        def _(pe):
            def score(i, k, first=False):
                n = i * RAWS + k
                if not first:
                    pe.wait_ge(gelued, n - 1)
                pe.wait_ge(hi_down, n + 1)
                out = s_ps[:, k % 2, 0:T]
                for c in range(DC):
                    w = hi[:, k % 2, c * P:(c + 1) * P]
                    pe.matmul(out, w, K.xp[:, 0, c], start=c == 0, stop=False)
                    pe.matmul(out, w, K.xp[:, 1, c], start=False, stop=False)
                pe.wait_ge(lo_down, n + 1)
                for c in range(DC):
                    mm = pe.matmul(out, lo[:, k % 2, c * P:(c + 1) * P], K.xp[:, 0, c], start=False, stop=c == DC - 1)
                mm.then_inc(product, 1)

            for k in range(RAWS):
                score(0, k, k < 2)
            with pe.Fori(1, BODIES) as i:
                for k in range(RAWS):
                    score(i, k)
            pe.wait_ge(chosen, 1)
            for n in range(2):
                for t in range(TT):
                    pe.transpose(t_ps[:, n, t * P:(t + 1) * P], pick[:, n, t], K.ident[:])
            for t in range(TT):
                mm = pe.transpose(t_ps[:, 2, t * P:(t + 1) * P],
                                  top[:, t].rearrange("p h j -> p (h j)"), K.ident[:])
            mm.then_inc(turned, 1)

            def route(i, k):
                pe.wait_ge(hot, i * 2 + k + 1)
                pe.wait_ge(hot_b, i * 2 + k + 1)
                for a in range(TOKS):
                    mm = pe.matmul(g_ps[:, k, a * P:(a + 1) * P], a_hot[:, k, a], b_hot[:, k, a],
                                   start=True, stop=True)
                mm.then_inc(routed, 1)

            for k in range(2):
                route(0, k)
            with pe.Fori(1, T // (2 * TOKS)) as i:
                for k in range(2):
                    pe.wait_ge(moved, i * 2 + k - 1)
                    route(i, k)

            def accumulate(i, k, first=False):
                n = i * RAWS + k
                pe.wait_ge(lo_h, n + 1)
                pe.wait_ge(hi_up, n + 1)
                for c in range(DC):
                    w = hi[:, k % 2, c * P:(c + 1) * P]
                    pe.matmul(o_ps[:, c], w, h_hi[:, k % 2], start=first and c % 2 == 0, stop=False,
                              skip_group_check=True)
                    pe.matmul(o_ps[:, c], w, h_lo[:, k % 2], start=False, stop=False, skip_group_check=True)
                pe.wait_ge(lo_up, n + 1)
                for c in range(DC):
                    mm = pe.matmul(o_ps[:, c], lo[:, k % 2, c * P:(c + 1) * P], h_hi[:, k % 2], start=False,
                                   stop=False, skip_group_check=True)
                mm.then_inc(out_sum, 1)

            pe.wait_ge(weighted, T // TOKS)
            for k in range(RAWS):
                accumulate(0, k, k == 0)
            with pe.Fori(1, BODIES) as i:
                for k in range(RAWS):
                    accumulate(i, k)

        @block.scalar
        def _(act):
            def cut_down(i, k, first=False):
                act.wait_ge(down_in[k], i * 16 + 16)
                if not first:
                    act.wait_ge(product, i * RAWS + k - 1)
                cut_hi(act, hi[:, k % 2], raw[:, k]).then_inc(hi_down, 1)

            def gelu(n, k):
                act.activation(h[:, bass.ds(n, 1), :], s_ps[:, k % 2:k % 2 + 1, 0:T], ACT.Gelu_apprx_tanh)\
                    .then_inc(gelued, 1)

            def body(i):
                for k in range(RAWS):
                    cut_down(i, k)
                    gelu(i * RAWS + k - 2, k)

            for k in range(RAWS):
                cut_down(0, k, k < 2)
                if k >= 2:
                    gelu(k - 2, k)
            with act.Fori(1, SILU_AT) as i:
                body(i)
            act.wait_ge(cond_in, 16)
            act.activation(cond[:, 0:NC], cond[:, 0:NC], ACT.Silu).then_inc(silued, 1)
            with act.Fori(SILU_AT, EXP_AT) as i:
                body(i)
            act.wait_ge(shifted, 1)
            act.activation(choice[:, 2], choice[:, 2], ACT.Exp).then_inc(exped, 1)
            with act.Fori(EXP_AT, TAIL // RAWS) as i:
                body(i)
            act.wait_ge(chosen, 1)
            with act.Fori(TAIL // RAWS, BODIES) as i:
                body(i)
            for n in (NK - 2, NK - 1):
                act.wait_ge(product, n + 1)
                gelu(n, n)
            act.wait_ge(turned, 1)
            act.activation(choice[:], t_ps, ACT.Copy).then_inc(copied, 1)

            def weigh_hot(i, k):
                act.wait_ge(hot_a, i * 2 + k + 1)
                for a in range(ACT_TOKS):
                    ins = act.activation(a_hot[:, k, a], a_hot[:, k, a], ACT.Copy,
                                         scale=choice[:, 2, bass.ds((i * 2 + k) * TOKS + a, 1)])
                ins.then_inc(hot, 1)

            def move(i, k, first=False):
                act.wait_ge(routed, i * 2 + k + 1)
                if not first:
                    act.wait_ge(weighted, i * 2 + k - 1)
                act.activation(g_sb[:, k].rearrange("p a e -> p (a e)"), g_ps[:, k], ACT.Copy).then_inc(moved, 1)

            for k in range(2):
                weigh_hot(0, k)
            for k in range(2):
                move(0, k, True)
                weigh_hot(1, k)
            with act.Fori(1, T // (2 * TOKS) - 1) as i:
                for k in range(2):
                    move(i, k)
                    weigh_hot(i + 1, k)
            for k in range(2):
                move(T // (2 * TOKS) - 1, k)

            def cut_up(i, k, first=False):
                n = i * RAWS + k
                if not first:
                    act.wait_ge(out_sum, n - 1)
                cut_hi(act, h_hi[:, k % 2:k % 2 + 1], h[:, bass.ds(n, 1), :]).then_inc(hi_h, 1)
                act.wait_ge(up_in[k], i * 16 + 16)
                cut_hi(act, hi[:, k % 2], raw[:, k]).then_inc(hi_up, 1)

            act.wait_ge(weighted, T // TOKS)
            for k in range(RAWS):
                cut_up(0, k, k < 2)
            with act.Fori(1, BODIES) as i:
                for k in range(RAWS):
                    cut_up(i, k)

        @block.gpsimd
        def _(pool):
            def low_down(i, k):
                pool.wait_ge(hi_down, i * RAWS + k + 1)
                cut_lo(pool, lo[:, k % 2], raw[:, k], hi[:, k % 2]).then_inc(lo_down, 1)

            with pool.Fori(0, BODIES) as i:
                for k in range(RAWS):
                    low_down(i, k)
            pool.wait_ge(gelued, NK)

            def weigh(i, k):
                pool.wait_ge(moved, i * 2 + k + 1)
                hh = h[:, :, bass.ds((i * 2 + k) * TOKS, TOKS)]
                pool.tensor_tensor(hh, g_sb[:, k].rearrange("p a e -> p e a"), hh, ALU.mult).then_inc(weighted, 1)

            with pool.Fori(0, T // (2 * TOKS)) as i:
                for k in range(2):
                    weigh(i, k)
            with pool.Fori(0, BODIES) as i:
                for k in range(RAWS):
                    n = i * RAWS + k
                    pool.wait_ge(hi_h, n + 1)
                    cut_lo(pool, h_lo[:, k % 2:k % 2 + 1], h[:, bass.ds(n, 1), :], h_hi[:, k % 2:k % 2 + 1])\
                        .then_inc(lo_h, 1)

        @block.vector
        def _(dve):
            chain = Chain(dve, v_step)
            iota16 = K.iota[:, 0:PK].unsqueeze(1).unsqueeze(1).to_broadcast([P, PH, PK, PK])
            for t in range(TT):
                dve.wait_ge(s_in[t], 16)
                top16(dve, chain, s[:, t], HP, val, idx)
                chain(dve.tensor_copy(idxf, idx))
                v2 = val.rearrange("p (h s) k -> p h s k", s=2)
                chain(dve.tensor_tensor(
                    cand.rearrange("p h (a b) -> p h a b", a=PK),
                    v2[:, :, 0].unsqueeze(3).to_broadcast([P, PH, PK, PK]),
                    v2[:, :, 1].unsqueeze(2).to_broadcast([P, PH, PK, PK]), ALU.add))
                top16(dve, chain, cand, PH, top[:, t], pos)
                for n in range(2):
                    if n == 0:
                        chain(dve.tensor_scalar(half, pos, 4, None, ALU.logical_shift_right))
                    else:
                        chain(dve.tensor_scalar(half, pos, PK - 1, None, ALU.bitwise_and))
                    chain(dve.tensor_copy(halff, half))
                    chain(dve.tensor_tensor(match, halff.unsqueeze(3).to_broadcast([P, PH, PK, PK]), iota16,
                                            ALU.is_equal))
                    i2 = idxf.rearrange("p (h s) k -> p h s k", s=2)[:, :, n]
                    chain(dve.tensor_tensor(match, match, i2.unsqueeze(2).to_broadcast([P, PH, PK, PK]), ALU.mult))
                    chain(dve.tensor_reduce(pick[:, n, t].rearrange("p (h j) -> p h j", h=PH), match, AX_X, ALU.add))
            tops = choice[:, 2].rearrange("p (a j) -> p a j", j=PK)
            chain(dve.tensor_copy(den[:].unsqueeze(2), tops[:, :, 0:1]))
            dve.tensor_tensor(tops, tops, den[:].unsqueeze(2).to_broadcast([P, TT * PH, PK]), ALU.subtract)\
                .then_inc(shifted, 1)

            def mod_columns(tile, slots, loads, done, conditions):
                for k in range(slots):
                    dve.wait_ge(mod_in[k], loads)
                    for n in range(conditions):
                        dve.tensor_tensor_reduce(waste[:], wm[:, k], cond[:, n], 1.0, 0.0, ALU.mult,
                                                 ALU.add, sums[:, k, n:n + 1]).then_inc(mod_sum, 1)
                        dve.wait_ge(mod_sum, done + (k * conditions + n + 1))
                dve.tensor_copy(mod[:, bass.ds(tile, slots), 0:conditions], sums[:, 0:slots, 0:conditions])\
                    .then_inc(mod_done, 1)

            BOTH = CTX_MOD // A_PER

            def mod_batch(j, conditions):
                dve.wait_ge(mod_done, j)
                done = j * (A_PER * conditions) + (0 if conditions == NC else BOTH * A_PER * (NC - 1))
                mod_columns(j * A_PER, A_PER, j * 16 + 16, done, conditions)

            dve.wait_ge(silued, 1)
            mod_columns(0, A_PER, 16, 0, NC)
            with dve.Fori(1, EXP_AT - A_FROM) as j:
                mod_batch(j, NC)
            dve.wait_ge(exped, 1)
            chain(dve.tensor_reduce(den[:], tops, AX_X, ALU.add))
            chain(dve.reciprocal(rden[:], den[:]))
            dve.tensor_tensor(tops, tops, rden[:].unsqueeze(2).to_broadcast([P, TT * PH, PK]), ALU.mult)\
                .then_inc(chosen, 1)
            with dve.Fori(EXP_AT - A_FROM, BOTH) as j:
                mod_batch(j, NC)
            with dve.Fori(BOTH, A_MOD // A_PER) as j:
                mod_batch(j, 1)
            dve.wait_ge(copied, 1)

            def make_hots(i, k):
                t = (i * 2 + k) * TOKS
                for n, toks in ((0, ACT_TOKS), (1, TOKS)):
                    ins = dve.tensor_tensor(hots[:, n, k, 0:toks], K.iota[:].unsqueeze(1).to_broadcast([P, toks, P]),
                                            choice[:, n, bass.ds(t, toks)].unsqueeze(2).to_broadcast([P, toks, P]),
                                            ALU.is_equal)
                    if n == 0:
                        ins.then_inc(hot_a, 1)
                for a in range(ACT_TOKS, TOKS):
                    ins = dve.tensor_scalar(a_hot[:, k, a], K.iota[:], choice[:, 0, bass.ds(t + a, 1)],
                                            choice[:, 2, bass.ds(t + a, 1)], ALU.is_equal, ALU.mult)
                ins.then_inc(hot_b, 1)

            for k in range(2):
                make_hots(0, k)
            with dve.Fori(1, T // (2 * TOKS)) as i:
                for k in range(2):
                    dve.wait_ge(routed, i * 2 + k - 1)
                    make_hots(i, k)

            def low_up(i, k):
                dve.wait_ge(hi_up, i * RAWS + k + 1)
                cut_lo(dve, lo[:, k % 2], raw[:, k], hi[:, k % 2]).then_inc(lo_up, 1)

            for k in range(RAWS):
                low_up(0, k)
            with dve.Fori(1, C_MOD + 1) as i:
                for k in range(RAWS):
                    low_up(i, k)
                    if k == 1:
                        dve.wait_ge(mod_done, i + (A_MOD // A_PER - 1))
                        mod_columns(i + (A_MOD - 1), 1, i * 16 + A_MOD // A_PER * 16,
                                    i + (A_MOD + CTX_MOD * (NC - 1) - 1), 1)
            with dve.Fori(C_MOD + 1, BODIES) as i:
                for k in range(RAWS):
                    low_up(i, k)
            dve.wait_ge(out_sum, NK)
            for c in range(0, DC, 2):
                dve.tensor_tensor(K.x[:, c:c + 2], o_ps[:, c:c + 2], K.x[:, c:c + 2], ALU.add)


class Head:

    def __init__(self, qk, v, out, sink=None):
        self.qk, self.v, self.out, self.sink = qk, v, out, sink


def attend(nc, K, name, heads, keys, chunks_of, mask, scale):
    units = [(h, t) for h in heads for t in range(TT)]
    with stage(nc, name) as st:
        scored, masked, shifted, exped, normed = (
            st.sem(x) for x in ("scored", "masked", "shifted", "exped", "normed"))
        turned, copied, product, stored, v_step = (
            st.sem(x) for x in ("turned", "copied", "product", "stored", "v_step"))
        nch = keys // P
        m = st.sb("m", [P, 2, keys])
        p = st.sb("p", [P, 2, keys])
        pn = st.sb("pn", [P, 2, keys])
        pt = st.sb("pt", [P, 2, nch, P])
        small = st.sb("small", [P, 2, 6])
        s_ps = st.ps("s", [P, 2, 512])
        t_ps = st.ps("t", [P, 2, 512])
        o_ps = st.ps("o", [P, 2, 512])
        block = st.ctx.enter_context(nc.Block())

        def width(h):
            return h.out.shape[0]

        @block.tensor
        def _(pe):
            def score(n):
                h, t = units[n]
                if n >= 2:
                    pe.wait_ge(masked, n - 1)
                for i, (q, k) in enumerate(h.qk):
                    mm = pe.matmul(s_ps[:, n % 2, 0:keys], q[:, t * P:(t + 1) * P], k,
                                   start=i == 0, stop=i == len(h.qk) - 1)
                mm.then_inc(scored, 1)

            def turn(n):
                t = units[n][1]
                pe.wait_ge(normed, n + 1)
                if n >= 2:
                    pe.wait_ge(copied, n - 1)
                for c in chunks_of[t]:
                    mm = pe.transpose(t_ps[:, n % 2, c * P:(c + 1) * P], pn[:, n % 2, c * P:(c + 1) * P], K.ident[:])
                mm.then_inc(turned, 1)

            def combine(n):
                h, t = units[n]
                pe.wait_ge(copied, n + 1)
                if n >= 2:
                    pe.wait_ge(stored, n - 1)
                at = h.out.base_partition() if callable(h.out.base_partition) else h.out.base_partition
                cs = chunks_of[t]
                for c in cs:
                    mm = pe.matmul(o_ps[at:at + width(h), n % 2, 0:P], h.v(c), pt[:, n % 2, c],
                                   start=c == cs[0], stop=c == cs[-1])
                mm.then_inc(product, 1)

            score(0)
            for n in range(len(units) + 2):
                if n + 1 < len(units):
                    score(n + 1)
                if 1 <= n <= len(units):
                    turn(n - 1)
                if n >= 2:
                    combine(n - 2)

        @block.vector
        def _(dve):
            chain = Chain(dve, v_step)

            def maximum(n):
                h, t = units[n]
                z = small[:, n % 2]
                dve.wait_ge(scored, n + 1)
                if n >= 2:
                    dve.wait_ge(exped, n - 1)
                dve.scalar_tensor_tensor(out=m[:, n % 2], in0=s_ps[:, n % 2, 0:keys], scalar=scale,
                                         in1=mask[:, t], op0=ALU.mult, op1=ALU.add).then_inc(masked, 1)
                dve.wait_ge(masked, n + 1)
                chain(dve.tensor_reduce(z[:, 0:1], m[:, n % 2], AX_X, ALU.max))
                bound = z[:, 0:1] if h.sink is None else h.sink
                dve.tensor_scalar(z[:, 1:2], z[:, 0:1], bound, -1.0, ALU.max, ALU.mult).then_inc(shifted, 1)

            def norm(n):
                h, t = units[n]
                z = small[:, n % 2]
                dve.wait_ge(exped, n + 1)
                total = z[:, 2:3]
                if h.sink is not None:
                    chain(dve.tensor_tensor(z[:, 4:5], z[:, 2:3], z[:, 3:4], ALU.add))
                    total = z[:, 4:5]
                chain(dve.reciprocal(z[:, 5:6], total))
                if n >= 2:
                    dve.wait_ge(turned, n - 1)
                dve.tensor_scalar(pn[:, n % 2], p[:, n % 2], z[:, 5:6], None, ALU.mult).then_inc(normed, 1)

            for n in range(len(units) + 1):
                if n < len(units):
                    maximum(n)
                if n >= 1:
                    norm(n - 1)

        @block.scalar
        def _(act):
            def exps(n):
                h, t = units[n]
                z = small[:, n % 2]
                act.wait_ge(shifted, n + 1)
                if n >= 2:
                    act.wait_ge(normed, n - 1)
                ins = act.activation(p[:, n % 2], m[:, n % 2], ACT.Exp, bias=z[:, 1:2], accum_out=z[:, 2:3])
                if h.sink is not None:
                    ins = act.activation(z[:, 3:4], h.sink, ACT.Exp, bias=z[:, 1:2])
                ins.then_inc(exped, 1)

            def copies(n):
                h, t = units[n]
                cs = chunks_of[t]
                act.wait_ge(turned, n + 1)
                if n >= 2:
                    act.wait_ge(product, n - 1)
                act.activation(pt[:, n % 2, cs[0]:cs[-1] + 1].rearrange("p c q -> p (c q)"),
                               t_ps[:, n % 2, cs[0] * P:(cs[-1] + 1) * P], ACT.Copy).then_inc(copied, 1)

            def store(n):
                h, t = units[n]
                at = h.out.base_partition() if callable(h.out.base_partition) else h.out.base_partition
                act.wait_ge(product, n + 1)
                act.activation(h.out[:, t * P:(t + 1) * P], o_ps[at:at + width(h), n % 2, 0:P], ACT.Copy)\
                    .then_inc(stored, 1)

            for n in range(len(units) + 2):
                if n < len(units):
                    exps(n)
                if 1 <= n <= len(units):
                    copies(n - 1)
                if n >= 2:
                    store(n - 2)


class Tok:

    def __init__(self, x, gain=None, rope=(), half=0):
        self.x, self.gain, self.rope, self.half = x, gain, rope, half


def token_norm_rope(nc, K, name, items, turns):
    with stage(nc, name) as st:
        squared, summed, rooted, v_step = (st.sem(x) for x in ("squared", "summed", "rooted", "v_step"))
        done, turned, copied = (st.sem(x) for x in ("done", "turned", "copied"))
        normed = [x for x in items if x.gain is not None]
        most = max([x.x.shape[2] * x.x.shape[3] for x in normed], default=1)
        widest = max([x.x.shape[2] * x.half for x in items], default=1) or 1
        sq = st.sb("sq", [P, 2, TT * most])
        ss = st.sb("ss", [P, 2, 32])
        root = st.sb("root", [P, 2, 32])
        rstd = st.sb("rstd", [P, 32])
        tmp = [st.sb(f"tmp{i}", [P, TT * widest]) for i in range(4)]
        t_ps = st.ps("t", [P, 4, 512])
        block = st.ctx.enter_context(nc.Block())

        @block.scalar
        def _(act):
            def square(n):
                heads, width = normed[n].x.shape[2], normed[n].x.shape[3]
                v = sq[:, n % 2, 0:TT * heads * width].rearrange("p (t h d) -> p t h d", t=TT, h=heads)
                if n >= 2:
                    act.wait_ge(summed, n - 1)
                act.activation(v, normed[n].x, ACT.Square).then_inc(squared, 1)

            for n in range(min(2, len(normed))):
                square(n)
            for n, it in enumerate(normed):
                heads, width = it.x.shape[2], it.x.shape[3]
                act.wait_ge(summed, n + 1)
                act.activation(root[:, n % 2, 0:TT * heads], ss[:, n % 2, 0:TT * heads], ACT.Sqrt, bias=K.eps[:],
                               scale=1.0 / width).then_inc(rooted, 1)
                if n + 2 < len(normed):
                    square(n + 2)
            for n, (item, src, dst) in enumerate(turns):
                act.wait_ge(turned, n + 1)
                act.activation(dst, t_ps[0:dst.shape[0], n % 4, 0:T], ACT.Copy).then_inc(copied, 1)

        @block.vector
        def _(dve):
            chain = Chain(dve, v_step)

            def total(n):
                heads, width = normed[n].x.shape[2], normed[n].x.shape[3]
                v = sq[:, n % 2, 0:TT * heads * width].rearrange("p (n d) -> p n d", d=width)
                dve.wait_ge(squared, n + 1)
                dve.tensor_reduce(ss[:, n % 2, 0:TT * heads], v, AX_X, ALU.add).then_inc(summed, 1)

            if normed:
                total(0)
            for n, it in enumerate(items):
                heads, width = it.x.shape[2], it.x.shape[3]
                if it.gain is not None:
                    if n + 1 < len(normed):
                        total(n + 1)
                    dve.wait_ge(rooted, n + 1)
                    chain(dve.reciprocal(rstd[:, 0:TT * heads], root[:, n % 2, 0:TT * heads]))
                    r = rstd[:, 0:TT * heads].rearrange("p (t h) -> p t h", t=TT)
                    for t in range(TT):
                        ins = dve.tensor_tensor(it.x[:, t], it.x[:, t],
                                                r[:, t].unsqueeze(2).to_broadcast([P, heads, width]), ALU.mult)
                    chain(ins)
                    for t in range(TT):
                        ins = dve.tensor_tensor(it.x[:, t], it.x[:, t],
                                                it.gain.unsqueeze(1).to_broadcast([P, heads, width]), ALU.mult)
                    chain(ins)
                half = it.half
                for at, cos, sin in it.rope:
                    x1, x2 = it.x[:, :, :, at:at + half], it.x[:, :, :, at + half:at + 2 * half]
                    a, b, c, d = (x[:, 0:TT * heads * half].rearrange("p (t h e) -> p t h e", t=TT, h=heads)
                                  for x in tmp)
                    for t in range(TT):
                        cs = cos[:, t].unsqueeze(1).to_broadcast([P, heads, half])
                        sn = sin[:, t].unsqueeze(1).to_broadcast([P, heads, half])
                        dve.tensor_tensor(a[:, t], x1[:, t], cs, ALU.mult)
                        dve.tensor_tensor(b[:, t], x2[:, t], sn, ALU.mult)
                        dve.tensor_tensor(c[:, t], x2[:, t], cs, ALU.mult)
                        ins = dve.tensor_tensor(d[:, t], x1[:, t], sn, ALU.mult)
                    chain(ins)
                    for t in range(TT):
                        dve.tensor_tensor(x1[:, t], a[:, t], b[:, t], ALU.subtract)
                        ins = dve.tensor_tensor(x2[:, t], c[:, t], d[:, t], ALU.add)
                    chain(ins)
                dve.engine_nop().then_inc(done, 1)

        @block.tensor
        def _(pe):
            for n, (item, src, dst) in enumerate(turns):
                pe.wait_ge(done, item + 1)
                if n >= 4:
                    pe.wait_ge(copied, n - 3)
                for t in range(TT):
                    mm = pe.transpose(t_ps[0:dst.shape[0], n % 4, t * P:(t + 1) * P], src[:, t], K.ident[:])
                mm.then_inc(turned, 1)


def angles(nc, K, dram, cos, sin):
    with stage(nc, "angles") as st:
        pos_in, v_step, reduced, sined = (st.sem(x) for x in ("pos_in", "v_step", "reduced", "sined"))
        pos = st.sb("pos", [P, TT], I32)
        posf = st.sb("posf", [P, TT])
        ang = st.sb("ang", [P, TT, 32])
        turn = st.sb("turn", [P, TT, 32])
        whole = st.sb("whole", [P, TT, 32], I32)
        wholef = st.sb("wholef", [P, TT, 32])
        tmp = st.sb("tmp", [P, TT, 32])
        rest = st.sb("rest", [P, 2, TT, 32])
        block = st.ctx.enter_context(nc.Block())
        c1 = 6.28125
        c2 = float(np.float32(np.floor((2 * np.pi - c1) * 2.0 ** 19) / 2.0 ** 19))
        c3 = float(np.float32(2 * np.pi - c1 - c2))

        @block.sync
        def _(sp):
            sp.dma_start(pos[:], dram["positions"]).then_inc(pos_in, 16)

        @block.vector
        def _(dve):
            chain = Chain(dve, v_step)
            dve.wait_ge(pos_in, 16)
            chain(dve.tensor_copy(posf[:], pos[:]))
            for t in range(TT):
                ins = dve.tensor_scalar(ang[:, t], K.row("inv_freq"), posf[:, t:t + 1], None, ALU.mult)
            chain(ins)
            for n, ahead in ((0, float(np.pi / 2)), (1, 0.0)):
                chain(dve.tensor_scalar(turn[:], ang[:], ahead, float(1 / (2 * np.pi)), ALU.add, ALU.mult))
                chain(dve.tensor_copy(whole[:], turn[:]))
                chain(dve.tensor_copy(wholef[:], whole[:]))
                chain(dve.scalar_tensor_tensor(out=tmp[:], in0=wholef[:], scalar=-c1, in1=ang[:],
                                               op0=ALU.mult, op1=ALU.add))
                chain(dve.scalar_tensor_tensor(out=turn[:], in0=wholef[:], scalar=-c2, in1=tmp[:],
                                               op0=ALU.mult, op1=ALU.add))
                chain(dve.scalar_tensor_tensor(out=tmp[:], in0=wholef[:], scalar=-c3, in1=turn[:],
                                               op0=ALU.mult, op1=ALU.add))
                chain(dve.tensor_scalar(turn[:], tmp[:], ahead, float(np.float32(3.1415925)), ALU.add, ALU.min))
                chain(dve.tensor_scalar(rest[:, n], turn[:], -float(np.float32(3.1415925)), None, ALU.max))
            dve.engine_nop().then_inc(reduced, 1)

        @block.scalar
        def _(act):
            act.wait_ge(reduced, 1)
            act.activation(cos, rest[:, 0], ACT.Sin)
            act.activation(sin, rest[:, 1], ACT.Sin).then_inc(sined, 1)


def mla_moba(nc, K, dram):
    with ExitStack() as keep:
        def sb(name, shape, dt=F32):
            return keep.enter_context(nc.sbuf_tensor(f"mla_{name}", shape, dt))

        cq, ckv, kpe = sb("cq", [P, 2, T]), sb("ckv", [P, 1, T]), sb("kpe", [P, TT, ROPE])
        qd, kd, vd = sb("qd", [P, TT, 512]), sb("kd", [P, TT, 512]), sb("vd", [P, TT, 512])
        cqn, ckvn = sb("cqn", [P, 2, 2, T], F32R), sb("ckvn", [P, 2, 1, T], F32R)
        qc, kc = sb("qc", [P, TT, CH, QK]), sb("kc", [P, TT, CH, QK])
        kv = sb("kv", [P, TT, CH, 2 * P])
        cos, sin = sb("cos", [P, TT, 32]), sb("sin", [P, TT, 32])
        qt, kt = sb("qt", [P, 8, T]), sb("kt", [P, 8, T])
        qpt, kpt = sb("qpt", [ROPE, CH, T]), sb("kpt", [ROPE, CH, T])
        mix = sb("mix", [P, DC, T])
        causal = sb("causal", [P, TT, T])
        K.rows = sb("rows", [P, NROW])
        w, x = dram["l1_w_in"], K.xp[:]
        project(nc, "l1_in", [
            Proj(w, 0, 256, x, "f", cq[:]),
            Proj(w, 256, 128, x, "f", ckv[:]),
            Proj(w, 384, ROPE, x, "t", kpe[:]),
            Proj(w, 448, 512, x, "t", qd[:]),
            Proj(w, 960, 512, x, "t", kd[:]),
            Proj(w, 1472, 512, x, "t", vd[:]),
        ], lambda st: [Norm(st, K, "n", K.x, K.col("l1_norm_mix"), pair=K.xp)],
            [(K.rows[:], dram["rows"].partition_broadcast(P))])
        angles(nc, K, dram, cos[:], sin[:])
        qcf, kvf = (a[:].rearrange("p t h d -> p t (h d)") for a in (qc, kv))
        project(nc, "uq", [
            Proj(dram["l1_mla_w_uq"], 0, 384, cqn[:], "t", qcf[:, :, 0:384]),
            Proj(dram["l1_mla_w_uq"], 384, 384, cqn[:], "t", qcf[:, :, 384:768]),
            Proj(dram["l1_mla_w_ukv"], 0, 512, ckvn[:], "t", kvf[:, :, 0:512], src=1),
            Proj(dram["l1_mla_w_ukv"], 512, 512, ckvn[:], "t", kvf[:, :, 512:1024], src=1),
        ], lambda st: [Norm(st, K, "q", cq, K.col("l1_mla_cq_norm"), width=256, pair=cqn),
                       Norm(st, K, "kv", ckv, K.col("l1_mla_ckv_norm"), width=128, pair=ckvn)])
        with stage(nc, "mla_keys") as st:
            cleared, half = st.sem("cleared"), st.sem("half")
            block = st.ctx.enter_context(nc.Block())

            @block.vector
            def _(dve):
                for t in range(TT):
                    dve.tensor_copy(kc[:, t, :, 0:NOPE], kv[:, t, :, 0:NOPE])
                    dve.tensor_copy(kc[:, t, :, NOPE:QK], kpe[:, t].unsqueeze(1).to_broadcast([P, CH, ROPE]))

            @block.gpsimd
            def _(pool):
                pool.memset(causal[:], 0.0).then_inc(cleared, 1)
                pool.wait_ge(cleared, 1)
                pool.affine_select(out=causal[:], in_=causal[:], compare_op=ALU.is_ge, fill=NEG, base=0,
                                   pattern=[[P, TT], [-1, T]], channel_multiplier=1)

        qd4, kd4, vd4 = (a[:].rearrange("p t (h d) -> p t h d", h=4) for a in (qd, kd, vd))
        rope = ((NOPE, cos, sin),)
        token_norm_rope(nc, K, "mla_qk", [
            Tok(qc[:], K.row("l1_mla_q_norm"), rope, ROPE // 2), Tok(kc[:], K.row("l1_mla_k_norm"), rope, ROPE // 2),
            Tok(qd4, K.row("l1_moba_q_norm")), Tok(kd4, K.row("l1_moba_k_norm")),
        ], [(n, src[:, :, h, at:at + width], dst[:, h])
            for n, src, at, width, dst in ((0, qc, 0, NOPE, qt), (0, qc, NOPE, ROPE, qpt), (1, kc, 0, NOPE, kt),
                                           (1, kc, NOPE, ROPE, kpt), (2, qd4, 0, P, qt[:, 4:8]), (3, kd4, 0, P, kt[:, 4:8]))
            for h in range(4)])

        def value(a, h, lo):
            return lambda c: a[:, c, h, lo:lo + P]

        seen = [[0], [0, 1]]
        attend(nc, K, "mla", [Head([(qt[:, h], kt[:, h]), (qpt[:, h], kpt[:, h])], value(kv, h, NOPE), mix[:, h])
                              for h in range(4)], T, seen, causal, float(QK) ** -0.5)
        attend(nc, K, "moba", [Head([(qt[:, 4 + h], kt[:, 4 + h])], value(vd4, h, 0), mix[:, 4 + h])
                               for h in range(4)], T, seen, causal, float(P) ** -0.5)
        project_residual(nc, K, "l1_out", dram["l1_w_out"], mix)


def modulation(nc, K, layer, M):
    m = K.mod[layer]
    with stage(nc, f"mod{layer}") as st:
        biased = st.sem("biased")
        block = st.ctx.enter_context(nc.Block())

        @block.vector
        def _(dve):
            bias = K.col("b_mod_2")[:, layer * MT:(layer + 1) * MT]
            for s, count in ((0, MT), (1, 5 * DC))[:m.shape[2]]:
                dve.tensor_tensor(m[:, 0:count, s], m[:, 0:count, s], bias[:, 0:count], ALU.add)\
                    .then_inc(biased, 1)
            dve.wait_ge(biased, m.shape[2])
            for k in range(3):
                g = K.col("norm_g_2")[:, (layer * 3 + k) * DC:(layer * 3 + k + 1) * DC]
                for s in range(m.shape[2] if k < 2 else 1):
                    scale = m[:, (3 * k + 1) * DC:(3 * k + 2) * DC, s]
                    dve.scalar_tensor_tensor(out=M.gain[:, k, s], in0=scale, scalar=1.0, in1=g,
                                             op0=ALU.add, op1=ALU.mult)
            for n, k in enumerate((2, 8)):
                for s in range(m.shape[2] if n == 0 else 1):
                    dve.tensor_scalar(M.half[:, n, s], m[:, k * DC:(k + 1) * DC, s], 0.5, None, ALU.mult)
            dve.tensor_tensor(M.pool[:], m[:, 5 * DC:6 * DC, 0], K.col("pool_scale_2"), ALU.mult)


class Stream:

    def __init__(self, x, gain, shift, gate, pair, load=None):
        self.x, self.gain, self.shift, self.gate, self.pair, self.load = x, gain, shift, gate, pair, load


def swiglu(nc, K, name, wi, wo, streams):
    n_s = len(streams)
    raws = 4
    with stage(nc, name) as st:
        w1_in = [st.sem(f"w1_in{s}") for s in range(raws)]
        w2_in = [st.sem(f"w2_in{s}") for s in range(raws)]
        stream_in = st.sem("stream_in")
        hi_1, lo_1, product, silued, gated, g_hi, g_lo = (
            st.sem(x) for x in ("hi_1", "lo_1", "product", "silued", "gated", "g_hi", "g_lo"))
        hi_2, lo_2, out_sum = (st.sem(x) for x in ("hi_2", "lo_2", "out_sum"))
        raw = st.sb("raw", [P, raws, D])
        hi, lo = st.sb("hi", [P, 2, D], F32R), st.sb("lo", [P, 2, D], F32R)
        g = st.sb("g", [P, 2, FT, n_s * T], F32R)
        gv = st.sb("gv", [P, 2, n_s * T])
        sl = st.sb("silu", [P, 2, n_s * T])
        acc = st.ps("acc", [P, 8, 512])
        au = lambda k, j: acc[:, 2 * k + j, 0:n_s * T]

        def out_ps(s, c):
            at = 4 * (s if n_s == 2 else 1) + c // 2
            return acc[:, at, (c % 2) * T:(c % 2 + 1) * T]

        norms = [Norm(st, K, f"n{n}", x.x, x.gain, x.shift, pair=x.pair, total=acc[:, 7 - n, 0:T])
                 for n, x in enumerate(streams)]
        block = st.ctx.enter_context(nc.Block())

        @block.sync
        def _(sp):
            for x in streams:
                if x.load is not None:
                    sp.dma_start(x.x[:], x.load).then_inc(stream_in, 16)
            for n in range(raws):
                sp.dma_start(raw[:, n], wi[n // 2, :, n % 2]).then_inc(w1_in[n], 16)
            with sp.Fori(1, FT // 2) as i:
                for n in range(raws):
                    sp.wait_ge(lo_1, i * raws + n - (raws - 1))
                    sp.dma_start(raw[:, n], wi[i * 2 + n // 2, :, n % 2]).then_inc(w1_in[n], 16)

            def second(f, slot):
                sp.dma_start(raw[:, slot], wo[f]).then_inc(w2_in[slot], 16)

            for f in range(raws):
                sp.wait_ge(lo_1, 2 * FT - (raws - 1) + f)
                second(f, f)
            for f in range(4, 6):
                sp.wait_ge(lo_2, f - (raws - 1))
                second(f, f % raws)
            with sp.Fori(1, (FT - 2) // 4) as i:
                for k in range(4):
                    sp.wait_ge(lo_2, i * 4 + k + 2 - (raws - 1))
                    second(i * 4 + k + 2, (k + 2) % raws)

        @block.tensor
        def _(pe):
            for n in norms:
                n.tensor(pe)

            def first(i, k, j, made=True):
                unit = i * 4 + 2 * k + j
                out = au(k, j)
                pe.wait_ge(hi_1, unit + 1)
                for c in range(DC):
                    w = hi[:, j, c * P:(c + 1) * P]
                    for s, x in enumerate(streams):
                        if not made:
                            pe.wait_ge(norms[s].done, c + 1)
                        at = out[:, s * T:(s + 1) * T]
                        pe.matmul(at, w, x.pair[:, 0, c], start=c == 0 and s == 0, stop=False, skip_group_check=True)
                        pe.matmul(at, w, x.pair[:, 1, c], start=False, stop=False, skip_group_check=True)
                pe.wait_ge(lo_1, unit + 1)
                for c in range(DC):
                    w = lo[:, j, c * P:(c + 1) * P]
                    for s, x in enumerate(streams):
                        mm = pe.matmul(out[:, s * T:(s + 1) * T], w, x.pair[:, 0, c], start=False,
                                       stop=c == DC - 1, skip_group_check=True)
                mm.then_inc(product, 1)

            for k in range(2):
                for j in range(2):
                    first(0, k, j, k + j > 0)
            with pe.Fori(1, FT // 2) as i:
                for k in range(2):
                    pe.wait_ge(gated, i * 2 + k - 1)
                    for j in range(2):
                        first(i, k, j)

            def second(f, k, start=False):
                pe.wait_ge(g_lo, f + 1)
                pe.wait_ge(hi_2, f + 1)
                gs = lambda cut, s: g[:, cut, bass.ds(f, 1), s * T:(s + 1) * T]
                for c in range(DC):
                    w = hi[:, k, c * P:(c + 1) * P]
                    for s in range(n_s):
                        pe.matmul(out_ps(s, c), w, gs(0, s), start=start and c % 2 == 0, stop=False,
                                  skip_group_check=True)
                        pe.matmul(out_ps(s, c), w, gs(1, s), start=False, stop=False, skip_group_check=True)
                pe.wait_ge(lo_2, f + 1)
                for c in range(DC):
                    for s in range(n_s):
                        mm = pe.matmul(out_ps(s, c), lo[:, k, c * P:(c + 1) * P], gs(0, s), start=False,
                                       stop=False, skip_group_check=True)
                mm.then_inc(out_sum, 1)

            if n_s == 2:
                pe.wait_ge(gated, FT)
            for k in range(2):
                second(k, k, k == 0)
            with pe.Fori(0, (FT - 2) // 4) as i:
                for k in range(4):
                    second(i * 4 + k + 2, k % 2)

        @block.scalar
        def _(act):
            for n, x in zip(norms, streams):
                if x.load is not None:
                    act.wait_ge(stream_in, 16)
                n.scalar_squares(act)

            def cut_first(i, k, j, fresh=False):
                act.wait_ge(w1_in[2 * k + j], i * 16 + 16)
                if not fresh:
                    act.wait_ge(product, i * 4 + 2 * k + j - 1)
                cut_hi(act, hi[:, j], raw[:, 2 * k + j]).then_inc(hi_1, 1)

            def silu(f, k, fresh=False):
                act.wait_ge(product, f * 2 + 1)
                if not fresh:
                    act.wait_ge(gated, f - 1)
                act.activation(sl[:, k], au(k, 0), ACT.Silu).then_inc(silued, 1)

            def cut_g(f, k):
                act.wait_ge(gated, f + 1)
                cut_hi(act, g[:, 0, bass.ds(f, 1)], gv[:, k:k + 1]).then_inc(g_hi, 1)

            for k in range(2):
                if k == 1:
                    for n in norms:
                        n.scalar(act)
                for j in range(2):
                    cut_first(0, k, j, k == 0)
            silu(0, 0, True)

            def first_body(i, fresh=False):
                for k in range(2):
                    for j in range(2):
                        cut_first(i, k, j)
                    silu(i * 2 + k - 1, 1 - k, fresh and k == 0)
                    cut_g(i * 2 + k - 2, k)

            first_body(1, True)
            with act.Fori(2, FT // 2) as i:
                first_body(i)
            silu(FT - 1, 1)
            for f in (FT - 2, FT - 1):
                cut_g(f, f % 2)

            def cut_second(f, slot, last_load):
                act.wait_ge(w2_in[slot], last_load)
                cut_hi(act, hi[:, slot % 2], raw[:, slot]).then_inc(hi_2, 1)

            for f in range(2):
                act.wait_ge(product, 2 * FT - 1 + f)
                cut_second(f, f, 16)
            with act.Fori(0, (FT - 2) // 4) as i:
                for k in range(4):
                    act.wait_ge(out_sum, i * 4 + k + 1)
                    cut_second(i * 4 + k + 2, (k + 2) % raws, i * 16 + (16 if k < 2 else 32))

        @block.vector
        def _(dve):
            for n, x in zip(norms, streams):
                if x.load is not None:
                    dve.wait_ge(stream_in, 16)
                n.vector_squares(dve)

            def low_first(i, k, j):
                dve.wait_ge(hi_1, i * 4 + 2 * k + j + 1)
                cut_lo(dve, lo[:, j], raw[:, 2 * k + j], hi[:, j]).then_inc(lo_1, 1)

            def gate(f, k, fresh=False):
                dve.wait_ge(silued, f + 1)
                if not fresh:
                    dve.wait_ge(g_lo, f - 1)
                dve.wait_ge(product, f * 2 + 2)
                dve.tensor_tensor(gv[:, k], au(k, 1), sl[:, k], ALU.mult).then_inc(gated, 1)

            def low_g(f, k):
                dve.wait_ge(g_hi, f + 1)
                cut_lo(dve, g[:, 1, bass.ds(f, 1)], gv[:, k:k + 1], g[:, 0, bass.ds(f, 1)]).then_inc(g_lo, 1)

            for k in range(2):
                if k == 1:
                    for n in norms:
                        n.vector(dve)
                for j in range(2):
                    low_first(0, k, j)
            gate(0, 0, True)

            def first_body(i, fresh=False):
                for k in range(2):
                    for j in range(2):
                        low_first(i, k, j)
                    gate(i * 2 + k - 1, 1 - k, fresh and k == 0)
                    low_g(i * 2 + k - 2, k)

            first_body(1, True)
            with dve.Fori(2, FT // 2) as i:
                first_body(i)
            gate(FT - 1, 1)
            for f in (FT - 2, FT - 1):
                low_g(f, f % 2)

            def low_second(f, slot):
                dve.wait_ge(hi_2, f + 1)
                cut_lo(dve, lo[:, slot % 2], raw[:, slot], hi[:, slot % 2]).then_inc(lo_2, 1)

            for f in range(2):
                low_second(f, f)
            with dve.Fori(0, (FT - 2) // 4) as i:
                for k in range(4):
                    low_second(i * 4 + k + 2, (k + 2) % raws)
            dve.wait_ge(out_sum, FT)
            for s, x in enumerate(streams):
                for c in range(DC):
                    dve.scalar_tensor_tensor(out=x.x[:, c], in0=out_ps(s, c), scalar=x.gate[:, c:c + 1],
                                             in1=x.x[:, c], op0=ALU.mult, op1=ALU.add)


def window_gla(nc, K, dram, m, M, ctx, ctx_pair):
    with ExitStack() as keep:
        def sb(name, shape, dt=F32):
            return keep.enter_context(nc.sbuf_tensor(f"wg_{name}", shape, dt))

        mix = sb("mix", [P, DC, T])
        K.rows = sb("rows", [P, NROW])
        w, x, xc = dram["w_in"], K.xp[:], ctx_pair[:]
        gq, gk, gv = sb("gq", [P, 2, T]), sb("gk", [P, 2, 2, T]), sb("gv", [P, 2, TT, 512])
        gr, zg = sb("gr", [P, 4, T]), sb("zg", [16, 2, 2, T])
        with ExitStack() as early:
            def eb(name, shape, dt=F32):
                return early.enter_context(nc.sbuf_tensor(f"wg_{name}", shape, dt))

            q = eb("q", [P, TT, 512])
            kv = eb("kv", [P, 2, TT, 256])
            qt, kt = eb("qt", [P, 4, T]), eb("kt", [P, WG, 2 * T])
            table, mask = eb("table", [P, TT, 4, 16]), eb("mask", [P, TT, 2 * T])
            full = eb("full", [P, TT, 2 * T])
            blocks = [
                Proj(w, 0, 512, x, "t", q[:]), Proj(w, 512, 256, x, "t", kv[:, 0]), Proj(w, 512, 256, xc, "t", kv[:, 1], src=1),
                Proj(w, 768, 256, x, "f", gq[:]), Proj(w, 1024, 256, x, "f", gk[:, 0]),
                Proj(w, 1024, 256, xc, "f", gk[:, 1], src=1), Proj(w, 1280, 512, x, "t", gv[:, 0]),
                Proj(w, 1280, 512, xc, "t", gv[:, 1], src=1),
            ]
            blocks += [Proj(w, 2304 + 16 * d, 16, y, "f", zg[:, d, s:s + 1], src=s) for d in range(2) for s, y in ((0, x), (1, xc))]
            blocks += [Proj(w, 1792, 512, x, "f", gr[:], ACT.Silu)]
            shift = m[:, 3 * DC:4 * DC]
            project(nc, "wg_in", blocks, lambda st: [
                Norm(st, K, "n", K.x, M.gain[:, 1, 0], shift[:, :, 0], pair=K.xp),
                Norm(st, K, "nc", ctx, M.gain[:, 1, 1], shift[:, :, 1], pair=ctx_pair),
            ], [(table[:], dram["rope_table"]), (K.rows[:], dram["rows"].partition_broadcast(P))])
            with stage(nc, "wg_mask") as st:
                step = st.sem("step")
                block = st.ctx.enter_context(nc.Block())

                @block.gpsimd
                def _(pool):
                    pool.memset(full[:], 0.0).then_inc(step, 1)
                    pool.memset(mask[:, :, T:2 * T], 0.0)
                    pool.wait_ge(step, 1)
                    pool.affine_select(out=full[:, :, 0:T], in_=full[:, :, 0:T], compare_op=ALU.is_ge, fill=NEG,
                                       base=P, pattern=[[P, TT], [-1, T]], channel_multiplier=1).then_inc(step, 1)
                    pool.wait_ge(step, 2)
                    pool.affine_select(out=mask[:, :, 0:T], in_=full[:, :, 0:T], compare_op=ALU.is_ge, fill=NEG,
                                       base=P, pattern=[[-P, TT], [1, T]], channel_multiplier=-1)

            q4 = q[:].rearrange("p t (h d) -> p t h d", h=WH)
            k4 = kv[:, 0, :, 0:128].rearrange("p t (h d) -> p t h d", h=WG)
            rope = ((0, table[:, :, 0], table[:, :, 1]), (32, table[:, :, 2], table[:, :, 3]))
            turns = [(0, q[:, :, P * i:P * (i + 1)], qt[:, i]) for i in range(4)]
            for g in range(WG):
                for at in (0, WD):
                    turns.append((1, k4[:, :, g], kt[at:at + WD, g, 0:T]))
                    turns.append((1, kv[:, 1, :, g * WD:(g + 1) * WD], kt[at:at + WD, g, T:2 * T]))
            token_norm_rope(nc, K, "wg_rope", [Tok(q4, None, rope, 16), Tok(k4, None, rope, 16)], turns)
            heads = []
            for i in range(WH):
                at, g = WD * (i % 2), i // (WH // WG)

                def v(c, g=g):
                    return kv[:, c // TT, c % TT, 128 + g * WD:128 + (g + 1) * WD]

                heads.append(Head([(qt[at:at + WD, i // 2], kt[at:at + WD, g])], v, mix[at:at + WD, i // 2],
                                  K.row("sink_2")[:, i:i + 1]))
            attend(nc, K, "window", heads, 2 * T, [[0, 1, 2, 3]] * 2, mask, WD ** -0.5)
        la = sb("la", [P, 2, 2, 2, T])
        log_decays(nc, K, dram, zg, la)
        gla(nc, K, gq, gk, gv, gr, la, mix)
        project_residual(nc, K, "wg_out", dram["w_out"], mix, m[:, 5 * DC:6 * DC, 0])


def log_decays(nc, K, dram, zg, la):
    with stage(nc, "decays") as st:
        loaded, product, biased, absed, exped, logged, v_step = (
            st.sem(x) for x in ("loaded", "product", "biased", "absed", "exped", "logged", "v_step"))
        w = st.sb("w", [16, 2, 256])
        z = st.sb("z", [P, 4, 2 * T])
        neg = st.sb("neg", [P, 4, 2 * T])
        ab = st.sb("ab", [P, 4, 2 * T])
        acc = st.ps("acc", [P, 4, 2 * T])
        block = st.ctx.enter_context(nc.Block())

        @block.sync
        def _(sp):
            sp.dma_start(w[:], dram["w_a2"]).then_inc(loaded, 16)

        @block.tensor
        def _(pe):
            pe.wait_ge(loaded, 16)
            for n in range(4):
                d, s = divmod(n, 2)
                for f in range(2):
                    mm = pe.matmul(acc[:, n, f * T:(f + 1) * T], w[:, d, f * P:(f + 1) * P], zg[:, d, s],
                                   start=True, stop=True)
            mm.then_inc(product, 1)

        @block.scalar
        def _(act):
            act.wait_ge(product, 1)
            for n in range(4):
                b = K.col("b_a_f_2" if n < 2 else "b_a_b_2")
                for f in range(2):
                    ins = act.activation(z[:, n, f * T:(f + 1) * T], acc[:, n, f * T:(f + 1) * T], ACT.Identity,
                                         bias=b[:, f:f + 1])
            ins.then_inc(biased, 1)
            act.wait_ge(absed, 1)
            act.activation(neg[:], ab[:], ACT.Exp, scale=-1.0).then_inc(exped, 1)
            act.wait_ge(exped, 1)
            act.activation(ab[:], neg[:], ACT.Ln, bias=K.ones[:, 0:1]).then_inc(logged, 1)

        @block.vector
        def _(dve):
            chain = Chain(dve, v_step)
            dve.wait_ge(biased, 1)
            dve.scalar_tensor_tensor(out=ab[:], in0=z[:], scalar=-1.0, in1=z[:], op0=ALU.mult, op1=ALU.max)\
                .then_inc(absed, 1)
            dve.wait_ge(logged, 1)
            chain(dve.scalar_tensor_tensor(out=neg[:], in0=z[:], scalar=0.0, in1=ab[:], op0=ALU.min,
                                           op1=ALU.subtract))
            dve.tensor_scalar(la[:].rearrange("p d s f t -> p (d s) (f t)"), neg[:], 1.0 / 16.0, None, ALU.mult)


def gla(nc, K, q, k, v, gr, la, mix):
    with stage(nc, "gla") as st:
        made, v_step, decayed, exped = (st.sem(x) for x in ("made", "v_step", "decayed", "exped"))
        keyed, turned, copied, summed = (st.sem(x) for x in ("keyed", "turned", "copied", "summed"))
        queried = st.sem("queried")
        scored, selected, stated, out_sum = (st.sem(x) for x in ("scored", "selected", "stated", "out_sum"))
        squared, normed, rooted = (st.sem(x) for x in ("squared", "normed", "rooted"))
        upto = st.sb("upto", [P, 2, P])
        pairs = st.sb("pairs", [P, 2, P], I32)
        carry_on = st.sb("carry_on", [P, 4 * T + BC])
        g2 = st.sb("g", [P, 2, 2, 2, T])
        e2 = st.sb("e", [P, 2, 3, 2, 2, T])
        qg2, kg2, ke2 = st.sb("qg", [P, 2, 2, T]), st.sb("kg", [P, 2, 2, T]), st.sb("ke", [P, 2, 2, 2, T])
        dec2 = st.sb("dec", [P, 2, 4, NBC])
        att2 = st.sb("att", [P, 2, 2, 2, TT, P])
        ket = st.sb("ket", [P, 2, 2, TT, P])
        carry = st.sb("carry", [P, 2, P])
        states2 = st.sb("states", [P, 2, NBC, 2, P])
        sq, root = st.sb("sq", [P, 2, 2, T]), st.sb("root", [P, 2, 2, T])
        t_ps = st.ps("t", [P, 2, 512])
        d_ps = st.ps("d", [P, 4, 512])
        o_ps = st.ps("o", [P, 2, 2, T])
        block = st.ctx.enter_context(nc.Block())
        sixteenth = lambda a: a.rearrange("p s f (n t) -> p (s f n) t", t=BC)
        flat = lambda a: a.rearrange("p s f t -> p (s f t)")
        add_of = lambda s, n, f: d_ps[:, 2 * s + n % 2, ((n // 2) * 2 + f) * P:((n // 2) * 2 + f + 1) * P]

        @block.gpsimd
        def _(pool):
            pool.memset(att2[:], 0.0)
            pool.memset(upto[:], 1.0).then_inc(made, 1)
            pool.memset(carry_on[:], 1.0).then_inc(made, 1)
            pool.wait_ge(made, 2)
            pool.memset(carry_on[:].rearrange("p (n t) -> p n t", t=BC)[:, :, 0:1], 0.0).then_inc(made, 1)
            pool.affine_select(out=upto[:, 0], in_=upto[:, 0], compare_op=ALU.is_ge, fill=0.0, base=0,
                               pattern=[[1, P]], channel_multiplier=-1).then_inc(made, 1)
            pool.affine_select(out=upto[:, 1], in_=upto[:, 1], compare_op=ALU.is_ge, fill=0.0, base=0,
                               pattern=[[-1, P]], channel_multiplier=1).then_inc(made, 1)
            pool.wait_ge(made, 5)
            pool.memset(upto[0:BC, 0, BC:P], 0.0).then_inc(made, 1)
            pool.memset(upto[BC:P, 1, 0:BC], 0.0).then_inc(made, 1)

        @block.vector
        def _(dve):
            chain = Chain(dve, v_step)
            dve.wait_ge(made, 7)
            chain(dve.tensor_copy(pairs[:], upto[:]))
            for d in range(2):
                g, e = g2[:, d], e2[:, d]
                last = BC - 1 if d == 0 else 0
                if d == 0:
                    chain(dve.tensor_tensor_scan(flat(g), carry_on[:, 0:4 * T], flat(la[:, d]), 0.0,
                                                 ALU.mult, ALU.add))
                else:
                    chain(dve.tensor_tensor_scan(flat(g)[:, ::-1], carry_on[:, 1:4 * T + 1][:, ::-1],
                                                 flat(la[:, d])[:, ::-1], 0.0, ALU.mult, ALU.add))
                gl = sixteenth(g)[:, :, last:last + 1]
                dve.tensor_tensor(sixteenth(e[:, 2]), gl.to_broadcast([P, 16, BC]), sixteenth(g), ALU.subtract)\
                    .then_inc(decayed, 1)
            for d in range(2):
                e = e2[:, d]
                dve.wait_ge(exped, d + 1)
                dve.tensor_tensor(ke2[:, d], k[:], e[:, 2], ALU.mult).then_inc(keyed, 1)
                dve.scalar_tensor_tensor(out=qg2[:, d], in0=q[:], scalar=float(BC) ** -0.5, in1=e[:, 0, 0],
                                         op0=ALU.mult, op1=ALU.mult)
                dve.tensor_tensor(kg2[:, d], k[:, 0], e[:, 1, 0], ALU.mult).then_inc(queried, 1)
            for d in range(2):
                att, states, dec = att2[:, d], states2[:, d], dec2[:, d]
                dve.wait_ge(scored, d + 1)
                dve.copy_predicated(att.rearrange("p a b t i -> p (a b t) i"),
                                    pairs[:, d].unsqueeze(1).to_broadcast([P, 8, P]),
                                    t_ps[:].rearrange("p a (b i) -> p (a b) i", i=P)).then_inc(selected, 1)
                chain(dve.memset(carry[:], 0.0))
                order = list(range(NBC)) if d == 0 else list(range(NBC))[::-1]
                for s in (1, 0):
                    for i, n in enumerate(order):
                        if s == 0 and i == 0:
                            chain(dve.tensor_copy(states[:, n], carry[:]))
                        if s == 0 and i == NBC - 1:
                            break
                        src = carry if s == 1 else states[:, n]
                        dst = carry if s == 1 else states[:, order[i + 1]]
                        for f in range(2):
                            ins = dve.scalar_tensor_tensor(out=dst[:, f], in0=src[:, f],
                                                           scalar=dec[:, 2 * s + f, n:n + 1],
                                                           in1=add_of(s, n, f), op0=ALU.mult, op1=ALU.add)
                        chain(ins)
                dve.engine_nop().then_inc(stated, 1)
            dve.wait_ge(rooted, 1)
            chain(dve.reciprocal(sq[:], root[:]))
            chain(dve.tensor_tensor(root[:], o_ps[:], sq[:], ALU.mult))
            for h in range(4):
                dve.scalar_tensor_tensor(out=mix[:, 4 + h], in0=root[:, h % 2, h // 2], scalar=K.col("gla_g_2"),
                                         in1=gr[:, h], op0=ALU.mult, op1=ALU.mult)

        @block.scalar
        def _(act):
            for d in range(2):
                g, e = g2[:, d], e2[:, d]
                last = BC - 1 if d == 0 else 0
                act.wait_ge(decayed, d + 1)
                act.activation(e[:, 2], e[:, 2], ACT.Exp)
                act.activation(dec2[:, d], g.rearrange("p s f (n t) -> p (s f) n t", t=BC)[:, :, :, last], ACT.Exp)
                act.activation(e[:, 0, 0], g[:, 0], ACT.Exp)
                act.activation(e[:, 1, 0], g[:, 0], ACT.Exp, scale=-1.0).then_inc(exped, 1)
            for d in range(2):
                act.wait_ge(turned, d + 1)
                if d:
                    act.wait_ge(summed, d)
                act.activation(ket[:].rearrange("p s f t e -> p s (f t e)"), t_ps[:], ACT.Copy).then_inc(copied, 1)
            act.wait_ge(out_sum, 2)
            act.activation(sq[:], o_ps[:], ACT.Square).then_inc(squared, 1)
            act.wait_ge(normed, 1)
            act.activation(root[:].rearrange("p a b t -> p a (b t)"), t_ps[:], ACT.Sqrt, bias=K.eps[:],
                           scale=1.0 / P).then_inc(rooted, 1)

        @block.tensor
        def _(pe):
            def turn(d):
                pe.wait_ge(keyed, d + 1)
                if d:
                    pe.wait_ge(selected, d)
                for s in range(2):
                    for f in range(2):
                        for t in range(TT):
                            mm = pe.transpose(t_ps[:, s, (2 * f + t) * P:(2 * f + t + 1) * P],
                                              ke2[:, d, s, f, t * P:(t + 1) * P], K.ident[:])
                mm.then_inc(turned, 1)

            def add(d):
                pe.wait_ge(copied, d + 1)
                if d:
                    pe.wait_ge(stated, d)
                for par in range(2):
                    for s in range(2):
                        for n in range(par, NBC, 2):
                            rows = slice(BC * par, BC * par + BC)
                            for h in range(4):
                                f, at = h // 2, BC * (h % 2)
                                mm = pe.matmul(add_of(s, n, f)[at:at + BC], ket[rows, s, f, n // 2, at:at + BC],
                                               v[rows, s, n // 2, h * P:(h + 1) * P], start=True, stop=True)
                mm.then_inc(summed, 1)

            def score(d):
                pe.wait_ge(queried, d + 1)
                for par in range(2):
                    rows = slice(BC * par, BC * par + BC)
                    for f in range(2):
                        for t in range(TT):
                            mm = pe.matmul(t_ps[:, par, (2 * f + t) * P:(2 * f + t + 1) * P],
                                           kg2[rows, d, f, t * P:(t + 1) * P], qg2[rows, d, f, t * P:(t + 1) * P],
                                           start=True, stop=True)
                mm.then_inc(scored, 1)

            def own(d):
                pe.wait_ge(selected, d + 1)
                for par in range(2):
                    for f in range(2):
                        for t in range(TT):
                            h = 2 * f + par
                            pe.matmul(o_ps[:, par, f, t * P:(t + 1) * P], v[:, 0, t, h * P:(h + 1) * P],
                                      att2[:, d, par, f, t], start=d == 0 and f == 0 and t == 0, stop=False,
                                      skip_group_check=True)

            def carried(d):
                pe.wait_ge(stated, d + 1)
                for par in range(2):
                    rows = slice(BC * par, BC * par + BC)
                    for f in range(2):
                        for n in range(NBC):
                            mm = pe.matmul(o_ps[:, par, f, n * BC:(n + 1) * BC], states2[rows, d, n, f],
                                           qg2[rows, d, f, n * BC:(n + 1) * BC], start=False, stop=d == 1,
                                           skip_group_check=True)
                mm.then_inc(out_sum, 1)

            turn(0)
            add(0)
            score(0)
            turn(1)
            own(0)
            add(1)
            carried(0)
            score(1)
            own(1)
            carried(1)
            pe.wait_ge(squared, 1)
            for a in range(2):
                mm = pe.matmul(t_ps[:, a], K.ones[:], sq[:, a].rearrange("p b t -> p (b t)"), start=True, stop=True)
            mm.then_inc(normed, 1)


def pool_mix(nc, K, dram, m, M):
    pad = 16
    wide = T + 2 * pad
    with stage(nc, "pool") as st:
        w_in, inv_in, cleared, v_step, product, ready = (
            st.sem(x) for x in ("w_in", "inv_in", "cleared", "v_step", "product", "ready"))
        w = st.sb("w", [P, 4, 2, T])
        inv = st.sb("inv", [P, 4, T])
        a, b, b2 = (st.sb(x, [P, DC, wide]) for x in ("a", "b", "b2"))
        pooled = st.sb("pooled", [P, DC, T])
        acc = st.ps("acc", [P, DC, T])
        h = a[:, :, pad:pad + T]
        norm = Norm(st, K, "n", K.x, M.gain[:, 1, 0], m[:, 3 * DC:4 * DC, 0], raw=h)
        block = st.ctx.enter_context(nc.Block())

        @block.sync
        def _(sp):
            sp.dma_start(w[:], dram["w_pool"].rearrange("g (c p) e -> p g c e", p=P)).then_inc(w_in, 16)
            sp.dma_start(inv[:], dram["pool_inv"].partition_broadcast(P)).then_inc(inv_in, 16)

        @block.gpsimd
        def _(pool):
            for x in (a, b, b2):
                pool.memset(x[:, :, 0:pad], 0.0)
                pool.memset(x[:, :, pad + T:], 0.0).then_inc(cleared, 1)

        @block.vector
        def _(dve):
            chain = Chain(dve, v_step)
            norm.vector_squares(dve)
            dve.wait_ge(cleared, 3)
            norm.vector(dve)
            dve.wait_ge(norm.done, DC)
            dve.wait_ge(inv_in, 16)
            src, dst, other = a, b, b2
            for g, (back, ahead) in enumerate(((1, 0), (1, 1), (2, 2), (4, 4))):
                lo, hi = 8, wide - 8
                chain(dve.tensor_tensor(dst[:, 2 * g:, lo:hi], src[:, 2 * g:, lo - back:hi - back],
                                        src[:, 2 * g:, lo + ahead:hi + ahead], ALU.add))
                cs = slice(2 * g, 2 * g + 2)
                chain(dve.tensor_tensor(pooled[:, cs], dst[:, cs, pad:pad + T],
                                        inv[:, g:g + 1].to_broadcast([P, 2, T]), ALU.mult))
                dve.tensor_tensor(pooled[:, cs], pooled[:, cs], h[:, cs], ALU.subtract).then_inc(ready, 1)
                src, dst, other = dst, other, dst
            for g in range(4):
                dve.wait_ge(product, g + 1)
                for c in (2 * g, 2 * g + 1):
                    dve.scalar_tensor_tensor(out=K.x[:, c], in0=acc[:, c], scalar=M.pool[:, c:c + 1], in1=K.x[:, c],
                                             op0=ALU.mult, op1=ALU.add)

        @block.tensor
        def _(pe):
            norm.tensor(pe)
            pe.wait_ge(w_in, 16)
            for g in range(4):
                pe.wait_ge(ready, g + 1)
                for j in range(2):
                    for c in range(2):
                        mm = pe.matmul(acc[:, 2 * g + j], w[:, g, c, j * P:(j + 1) * P], pooled[:, 2 * g + c],
                                       start=c == 0, stop=c == 1)
                mm.then_inc(product, 1)

        @block.scalar
        def _(act):
            norm.scalar_squares(act)
            norm.scalar(act)


def second_block(nc, K, dram, out):
    with ExitStack() as keep:
        def sb(name, shape, dt=F32):
            return keep.enter_context(nc.sbuf_tensor(f"b2_{name}", shape, dt))

        M = Store()
        M.gain, M.half, M.pool = sb("gain", [P, 3, 2, DC]), sb("half", [P, 2, 2, DC]), sb("pool", [P, DC])
        for layer in range(2):
            m = K.mod[layer]
            modulation(nc, K, layer, M)
            shift = lambda k, s: m[:, 3 * k * DC:(3 * k + 1) * DC, s]
            first = Stream(K.x, M.gain[:, 0, 0], shift(0, 0), M.half[:, 0, 0], K.xp)
            weights = dram["ffn1_wi"][layer], dram["ffn1_wo"][layer]
            if layer == 0:
                with nc.sbuf_tensor("ctx_stream", [P, DC, T], F32) as ctx, \
                        nc.sbuf_tensor("ctx_normed", [P, 2, DC, T], F32R) as ctx_pair:
                    swiglu(nc, K, "ffn1_0", *weights, [
                        first, Stream(ctx, M.gain[:, 0, 1], shift(0, 1), M.half[:, 0, 1], ctx_pair, dram["ctx"])])
                    window_gla(nc, K, dram, m, M, ctx, ctx_pair)
            else:
                swiglu(nc, K, "ffn1_1", *weights, [first])
                pool_mix(nc, K, dram, m, M)
            swiglu(nc, K, f"ffn2_{layer}", dram["ffn2_wi"][layer], dram["ffn2_wo"][layer],
                   [Stream(K.x, M.gain[:, 2, 0], shift(2, 0), M.half[:, 1, 0], K.xp)])
    finish(nc, K, out)


def finish(nc, K, out):
    with stage(nc, "finish") as st:
        stored = st.sem("stored")
        y = st.sb("y", [P, DC, T])
        norm = Norm(st, K, "n", K.x, K.col("final_g_2"), raw=y)
        block = st.ctx.enter_context(nc.Block())

        @block.sync
        def _(sp):
            for c in range(0, DC, 4):
                sp.wait_ge(norm.done, c + 4)
                sp.dma_start(out[:, c:c + 4], y[:, c:c + 4]).then_inc(stored, 16)
            sp.wait_ge(stored, 16 * 2)

        @block.tensor
        def _(pe):
            norm.tensor(pe)

        @block.scalar
        def _(act):
            norm.scalar_squares(act)
            norm.scalar(act)

        @block.vector
        def _(dve):
            norm.vector_squares(dve)
            norm.vector(dve)


def program(nc, dram, out):
    with ExitStack() as keep:
        K = Store()
        setup(nc, keep, dram, K)
        hgrn_gmlp(nc, K, dram)
        peer(nc, K, dram, 0)
        mla_moba(nc, K, dram)
        peer(nc, K, dram, 1)
        second_block(nc, K, dram, out)


def by_column(a):
    return np.asarray(a).reshape(-1, P).T


def layouts(a):
    feature_major = lambda x: np.ascontiguousarray(x[0].T.reshape(DC, P, T).transpose(1, 0, 2))
    half = np.arange(ROPE // 2, dtype=np.float32) / (ROPE // 2)
    inv_freq = np.float32(10000.0) ** (-half)
    rows = [inv_freq if name == "inv_freq" else np.asarray(a[name]).reshape(-1) for name, _ in ROWS]
    freqs = np.float32(10000.0) ** (-np.arange(16, dtype=np.float32) / np.float32(16))
    t = np.arange(T, dtype=np.float32)
    at = [(np.floor(t / 64)[:, None] * freqs).astype(np.float32), ((t % 64)[:, None] * freqs).astype(np.float32)]
    table = np.stack([f(x) for x in at for f in (np.cos, np.sin)], 1).astype(np.float32)
    counts = [np.minimum(t + w // 2, T) - np.maximum(t - w // 2, 0) for w in (2, 4, 8, 16)]
    out = {
        "x": feature_major(a["x"]),
        "ctx": feature_major(a["ctx_2"]),
        "cols": np.concatenate([by_column(a[name]) for name, _ in COLS], 1),
        "rows": np.concatenate(rows),
        "positions": a["positions"].reshape(TT, P).T,
        "l0_w_in": a["l0_w_in"], "l0_w_out": a["l0_w_out"], "l1_w_in": a["l1_w_in"], "l1_w_out": a["l1_w_out"],
        "w_s": a["l0_gmlp_w_s"].transpose(2, 0, 1),
        "l1_mla_w_uq": a["l1_mla_w_uq"], "l1_mla_w_ukv": a["l1_mla_w_ukv"],
        "w_mod": a["w_mod_2"].transpose(0, 2, 1).reshape(2, MT, P, D),
        "cond": np.stack([a["c_2"].reshape(D), a["c_ctx_2"].reshape(D)]),
        "w_in": a["w_in_2"][0], "w_out": a["w_out_2"][0],
        "w_a2": np.stack([a["w_a2_f_2"][0], a["w_a2_b_2"][0]], 1),
        "rope_table": table.reshape(TT, P, 4, 16).transpose(1, 0, 2, 3),
        "w_pool": a["w_pool_2"][0],
        "pool_inv": np.stack([np.float32(1) / c for c in counts]).astype(np.float32),
    }
    for n in ("ffn1", "ffn2"):
        out[f"{n}_wi"] = a[f"{n}_wi_2"].reshape(2, DC, P, 2, FT, P).transpose(0, 4, 2, 3, 1, 5)\
            .reshape(2, FT, P, 2, DC * P)
        out[f"{n}_wo"] = a[f"{n}_wo_2"].reshape(2, FT, P, D)
    for n in ("l0", "l1"):
        out[f"{n}_peer_w_query"] = a[f"{n}_peer_w_query"]
        out[f"{n}_sub_keys"] = a[f"{n}_peer_sub_keys"].transpose(3, 0, 1, 2).reshape(P, HP, NK)
        out[f"{n}_down"] = a[f"{n}_peer_expert_down"].reshape(NK, NK, DC, P).transpose(1, 3, 2, 0)\
            .reshape(NK, P, DC * NK)
        out[f"{n}_up"] = a[f"{n}_peer_expert_up"].reshape(NK, NK, D)
    return {name: np.ascontiguousarray(x) for name, x in out.items()}


def kernel(**inputs):
    import concourse.bacc as bacc
    from concourse.bass_utils import run_bass_kernel_spmd as run

    arrays = layouts({name: np.asarray(x) for name, x in inputs.items()})
    nc = bacc.Bacc("TRN2", target_bir_lowering=False, num_devices=1)
    dram = {name: nc.dram_tensor(f"in_{name}", x.shape, mybir.dt.from_np(x.dtype), kind="ExternalInput").ap()
            for name, x in arrays.items()}
    out = nc.dram_tensor("out", [P, DC, T], F32, kind="ExternalOutput").ap()
    dram["scores"] = nc.dram_tensor("scores", [2, P, TT, HP, NK], F32, kind="Internal").ap()
    program(nc, dram, out)
    result = run(nc, [{f"in_{name}": x for name, x in arrays.items()}], core_ids=[0])
    y = np.asarray(result.results[0]["out"])
    return np.ascontiguousarray(y.transpose(1, 0, 2).reshape(D, T).T)[None]
```

```python
from contextlib import ExitStack, contextmanager

import numpy as np

import concourse.bass as bass
from concourse import mybir

F32 = mybir.dt.float32
I32 = mybir.dt.int32
U32 = mybir.dt.uint32
F32R = mybir.dt.float32r
ALU = mybir.AluOpType
ACT = mybir.ActivationFunctionType
AX_X = mybir.AxisListType.X

P = 128
D = 1024
DC = D // P
T = 256
TT = T // P
EPS = 1e-6
NEG = -1.0e30
LOWEST = -3.0e38

PH, NK, PK = 8, 128, 16
HP = 2 * PH
TOKS = 4
RAWS = 4

AH, HC = 4, 32
NB = T // HC
CH, NOPE, ROPE = 4, 128, 64
QK = NOPE + ROPE
FF = 2816
FT = FF // P
NMOD = 9
MT = NMOD * D // P
BC = 64
NBC = T // BC
WH, WD, WG = 8, 64, 2

COLS = [
    ("l0_norm_mix", 8), ("l0_hgrn_out_norm", 4), ("l0_norm_ffn", 8), ("l1_norm_mix", 8),
    ("l1_mla_cq_norm", 2), ("l1_mla_ckv_norm", 1), ("l1_norm_ffn", 8), ("c_2", 8), ("c_ctx_2", 8),
    ("b_mod_2", 2 * MT), ("norm_g_2", 48), ("b_a_f_2", 2), ("b_a_b_2", 2), ("gla_g_2", 1),
    ("pool_scale_2", 8), ("final_g_2", 8), ("lb_logits", 12),
]
COL_AT, NCOL = {}, 0
for _name, _n in COLS:
    COL_AT[_name] = (NCOL, NCOL + _n)
    NCOL += _n
ROWS = [
    ("l0_gmlp_v_norm", 512), ("l1_mla_q_norm", QK), ("l1_mla_k_norm", QK), ("l1_moba_q_norm", 128),
    ("l1_moba_k_norm", 128), ("sink_2", 8), ("l0_gmlp_b_s", 512), ("inv_freq", 32),
]
ROW_AT, NROW = {}, 0
for _name, _n in ROWS:
    ROW_AT[_name] = (NROW, NROW + _n)
    NROW += _n

UNIT = 1024
STAGE_SEM = 170


class Stage:

    def __init__(self, nc, ctx, name):
        self.nc, self.ctx, self.name, self.n_sems = nc, ctx, name, 0

    def sb(self, name, shape, dt=F32):
        return self.ctx.enter_context(self.nc.sbuf_tensor(f"{self.name}_{name}", shape, dt))

    def ps(self, name, shape):
        return self.ctx.enter_context(self.nc.psum_tensor(f"{self.name}_{name}", shape, F32))

    def sem(self, name):
        self.n_sems += 1
        return self.ctx.enter_context(
            self.nc.semaphore(f"{self.name}_{name}", STAGE_SEM + self.n_sems - 1))


@contextmanager
def stage(nc, name):
    with ExitStack() as ctx:
        st = Stage(nc, ctx, name)
        yield st
    nc.all_engine_barrier(sems_to_clear=range(STAGE_SEM, STAGE_SEM + st.n_sems))


class Chain:

    def __init__(self, eng, sem):
        self.eng, self.sem, self.n = eng, sem, 0

    def __call__(self, instruction):
        self.n += 1
        instruction.then_inc(self.sem, 1)
        self.eng.wait_ge(self.sem, self.n)


class Store:
    pass


def setup(nc, keep, dram, K):
    def sb(name, shape, dt=F32):
        return keep.enter_context(nc.sbuf_tensor(name, shape, dt))

    K.x = sb("x_stream", [P, DC, T])
    K.xp = sb("x_normed", [P, 2, DC, T], F32R)
    K.cols = sb("cols", [P, NCOL])
    K.ones = sb("ones", [P, P])
    K.ident = sb("ident", [P, P])
    K.iota = sb("iota", [P, P])
    K.eps = sb("eps", [P, 1])
    K.lb = sb("lower_bound", [P, AH])
    K.nlb = sb("one_less_lower_bound", [P, AH])
    K.mod = [sb(f"mod{n}", [P, MT, 2 - n]) for n in range(2)]
    K.inv_freq = sb("inv_freq", [P, 32])
    K.cos, K.sin = sb("cos", [P, TT, 32]), sb("sin", [P, TT, 32])
    K.scores_stored = [keep.enter_context(nc.semaphore(f"scores_stored{i}", 150 + i)) for i in range(2 * TT)]
    K.col = lambda name: K.cols[:, COL_AT[name][0]:COL_AT[name][1]]
    K.row = lambda name: K.rows[:, ROW_AT[name][0]:ROW_AT[name][1]]

    with stage(nc, "setup") as st:
        cols_in, x_in, freq_in = st.sem("cols_in"), st.sem("x_in"), st.sem("freq_in")
        filled, v_step, exped = st.sem("filled"), st.sem("v_step"), st.sem("exped")
        cleared, shifted = st.sem("cleared"), st.sem("shifted")
        e = st.sb("e", [P, 3, AH])
        mx = st.sb("mx", [P, AH])
        mx2 = st.sb("mx2", [P, AH])
        block = st.ctx.enter_context(nc.Block())

        @block.sync
        def _(sp):
            sp.dma_start(K.cols[:], dram["cols"]).then_inc(cols_in, 16)
            sp.dma_start(K.x[:], dram["x"]).then_inc(x_in, 16)
            at = ROW_AT["inv_freq"]
            sp.dma_start(K.inv_freq[:], dram["rows"][at[0]:at[1]].partition_broadcast(P)).then_inc(freq_in, 16)
            sp.wait_ge(x_in, 16)
            sp.wait_ge(freq_in, 16)

        @block.gpsimd
        def _(pool):
            pool.memset(K.ones[:], 1.0)
            pool.memset(K.eps[:], EPS)
            pool.memset(K.ident[:], 0.0).then_inc(cleared, 1)
            pool.iota(K.iota[:], pattern=[[1, P]], base=0, channel_multiplier=0,
                      allow_small_or_imprecise_dtypes=True)
            pool.wait_ge(cleared, 1)
            pool.affine_select(out=K.ident[:], in_=K.ident[:], compare_op=ALU.not_equal, fill=1.0,
                               base=0, pattern=[[-1, P]], channel_multiplier=1).then_inc(filled, 1)

        @block.vector
        def _(dve):
            chain = Chain(dve, v_step)
            dve.wait_ge(cols_in, 16)
            lg = K.col("lb_logits").rearrange("p (r h) -> p r h", r=3)
            chain(dve.tensor_tensor(mx[:], lg[:, 0], lg[:, 1], ALU.max))
            chain(dve.tensor_tensor(mx2[:], mx[:], lg[:, 2], ALU.max))
            dve.tensor_tensor(e[:], lg, mx2[:].unsqueeze(1).to_broadcast([P, 3, AH]),
                              ALU.subtract).then_inc(shifted, 1)
            dve.wait_ge(exped, 1)
            chain(dve.tensor_tensor(mx[:], e[:, 0], e[:, 1], ALU.add))
            chain(dve.tensor_tensor(mx2[:], mx[:], e[:, 2], ALU.add))
            chain(dve.reciprocal(mx[:], mx2[:]))
            chain(dve.tensor_tensor(K.lb[:], e[:, 0], mx[:], ALU.mult))
            chain(dve.tensor_scalar(K.nlb[:], K.lb[:], -1.0, 1.0, ALU.mult, ALU.add))

        @block.scalar
        def _(act):
            act.wait_ge(shifted, 1)
            act.activation(e[:], e[:], ACT.Exp).then_inc(exped, 1)



def cut_hi(act, hi, v):
    return act.activation(hi, v, ACT.Copy)


def cut_lo(eng, lo, v, hi):
    return eng.tensor_tensor(lo, v, hi.bitcast(F32), ALU.subtract)


def multiply(pe, out, w_hi, w_lo, x_hi, x_lo, start, stop, lax=False):
    pe.matmul(out, w_hi, x_hi, start=start, stop=False, skip_group_check=lax)
    pe.matmul(out, w_hi, x_lo, start=False, stop=False, skip_group_check=lax)
    return pe.matmul(out, w_lo, x_hi, start=False, stop=stop, skip_group_check=lax)


class Norm:

    def __init__(self, st, K, tag, src, gain, shift=None, width=D, pair=None, raw=None, total=None):
        self.K, self.src, self.gain, self.shift, self.width = K, src, gain, shift, width
        self.pair, self.raw = pair, raw
        self.chunks, self.tokens = src.shape[1], src.shape[2]
        self.scalar_at = self.vector_at = self.scaled_at = 0
        self.squared_a, self.squared_v, self.summed, self.rooted, self.inverted, self.scaled, self.cut, self.done_v, self.done_p = (
            st.sem(f"{tag}_{x}") for x in
            ("squared_a", "squared_v", "summed", "rooted", "inverted", "scaled", "cut", "done_v", "done_p"))
        self.sq = st.sb(f"{tag}_sq", [P, self.chunks, self.tokens])
        self.root = st.sb(f"{tag}_root", [P, self.tokens])
        self.primed = st.sb(f"{tag}_primed", [P, 1])
        self.rstd = st.sb(f"{tag}_rstd", [P, self.tokens])
        self.total = st.ps(f"{tag}_total", [P, 512])[:, 0:self.tokens] if total is None else total

    def tensor(self, pe):
        for c in range(self.chunks):
            pe.wait_ge(self.squared_v if c % 2 else self.squared_a, c // 2 + 1)
            mm = pe.matmul(self.total, self.K.ones[:], self.sq[:, c], start=c == 0, stop=c == self.chunks - 1)
        mm.then_inc(self.summed, 1)

    def scalar_squares(self, act):
        for c in range(0, self.chunks, 2):
            act.activation(self.sq[:, c], self.src[:, c], ACT.Square).then_inc(self.squared_a, 1)
        act.activation(self.primed[:], self.K.eps[:], ACT.Sqrt)

    def vector_squares(self, dve):
        for c in range(1, self.chunks, 2):
            dve.tensor_tensor(self.sq[:, c], self.src[:, c], self.src[:, c], ALU.mult).then_inc(self.squared_v, 1)

    def scalar_root(self, act):
        act.wait_ge(self.summed, 1)
        act.activation(self.root[:], self.total, ACT.Sqrt, bias=self.K.eps[:], scale=1.0 / self.width)\
            .then_inc(self.rooted, 1)

    def vector_root(self, dve):
        dve.wait_ge(self.rooted, 1)
        dve.reciprocal(self.rstd[:], self.root[:]).then_inc(self.inverted, 1)
        dve.wait_ge(self.inverted, 1)

    def scalar_to(self, act, end):
        for c in range(self.scalar_at, end):
            act.wait_ge(self.scaled, c + 1)
            if self.shift is None:
                ins = cut_hi(act, self.pair[:, 0, c], self.sq[:, c])
            else:
                ins = act.activation(self.pair[:, 0, c], self.sq[:, c], ACT.Identity, bias=self.shift[:, c:c + 1])
                if c % 2:
                    ins = act.activation(self.sq[:, c], self.sq[:, c], ACT.Identity, bias=self.shift[:, c:c + 1])
            ins.then_inc(self.cut, 1)
        self.scalar_at = max(self.scalar_at, end)

    def vector_to(self, dve, end):
        for c in range(self.vector_at, end):
            for n in range(self.scaled_at, min(c + 3, self.chunks)):
                dve.scalar_tensor_tensor(out=self.sq[:, n], in0=self.src[:, n], scalar=self.gain[:, n:n + 1],
                                         in1=self.rstd[:], op0=ALU.mult, op1=ALU.mult).then_inc(self.scaled, 1)
                self.scaled_at = n + 1
            shift = 0.0 if self.shift is None else self.shift[:, c:c + 1]
            if self.pair is not None:
                if c % 2:
                    continue
                dve.wait_ge(self.cut, c + 1)
                ins = dve.scalar_tensor_tensor(out=self.pair[:, 1, c], in0=self.sq[:, c], scalar=shift,
                                               in1=self.pair[:, 0, c].bitcast(F32), op0=ALU.add, op1=ALU.subtract)
            else:
                dve.wait_ge(self.scaled, c + 1)
                ins = dve.tensor_scalar(self.raw[:, c], self.sq[:, c], shift, None, ALU.add)
            ins.then_inc(self.done_v, 1)
        self.vector_at = max(self.vector_at, end)

    def gpsimd(self, pool):
        for c in range(1, self.chunks, 2):
            pool.wait_ge(self.cut, c + 1)
            cut_lo(pool, self.pair[:, 1, c], self.sq[:, c], self.pair[:, 0, c]).then_inc(self.done_p, 1)

    def wait_chunk(self, eng, c):
        eng.wait_ge(self.done_p if c % 2 else self.done_v, c // 2 + 1)


class HeadNorms:

    def __init__(self, st, K, sq, sums, out):
        self.K, self.sq, self.sums, self.out, self.n = K, sq, sums, out, sq.shape[1] // P
        self.summed, self.rooted, self.inverted, self.spread = (
            st.sem(f"heads_{x}") for x in ("summed", "rooted", "inverted", "spread"))
        self.root, self.rstd = (st.sb(f"heads_{x}", [P, self.n]) for x in ("root", "rstd"))

    def tensor(self, pe):
        for i in range(self.n):
            mm = pe.matmul(self.sums[:, i:i + 1], self.sq[:, i * P:(i + 1) * P], self.K.ones[:, 0:1],
                           start=True, stop=True)
        mm.then_inc(self.summed, 1)
        pe.wait_ge(self.inverted, 1)
        for i in range(self.n):
            mm = pe.matmul(self.out[:, i * P:(i + 1) * P], self.rstd[:, i:i + 1].to_broadcast([P, P]),
                           self.K.ident[:], start=True, stop=True)
        mm.then_inc(self.spread, 1)

    def scalar(self, act):
        act.wait_ge(self.summed, 1)
        act.activation(self.root[:], self.sums, ACT.Sqrt, bias=self.K.eps[:], scale=1.0 / P).then_inc(self.rooted, 1)

    def vector(self, dve):
        dve.wait_ge(self.rooted, 1)
        dve.reciprocal(self.rstd[:], self.root[:]).then_inc(self.inverted, 1)


class Cut:

    def __init__(self, st, tag, v, pair):
        self.v, self.pair, self.chunks = v, pair, v.shape[1]
        self.cut, self.done_v, self.done_p = (st.sem(f"{tag}_{x}") for x in ("cut", "done_v", "done_p"))
        self.scalar_at = self.vector_at = 0

    def tensor(self, pe):
        pass

    def scalar_squares(self, act):
        pass

    def vector_squares(self, dve):
        pass

    def scalar_root(self, act):
        pass

    def vector_root(self, dve):
        pass

    def scalar_to(self, act, end):
        for c in range(self.scalar_at, end):
            cut_hi(act, self.pair[:, 0, c], self.v[:, c]).then_inc(self.cut, 1)
        self.scalar_at = max(self.scalar_at, end)

    def vector_to(self, dve, end):
        for c in range(self.vector_at, end):
            if c % 2 == 0:
                dve.wait_ge(self.cut, c + 1)
                cut_lo(dve, self.pair[:, 1, c], self.v[:, c], self.pair[:, 0, c]).then_inc(self.done_v, 1)
        self.vector_at = max(self.vector_at, end)

    def gpsimd(self, pool):
        for c in range(1, self.chunks, 2):
            pool.wait_ge(self.cut, c + 1)
            cut_lo(pool, self.pair[:, 1, c], self.v[:, c], self.pair[:, 0, c]).then_inc(self.done_p, 1)

    def wait_chunk(self, eng, c):
        eng.wait_ge(self.done_p if c % 2 else self.done_v, c // 2 + 1)


class Proj:

    def __init__(self, w, c0, width, x, form, out, func=ACT.Copy, gate=None, src=0):
        self.w, self.c0, self.width, self.x, self.form, self.out = w, c0, width, x, form, out
        self.func, self.gate, self.src = func, gate, src


class Units:
    RAWS = 6

    def __init__(self, ring, blocks):
        self.ring, self.blocks, self.units, self.last_of = ring, blocks, [], []
        self.preloaded = 0
        for b, blk in enumerate(blocks):
            chunks = blk.x.shape[2]
            step = max(1, min(chunks, UNIT // blk.width))
            self.units += [(b, c, min(c + step, chunks)) for c in range(0, chunks, step)]
            self.last_of.append(len(self.units) - 1)

    def view(self, buf, n):
        b, c0, c1 = self.units[n]
        blk = self.blocks[b]
        k, size = blk.x.shape[0], (c1 - c0) * blk.width
        return buf[0:k, 0:size], buf[0:k, 0:size].rearrange("p (c n) -> p c n", n=blk.width)

    def load(self, eng, n):
        b, c0, c1 = self.units[n]
        blk = self.blocks[b]
        k = blk.x.shape[0]
        return eng.dma_start(self.view(self.ring[:, n % self.RAWS], n)[1],
                             blk.w[c0 * k:c1 * k, blk.c0:blk.c0 + blk.width].rearrange("(c p) n -> p c n", p=k))

    def preload(self, sp, sem):
        self.preloaded = min(self.RAWS, len(self.units))
        for n in range(self.preloaded):
            self.load(sp, n).then_inc(sem[n], 16)
        for n in range(self.preloaded):
            sp.wait_ge(sem[n], 16)


def project(nc, name, blocks, sources=lambda st: (), loads=(), ahead=None):
    raws, pairs = Units.RAWS, 3
    with stage(nc, name) as st:
        loaded = [st.sem(f"loaded{s}") for s in range(raws)]
        cut, ready, product, evacuated, hi_out = (
            st.sem(x) for x in ("cut", "ready", "product", "evacuated", "hi_out"))
        others, ready_0 = st.sem("others"), st.sem("ready_0")
        stream = Units(st.sb("raw", [P, raws, UNIT]), blocks) if ahead is None else ahead
        raw, units, last_of, view = stream.ring, stream.units, stream.last_of, stream.view
        hi = st.sb("hi", [P, pairs, UNIT], F32R)
        lo = st.sb("lo", [P, pairs, UNIT], F32R)
        acc = st.ps("acc", [P, 2, 2 * 512])
        src = sources(st)
        block = st.ctx.enter_context(nc.Block())

        def makes_for(n):
            return range(n, min(n + (3 if n >= 4 else 1), len(units))) if src else ()

        def wait_ready(eng, n):
            if n == 0:
                eng.wait_ge(ready_0, 1)
            else:
                eng.wait_ge(ready, n)

        @block.sync
        def _(sp):
            for n in range(stream.preloaded, len(units)):
                if n >= raws:
                    wait_ready(sp, n - raws)
                stream.load(sp, n).then_inc(loaded[n % raws], 16)
            for n, (dst, source) in enumerate(loads):
                sp.dma_start(dst, source).then_inc(others, 16)
                sp.wait_ge(others, 16 * (n + 1))

        @block.tensor
        def _(pe):
            for s in src:
                s.tensor(pe)
            waited = [0] * len(src)
            for n, (b, c0, c1) in enumerate(units):
                blk = blocks[b]
                wait_ready(pe, n)
                if c0 == 0 and b >= 2:
                    pe.wait_ge(evacuated, b - 1)
                wh, wl = view(hi[:, n % pairs], n)[1], view(lo[:, n % pairs], n)[1]
                for c in range(c0, c1):
                    end = c == blk.x.shape[2] - 1
                    if src and waited[blk.src] < c + 1:
                        src[blk.src].wait_chunk(pe, c)
                        waited[blk.src] = c + 1
                    xh, xl = blk.x[:, 0, c], blk.x[:, 1, c]
                    if blk.form == "t":
                        for j in range(TT):
                            js = slice(j * P, (j + 1) * P)
                            mm = multiply(pe, acc[:, b % 2, j * 512:j * 512 + blk.width], xh[:, js], xl[:, js],
                                          wh[:, c - c0], wl[:, c - c0], c == 0, end)
                    else:
                        for j in range(-(-blk.width // P)):
                            m = min(P, blk.width - j * P)
                            js = slice(j * P, j * P + m)
                            mm = multiply(pe, acc[0:m, b % 2, j * T:(j + 1) * T], wh[:, c - c0, js],
                                          wl[:, c - c0, js], xh, xl, c == 0 and j % 2 == 0, end, lax=True)
                mm.then_inc(product, 1)

        def tiles(b):
            blk = blocks[b]
            m = min(P, blk.width)
            return acc[0:m, b % 2, 0:-(-blk.width // P) * T].rearrange("p (j t) -> p j t", t=T)

        @block.gpsimd
        def _(pool):
            pool.wait_ge(cut, 1)
            cut_lo(pool, view(lo[:, 0], 0)[0], view(raw[:, 0], 0)[0], view(hi[:, 0], 0)[0]).then_inc(ready_0, 1)
            for s in src:
                s.gpsimd(pool)

        @block.scalar
        def _(act):
            def evacuate(b):
                blk = blocks[b]
                if blk.form == "+":
                    return
                act.wait_ge(product, last_of[b] + 1)
                if blk.form == "t":
                    s = acc[:, b % 2, :].rearrange("p (j n) -> p j n", n=512)[:, :, 0:blk.width]
                    act.activation(blk.out, s, blk.func).then_inc(evacuated, 1)
                elif blk.form == "f":
                    act.activation(blk.out, tiles(b), blk.func).then_inc(evacuated, 1)
                else:
                    cut_hi(act, blk.out[:, 0], tiles(b)).then_inc(hi_out, 1)

            for s in src:
                s.scalar_squares(act)
            b = 0
            for n in range(len(units)):
                if n >= stream.preloaded:
                    act.wait_ge(loaded[n % raws], 16 * (n // raws + (0 if stream.preloaded else 1)))
                if n >= pairs:
                    act.wait_ge(product, n - pairs + 1)
                cut_hi(act, view(hi[:, n % pairs], n)[0], view(raw[:, n % raws], n)[0]).then_inc(cut, 1)
                if n == 0:
                    for s in src:
                        s.scalar_root(act)
                for m in makes_for(n):
                    src[blocks[units[m][0]].src].scalar_to(act, units[m][2])
                while b < len(blocks) and last_of[b] + pairs <= n:
                    evacuate(b)
                    b += 1
            for b in range(b, len(blocks)):
                evacuate(b)

        @block.vector
        def _(dve):
            def evacuate(b):
                blk = blocks[b]
                if blk.form == "+":
                    dve.wait_ge(product, last_of[b] + 1)
                    for j in range(blk.width // P):
                        scale = 1.0 if blk.gate is None else blk.gate[:, j:j + 1]
                        ins = dve.scalar_tensor_tensor(out=blk.out[:, j], in0=tiles(b)[:, j], scalar=scale,
                                                       in1=blk.out[:, j], op0=ALU.mult, op1=ALU.add)
                    ins.then_inc(evacuated, 1)
                elif blk.form == "p":
                    dve.wait_ge(hi_out, b + 1)
                    cut_lo(dve, blk.out[:, 1], tiles(b), blk.out[:, 0]).then_inc(evacuated, 1)

            for s in src:
                s.vector_squares(dve)
            for s in src:
                s.vector_root(dve)
            b = 0
            for n in range(len(units)):
                if n:
                    dve.wait_ge(cut, n + 1)
                    cut_lo(dve, view(lo[:, n % pairs], n)[0], view(raw[:, n % raws], n)[0],
                           view(hi[:, n % pairs], n)[0]).then_inc(ready, 1)
                for m in makes_for(n):
                    src[blocks[units[m][0]].src].vector_to(dve, units[m][2])
                while b < len(blocks) and last_of[b] + pairs <= n:
                    evacuate(b)
                    b += 1
            for b in range(b, len(blocks)):
                evacuate(b)


def residual_units(K, ring, w, gate=None):
    return Units(ring, [Proj(w, n * 512, 512, K.xp[:], "+", K.x[:, 4 * n:4 * n + 4],
                   gate=None if gate is None else gate[:, 4 * n:4 * n + 4]) for n in range(2)])


def project_residual(nc, K, name, units, x):
    project(nc, name, units.blocks, lambda st: [Cut(st, "x", x, K.xp)], ahead=units)


def hgrn_gmlp(nc, K, dram):
    with ExitStack() as keep:
        def sb(name, shape, dt=F32):
            return keep.enter_context(nc.sbuf_tensor(name, shape, dt))

        q, f, og = sb("hg_q", [P, AH, T]), sb("hg_f", [P, AH, T]), sb("hg_og", [P, AH, T])
        v, u, gv = sb("hg_v", [P, TT, 512]), sb("hg_u", [P, 4, T]), sb("hg_gv", [P, TT, 512])
        mix = sb("hg_mix", [P, DC, T])
        K.rows = sb("hg_rows", [P, NROW])
        w, x = dram["l0_w_in"], K.xp[:]
        project(nc, "l0_in", [
            Proj(w, 0, 512, x, "f", q[:]),
            Proj(w, 512, 512, x, "f", f[:], ACT.Sigmoid),
            Proj(w, 1024, 512, x, "t", v[:], ACT.Silu),
            Proj(w, 1536, 512, x, "f", og[:], ACT.Silu),
            Proj(w, 2048, 512, x, "f", u[:], ACT.Gelu_apprx_tanh),
            Proj(w, 2560, 512, x, "t", gv[:], ACT.Gelu_apprx_tanh),
        ], lambda st: [Norm(st, K, "n", K.x, K.col("l0_norm_mix"), pair=K.xp)],
            [(K.rows[:], dram["rows"].partition_broadcast(P))])
        out = residual_units(K, sb("l0_ring", [P, Units.RAWS, UNIT]), dram["l0_w_out"])
        hgrn(nc, K, q, f, v, og, mix, lambda st: Gmlp(st, K, dram, u, gv, mix), out)
        project_residual(nc, K, "l0_out", out, mix)


def hgrn(nc, K, q, f, v, og, mix, gmlp, next_units):
    with stage(nc, "hgrn") as st:
        v_step, masked, ready, product = (st.sem(x) for x in ("v_step", "masked", "ready", "product"))
        scored, turned, copied, state_add = (st.sem(x) for x in ("scored", "turned", "copied", "state_add"))
        state, added, out_sum, squared = (st.sem(x) for x in ("state", "added", "out_sum", "squared"))
        decay, ready_p = st.sem("decay"), st.sem("ready_p")
        SPLIT = AH * NB // 2
        cum = st.sb("cum", [P, AH, T])
        inner = st.sb("inner", [P, AH, T])
        first = st.sb("first", [P, AH, T])
        qd = st.sb("qd", [P, AH, T])
        decays = st.sb("decays", [P, 2, AH, T])
        decayed = decays[:, (HC - 1) % 2]
        pair = st.sb("pair", [P, 2, AH, T])
        onehot = st.sb("onehot", [P, HC, HC])
        score = st.sb("score", [HC, AH, T])
        own = st.sb("own", [P, P // HC])
        own2 = st.sb("own2", [P, P // HC])
        diag = st.sb("diag", [P, AH * TT, P // HC, HC])
        kt = st.sb("kt", [P, AH * TT, P])
        states = st.sb("states", [P, NB, AH, P])
        startm = st.sb("startm", [P, HC])
        sq = st.sb("sq", [P, AH, T])
        gated = st.sb("gated", [P, AH, T])
        a_ps = st.ps("a", [P, AH, T])
        t_ps = st.ps("t", [P, AH, T])
        d_ps = st.ps("d", [P, 2, 512])
        o_ps = st.ps("o", [P, AH, T])
        preloaded = [st.sem(f"preloaded{n}") for n in range(Units.RAWS)]
        head_norms = HeadNorms(st, K, sq[:].rearrange("p h t -> p (h t)"), d_ps[:, 1, 0:AH * TT],
                               a_ps[:].rearrange("p h t -> p (h t)"))
        gmlp = gmlp(st)
        at_ps = d_ps[:, 0, 0:AH * TT * HC].rearrange("p (n t) -> p n t", t=HC)
        block = st.ctx.enter_context(nc.Block())
        chunk = lambda a: a.rearrange("p h (b t) -> p (h b) t", t=HC)

        @block.sync
        def _(sp):
            gmlp.sync(sp)
            next_units.preload(sp, preloaded)

        @block.gpsimd
        def _(pool):
            pool.memset(onehot[:], 0.0).then_inc(masked, 1)
            pool.memset(own[:], 1.0).then_inc(masked, 1)
            pool.memset(startm[:], 0.0).then_inc(masked, 1)
            pool.wait_ge(masked, 3)
            pool.affine_select(out=onehot[:], in_=onehot[:], compare_op=ALU.not_equal, fill=1.0, base=0,
                               pattern=[[1, HC], [-1, HC]], channel_multiplier=0).then_inc(masked, 1)
            pool.affine_select(out=own2[:], in_=own[:], compare_op=ALU.is_ge, fill=0.0, base=0,
                               pattern=[[-HC, P // HC]], channel_multiplier=1).then_inc(masked, 1)
            pool.affine_select(out=startm[:], in_=startm[:], compare_op=ALU.not_equal, fill=1.0, base=0,
                               pattern=[[1, HC]], channel_multiplier=0).then_inc(masked, 1)
            pool.wait_ge(masked, 6)
            pool.affine_select(out=own[:], in_=own2[:], compare_op=ALU.is_ge, fill=0.0, base=HC - 1,
                               pattern=[[HC, P // HC]], channel_multiplier=-1).then_inc(masked, 1)
            qc = chunk(q[:])
            for i in range(HC):
                pool.wait_ge(decay, i + 1)
                if i >= 2:
                    pool.wait_ge(product, i - 1)
                pool.tensor_tensor(chunk(pair[:, i % 2])[:, 0:SPLIT, 0:i + 1],
                                   chunk(decays[:, i % 2])[:, 0:SPLIT, 0:i + 1],
                                   qc[:, 0:SPLIT, i:i + 1].to_broadcast([P, SPLIT, i + 1]), ALU.mult)\
                    .then_inc(ready_p, 1)
            gmlp.gpsimd(pool)

        @block.vector
        def _(dve):
            chain = Chain(dve, v_step)
            for h in range(AH):
                ins = dve.tensor_scalar(f[:, h], f[:, h], K.nlb[:, h:h + 1], K.lb[:, h:h + 1], ALU.mult, ALU.add)
            chain(ins)
            for n in range(2):
                ins = dve.tensor_scalar(decays[:, n], f[:], -1.0, 1.0, ALU.mult, ALU.add)
            chain(ins)
            dve.wait_ge(masked, 7)
            starts = startm[:].unsqueeze(1).to_broadcast([P, AH * NB, HC])
            chain(dve.tensor_tensor(chunk(first[:]), chunk(f[:]), starts, ALU.mult))
            chain(dve.tensor_tensor(inner[:], f[:], first[:], ALU.subtract))
            chain(dve.tensor_tensor_scan(cum[:].rearrange("p h t -> p (h t)"),
                                         inner[:].rearrange("p h t -> p (h t)"),
                                         first[:].rearrange("p h t -> p (h t)"), 0.0, ALU.mult, ALU.add))
            dve.tensor_tensor(qd[:], q[:], cum[:], ALU.mult)
            qc, fc = chunk(q[:]), chunk(f[:])
            dve.engine_nop().then_inc(decay, 1)
            for i in range(HC):
                src, dst = chunk(decays[:, (i + 1) % 2]), chunk(decays[:, i % 2])
                if i:
                    if i >= 2:
                        dve.wait_ge(ready_p, i - 1)
                    dve.tensor_tensor(dst[:, :, 0:i], src[:, :, 0:i],
                                      fc[:, :, i:i + 1].to_broadcast([P, AH * NB, i]), ALU.mult).then_inc(decay, 1)
                    dve.wait_ge(decay, i + 1)
                if i >= 2:
                    dve.wait_ge(product, i - 1)
                dve.tensor_tensor(chunk(pair[:, i % 2])[:, SPLIT:, 0:i + 1], dst[:, SPLIT:, 0:i + 1],
                                  qc[:, SPLIT:, i:i + 1].to_broadcast([P, AH * NB - SPLIT, i + 1]), ALU.mult)\
                    .then_inc(ready, 1)
            gmlp.vector_norm(dve)
            chain(dve.memset(states[:, 0], 0.0))
            for b in range(NB - 1):
                dve.wait_ge(state_add, b + 1)
                for h in range(AH):
                    t = b * HC + HC - 1
                    ins = dve.scalar_tensor_tensor(out=states[:, b + 1, h], in0=states[:, b, h],
                                                   scalar=cum[:, h, t:t + 1],
                                                   in1=d_ps[:, b % 2, h * P:(h + 1) * P],
                                                   op0=ALU.mult, op1=ALU.add)
                ins.then_inc(state, 1)
                dve.wait_ge(state, b + 1)
            dve.wait_ge(turned, 2)
            dve.tensor_tensor(
                diag[:], at_ps.unsqueeze(2).to_broadcast([P, AH * TT, P // HC, HC]),
                own[:].unsqueeze(1).unsqueeze(3).to_broadcast([P, AH * TT, P // HC, HC]), ALU.mult)\
                .then_inc(added, 1)
            dve.wait_ge(squared, 1)
            for h in range(AH):
                g = K.col("l0_hgrn_out_norm")[:, h:h + 1]
                ins = dve.scalar_tensor_tensor(out=gated[:, h], in0=o_ps[:, h], scalar=g, in1=og[:, h],
                                               op0=ALU.mult, op1=ALU.mult)
            chain(ins)
            head_norms.vector(dve)
            dve.wait_ge(head_norms.spread, 1)
            dve.tensor_tensor(mix[:, 0:AH], a_ps[:], gated[:], ALU.mult)
            gmlp.vector_gate(dve, t_ps)

        @block.tensor
        def _(pe):
            pe.wait_ge(masked, 7)
            for i in range(HC):
                pe.wait_ge(ready, i + 1)
                pe.wait_ge(ready_p, i + 1)
                for half in range(2):
                    hs = slice(half * 2, half * 2 + 2)
                    mm = pe.matmul(chunk(a_ps[0:HC, hs])[:, :, 0:i + 1], onehot[:, i, :],
                                   chunk(pair[:, i % 2, hs])[:, :, 0:i + 1],
                                   start=i == 0, stop=i == HC - 1, skip_group_check=True)
                mm.then_inc(product, 1)
            for h in range(AH):
                for t in range(TT):
                    mm = pe.transpose(t_ps[:, h, t * P:(t + 1) * P], decayed[:, h, t * P:(t + 1) * P], K.ident[:])
            mm.then_inc(turned, 1)
            pe.wait_ge(copied, 1)
            for b in range(NB - 1):
                t, at = b * HC // P, b * HC % P
                if b >= 2:
                    pe.wait_ge(state, b - 1)
                for h in range(AH):
                    mm = pe.matmul(d_ps[:, b % 2, h * P:(h + 1) * P], kt[at:at + HC, h * TT + t, :],
                                   v[at:at + HC, t, h * P:(h + 1) * P], start=True, stop=True)
                mm.then_inc(state_add, 1)
            pe.wait_ge(scored, 1)
            pe.wait_ge(state, NB - 1)
            for h in range(AH):
                for t in range(TT):
                    mm = pe.transpose(at_ps[:, h * TT + t, :], score[:, h, t * P:(t + 1) * P], K.ident[0:HC, 0:HC])
            mm.then_inc(turned, 1)
            pe.wait_ge(added, 1)
            for h in range(AH):
                for t in range(TT):
                    pe.matmul(o_ps[:, h, t * P:(t + 1) * P], v[:, t, h * P:(h + 1) * P],
                              diag[:, h * TT + t].rearrange("p j t -> p (j t)"),
                              start=h % 2 == 0 and t == 0, stop=False, skip_group_check=True)
            for h in range(AH):
                for b in range(1, NB):
                    mm = pe.matmul(o_ps[:, h, b * HC:(b + 1) * HC], states[:, b, h], qd[:, h, b * HC:(b + 1) * HC],
                                   start=False, stop=True, skip_group_check=True)
            mm.then_inc(out_sum, 1)
            pe.wait_ge(squared, 1)
            head_norms.tensor(pe)
            gmlp.tensor(pe, t_ps)

        @block.scalar
        def _(act):
            gmlp.scalar_squares(act)
            gmlp.scalar_root(act)
            act.wait_ge(turned, 1)
            act.activation(kt[:].rearrange("p (h t) k -> p h (t k)", t=TT), t_ps[:], ACT.Copy).then_inc(copied, 1)
            act.wait_ge(product, HC)
            act.activation(score[:], a_ps[0:HC], ACT.Copy).then_inc(scored, 1)
            act.wait_ge(out_sum, 1)
            act.activation(sq[:], o_ps[:], ACT.Square).then_inc(squared, 1)
            head_norms.scalar(act)


class Gmlp:
    GROUPS = 4

    def __init__(self, st, K, dram, u, gv, mix):
        self.K, self.dram, self.u, self.gv, self.mix = K, dram, u, gv, mix
        self.w_in, self.kept, self.squared, self.summed, self.rooted, self.v_step, self.normed, self.mixed = (
            st.sem(f"gmlp_{x}") for x in ("w_in", "kept", "squared", "summed", "rooted", "v_step", "normed", "mixed"))
        self.w, self.wc = (st.sb(f"gmlp_{x}", [P, self.GROUPS, P]) for x in ("w", "wc"))
        self.sq = st.sb("gmlp_sq", [P, TT * self.GROUPS, P])
        self.ss, self.root, self.rstd = (st.sb(f"gmlp_{x}", [P, TT * self.GROUPS]) for x in ("ss", "root", "rstd"))
        self.g4 = gv[:].rearrange("p n (g d) -> p (n g) d", g=self.GROUPS)

    def sync(self, sp):
        sp.dma_start(self.w[:], self.dram["w_s"]).then_inc(self.w_in, 16)

    def gpsimd(self, pool):
        pool.wait_ge(self.w_in, 16)
        pool.affine_select(out=self.wc[:], in_=self.w[:], compare_op=ALU.is_ge, fill=0.0, base=0,
                           pattern=[[0, self.GROUPS], [1, P]], channel_multiplier=-1).then_inc(self.kept, 1)

    def scalar_squares(self, act):
        act.activation(self.sq[:], self.g4, ACT.Square).then_inc(self.squared, 1)

    def scalar_root(self, act):
        act.wait_ge(self.summed, 1)
        act.activation(self.root[:], self.ss[:], ACT.Sqrt, bias=self.K.eps[:], scale=1.0 / P).then_inc(self.rooted, 1)

    def vector_norm(self, dve):
        chain = Chain(dve, self.v_step)
        dve.wait_ge(self.squared, 1)
        dve.tensor_reduce(self.ss[:], self.sq[:], AX_X, ALU.add).then_inc(self.summed, 1)
        dve.wait_ge(self.rooted, 1)
        chain(dve.reciprocal(self.rstd[:], self.root[:]))
        chain(dve.tensor_tensor(self.g4, self.g4,
                                self.rstd[:].unsqueeze(2).to_broadcast([P, TT * self.GROUPS, P]), ALU.mult))
        dve.tensor_tensor(self.gv[:], self.gv[:], self.K.row("l0_gmlp_v_norm").unsqueeze(1)
                          .to_broadcast([P, TT, 512]), ALU.mult).then_inc(self.normed, 1)

    def tensor(self, pe, acc):
        pe.wait_ge(self.kept, 1)
        pe.wait_ge(self.normed, 1)
        bias = self.K.row("l0_gmlp_b_s")
        for g in range(self.GROUPS):
            for n in range(TT):
                out = acc[:, g, n * P:(n + 1) * P]
                pe.matmul(out, self.gv[:, n, g * P:(g + 1) * P], self.wc[:, g, :], start=True, stop=False)
                mm = pe.matmul(out, self.K.ones[0:1, :], bias[0:1, g * P:(g + 1) * P], start=False, stop=True)
        mm.then_inc(self.mixed, 1)

    def vector_gate(self, dve, acc):
        dve.wait_ge(self.mixed, 1)
        dve.tensor_tensor(self.mix[:, 4:8], acc[:], self.u[:], ALU.mult)


def peer(nc, K, dram, layer, beside):
    name = f"peer{layer}"
    with nc.sbuf_tensor(f"{name}_raw", [P, RAWS, D], F32) as raw:
        with nc.sbuf_tensor(f"{name}_q", [P, 2, HP, T], F32R) as q, \
                nc.sbuf_tensor(f"{name}_keys", [P, HP, NK], F32) as keys:
            project(nc, f"{name}_q", [
                Proj(dram[f"l{layer}_peer_w_query"], n * 512, 512, K.xp[:], "p", q[:, :, 4 * n:4 * n + 4])
                for n in range(4)],
                lambda st: [Norm(st, K, "n", K.x, K.col(f"l{layer}_norm_ffn"), pair=K.xp)],
                [(keys[:], dram[f"l{layer}_sub_keys"])])
            peer_scores(nc, K, name, keys, q, dram["scores"][layer], dram[f"l{layer}_down"], raw, beside)
        peer_experts(nc, K, name, layer, dram, raw)


def peer_scores(nc, K, name, keys, q, out, down, raw, beside):
    with stage(nc, f"{name}_s") as st:
        product, copied = st.sem("product"), st.sem("copied")
        down_in = [st.sem(f"down_in{i}") for i in range(RAWS)]
        keys_pair = st.sb("keys_pair", [P, 2, HP, NK], F32R)
        s = st.sb("s", [P, TT, HP, NK])
        acc = st.ps("acc", [P, 4, 4, NK])
        by_four = lambda a: a.rearrange("p (b j) n -> p b (j n)", j=4)
        cut = Cut(st, "keys", by_four(keys[:]), keys_pair[:].rearrange("p s (b j) n -> p s b (j n)", j=4))
        beside = beside(st)
        block = st.ctx.enter_context(nc.Block())

        @block.sync
        def _(sp):
            beside.sync(sp)
            for k in range(RAWS):
                sp.dma_start(raw[:, k], down[k]).then_inc(down_in[k], 16)
            for i, done in enumerate(K.scores_stored):
                t, part = i // 2, slice(HP // 2 * (i % 2), HP // 2 * (i % 2 + 1))
                sp.wait_ge(copied, 2 * (i + 1))
                sp.dma_start(out[:, t, part], s[:, t, part]).then_inc(done, 16)
            for done in down_in:
                sp.wait_ge(done, 16)

        @block.tensor
        def _(pe):
            for n in range(TT * 4):
                t, b = divmod(n, 4)
                if t == 0:
                    cut.wait_chunk(pe, b)
                if n >= 4:
                    pe.wait_ge(copied, n - 3)
                for j in range(4):
                    hp, ts = 4 * b + j, slice(t * P, (t + 1) * P)
                    mm = multiply(pe, acc[:, n % 4, j], q[:, 0, hp, ts], q[:, 1, hp, ts], keys_pair[:, 0, hp],
                                  keys_pair[:, 1, hp], True, True)
                mm.then_inc(product, 1)

        @block.scalar
        def _(act):
            cut.scalar_to(act, 4)
            for n in range(TT * 4):
                t, b = divmod(n, 4)
                act.wait_ge(product, n + 1)
                act.activation(s[:, t, 4 * b:4 * b + 4], acc[:, n % 4], ACT.Copy).then_inc(copied, 1)
            beside.scalar(act)

        @block.gpsimd
        def _(pool):
            cut.gpsimd(pool)

        @block.vector
        def _(dve):
            cut.vector_to(dve, 4)
            beside.vector(dve)


def peer_experts(nc, K, name, layer, dram, raw):
    down, up, w_mod = dram[f"l{layer}_down"], dram[f"l{layer}_up"], dram["w_mod"][layer]
    BODIES = NK // RAWS
    NC = 2 - layer
    mod = K.mod[layer]
    A_FROM, A_PER = 11, 2
    A_MOD = A_PER * (BODIES - A_FROM)
    SILU_AT, EXP_AT = 7, 16
    C_MOD = MT - A_MOD
    CTX_MOD = 5 * DC
    ACT_TOKS = 3
    TAIL = 88
    with stage(nc, f"{name}_e") as st:
        down_in = [st.sem(f"down_in{i}") for i in range(RAWS)]
        up_in = [st.sem(f"up_in{i}") for i in range(RAWS)]
        mod_in = [st.sem(f"mod_in{i}") for i in range(A_PER)]
        s_in = [st.sem(f"s_in{t}") for t in range(TT)]
        cond_in, silued, mod_sum, mod_done = (st.sem(x) for x in ("cond_in", "silued", "mod_sum", "mod_done"))
        hi_down, lo_down, product, gelued = (st.sem(x) for x in ("hi_down", "lo_down", "product", "gelued"))
        v_step, shifted, exped, chosen, turned, copied = (
            st.sem(x) for x in ("v_step", "shifted", "exped", "chosen", "turned", "copied"))
        hot_a, hot_b, hot, routed, moved, weighted = (
            st.sem(x) for x in ("hot_a", "hot_b", "hot", "routed", "moved", "weighted"))
        hi_up, lo_up, hi_h, lo_h, out_sum = (st.sem(x) for x in ("hi_up", "lo_up", "hi_h", "lo_h", "out_sum"))
        hi = st.sb("hi", [P, 2, D], F32R)
        lo = st.sb("lo", [P, 2, D], F32R)
        h = st.sb("h", [P, NK, T])
        wm = st.sb("wm", [P, A_PER, D])
        cond = st.sb("cond", [P, 2, D])
        sums = st.sb("sums", [P, A_PER, NC])
        choice = st.sb("choice", [P, 3, T])
        den = st.sb("den", [P, TT * PH])
        rden = st.sb("rden", [P, TT * PH])
        tail = h[:, TAIL:].rearrange("p a t -> p (a t)")
        at = 0

        def part(size):
            nonlocal at
            at += size
            return tail[:, at - size:at]

        s = part(TT * HP * NK).rearrange("p (t a n) -> p t a n", t=TT, a=HP)
        cand = part(PH * PK * PK).rearrange("p (h c) -> p h c", h=PH)
        match = part(PH * PK * PK).rearrange("p (h j a) -> p h j a", h=PH, a=PK)
        val = part(HP * PK).rearrange("p (a k) -> p a k", k=PK)
        idx = part(HP * PK).bitcast(U32).rearrange("p (a k) -> p a k", k=PK)
        idxf = part(HP * PK).rearrange("p (a k) -> p a k", k=PK)
        pos, half = (part(PH * PK).bitcast(U32).rearrange("p (h k) -> p h k", k=PK) for _ in range(2))
        halff = part(PH * PK).rearrange("p (h k) -> p h k", k=PK)
        pick = choice[:, 0:2].rearrange("p n (t e) -> p n t e", t=TT)
        top = choice[:, 2].rearrange("p (t h j) -> p t h j", t=TT, h=PH)
        hots = wm[:].rearrange("p n (k a e) -> p n k a e", k=2, a=TOKS)
        a_hot, b_hot = hots[:, 0], hots[:, 1]
        g_sb = cond[:, 1].rearrange("p (k a e) -> p k a e", k=2, a=TOKS)
        h_hi, h_lo = K.xp[:, 0, 0:2], K.xp[:, 1, 0:2]
        s_ps = st.ps("s", [P, 2, 512])
        waste = st.ps("waste", [P, D])
        o_ps = st.ps("o", [P, DC, T])
        g_ps = o_ps[:, 0:4, :].rearrange("p (b c) t -> p b (c t)", b=2)
        t_ps = o_ps[:, 4:7, :]
        s_banks = [s_ps[:, 0, 0:T], s_ps[:, 1, 0:T], o_ps[:, 0], o_ps[:, 2]]
        block = st.ctx.enter_context(nc.Block())

        def top16(dve, chain, src, rows, values, indices):
            for first in (0, 8):
                for r in range(rows):
                    ins = dve.max(values[:, r, first:first + 8], src[:, r])
                chain(ins)
                for r in range(rows):
                    ins = dve.max_index(indices[:, r, first:first + 8], values[:, r, first:first + 8], src[:, r])
                chain(ins)
                if first == 0:
                    for r in range(rows):
                        ins = dve.match_replace(src[:, r], values[:, r, 0:8], src[:, r], LOWEST)
                    chain(ins)

        @block.sync
        def _(sp):
            def load_mod(n, k):
                sp.dma_start(wm[:, k], w_mod[n]).then_inc(mod_in[k], 16)

            def down_body(i):
                for k in range(RAWS):
                    sp.wait_ge(lo_down, i * RAWS + k - (RAWS - 1))
                    sp.dma_start(raw[:, k], down[i * RAWS + k]).then_inc(down_in[k], 16)

            for done in K.scores_stored:
                sp.wait_ge(done, 16 * (layer + 1))
            for t in range(TT):
                sp.dma_start(s[:, t], dram["scores"][layer][:, t]).then_inc(s_in[t], 16)
            with sp.Fori(1, SILU_AT - 3) as i:
                down_body(i)
            sp.dma_start(cond[:, 0:NC], dram["cond"][0:NC].partition_broadcast(P)).then_inc(cond_in, 16)
            with sp.Fori(SILU_AT - 3, A_FROM) as i:
                down_body(i)
            for k in range(A_PER):
                load_mod(k, k)
            with sp.Fori(A_FROM, A_FROM + 1) as i:
                down_body(i)
            with sp.Fori(A_FROM + 1, BODIES) as i:
                down_body(i)
                for k in range(A_PER):
                    sp.wait_ge(mod_done, i - A_FROM)
                    load_mod((i - A_FROM) * A_PER + k, k)
            for k in range(RAWS):
                sp.wait_ge(lo_down, NK - (RAWS - 1) + k)
                sp.dma_start(raw[:, k], up[:, k]).then_inc(up_in[k], 16)
            def up_body(i, with_mod):
                for k in range(RAWS):
                    sp.wait_ge(lo_up, i * RAWS + k - (RAWS - 1))
                    sp.dma_start(raw[:, k], up[:, bass.ds(i * RAWS + k, 1)].rearrange("p a d -> p (a d)"))\
                        .then_inc(up_in[k], 16)
                    if k == 0 and with_mod:
                        sp.wait_ge(mod_done, i + (A_MOD // A_PER - 1))
                        load_mod(i + (A_MOD - 1), 0)

            with sp.Fori(1, C_MOD + 1) as i:
                up_body(i, True)
            with sp.Fori(C_MOD + 1, BODIES) as i:
                up_body(i, False)

        @block.tensor
        def _(pe):
            def score(i, k, first=False):
                n = i * RAWS + k
                if not first:
                    pe.wait_ge(gelued, n - (RAWS - 1))
                pe.wait_ge(hi_down, n + 1)
                out = s_banks[k]
                for c in range(DC):
                    w = hi[:, k % 2, c * P:(c + 1) * P]
                    pe.matmul(out, w, K.xp[:, 0, c], start=c == 0, stop=False)
                    pe.matmul(out, w, K.xp[:, 1, c], start=False, stop=False)
                pe.wait_ge(lo_down, n + 1)
                for c in range(DC):
                    mm = pe.matmul(out, lo[:, k % 2, c * P:(c + 1) * P], K.xp[:, 0, c], start=False, stop=c == DC - 1)
                mm.then_inc(product, 1)

            for k in range(RAWS):
                score(0, k, True)
            with pe.Fori(1, BODIES) as i:
                for k in range(RAWS):
                    score(i, k)
            pe.wait_ge(chosen, 1)
            pe.wait_ge(gelued, NK)
            for n in range(2):
                for t in range(TT):
                    pe.transpose(t_ps[:, n, t * P:(t + 1) * P], pick[:, n, t], K.ident[:])
            for t in range(TT):
                mm = pe.transpose(t_ps[:, 2, t * P:(t + 1) * P],
                                  top[:, t].rearrange("p h j -> p (h j)"), K.ident[:])
            mm.then_inc(turned, 1)

            def route(i, k):
                pe.wait_ge(hot, i * 2 + k + 1)
                pe.wait_ge(hot_b, i * 2 + k + 1)
                for a in range(TOKS):
                    mm = pe.matmul(g_ps[:, k, a * P:(a + 1) * P], a_hot[:, k, a], b_hot[:, k, a],
                                   start=True, stop=True)
                mm.then_inc(routed, 1)

            for k in range(2):
                route(0, k)
            with pe.Fori(1, T // (2 * TOKS)) as i:
                for k in range(2):
                    pe.wait_ge(moved, i * 2 + k - 1)
                    route(i, k)

            def accumulate(i, k, first=False):
                n = i * RAWS + k
                pe.wait_ge(lo_h, n + 1)
                pe.wait_ge(hi_up, n + 1)
                for c in range(DC):
                    w = hi[:, k % 2, c * P:(c + 1) * P]
                    pe.matmul(o_ps[:, c], w, h_hi[:, k % 2], start=first and c % 2 == 0, stop=False,
                              skip_group_check=True)
                    pe.matmul(o_ps[:, c], w, h_lo[:, k % 2], start=False, stop=False, skip_group_check=True)
                pe.wait_ge(lo_up, n + 1)
                for c in range(DC):
                    mm = pe.matmul(o_ps[:, c], lo[:, k % 2, c * P:(c + 1) * P], h_hi[:, k % 2], start=False,
                                   stop=False, skip_group_check=True)
                mm.then_inc(out_sum, 1)

            pe.wait_ge(weighted, T // TOKS)
            for k in range(RAWS):
                accumulate(0, k, k == 0)
            with pe.Fori(1, BODIES) as i:
                for k in range(RAWS):
                    accumulate(i, k)

        @block.scalar
        def _(act):
            def cut_down(i, k, first=False, preloaded=False):
                if not preloaded:
                    act.wait_ge(down_in[k], i * 16)
                if not first:
                    act.wait_ge(product, i * RAWS + k - 1)
                cut_hi(act, hi[:, k % 2], raw[:, k]).then_inc(hi_down, 1)

            def gelu(n, k):
                act.activation(h[:, bass.ds(n, 1), :], s_banks[k].unsqueeze(1), ACT.Gelu_apprx_tanh)\
                    .then_inc(gelued, 1)

            def body(i):
                for k in range(RAWS):
                    cut_down(i, k)
                    gelu(i * RAWS + k - 2, (k - 2) % RAWS)

            for k in range(RAWS):
                cut_down(0, k, k < 2, True)
                if k >= 2:
                    gelu(k - 2, k - 2)
            with act.Fori(1, SILU_AT) as i:
                body(i)
            act.wait_ge(cond_in, 16)
            act.activation(cond[:, 0:NC], cond[:, 0:NC], ACT.Silu).then_inc(silued, 1)
            with act.Fori(SILU_AT, EXP_AT) as i:
                body(i)
            act.wait_ge(shifted, 1)
            act.activation(choice[:, 2], choice[:, 2], ACT.Exp).then_inc(exped, 1)
            with act.Fori(EXP_AT, TAIL // RAWS) as i:
                body(i)
            act.wait_ge(chosen, 1)
            with act.Fori(TAIL // RAWS, BODIES) as i:
                body(i)
            for n in (NK - 2, NK - 1):
                act.wait_ge(product, n + 1)
                gelu(n, n % RAWS)
            act.wait_ge(turned, 1)
            act.activation(choice[:], t_ps, ACT.Copy).then_inc(copied, 1)

            def weigh_hot(i, k):
                act.wait_ge(hot_a, i * 2 + k + 1)
                for a in range(ACT_TOKS):
                    ins = act.activation(a_hot[:, k, a], a_hot[:, k, a], ACT.Copy,
                                         scale=choice[:, 2, bass.ds((i * 2 + k) * TOKS + a, 1)])
                ins.then_inc(hot, 1)

            def move(i, k, first=False):
                act.wait_ge(routed, i * 2 + k + 1)
                if not first:
                    act.wait_ge(weighted, i * 2 + k - 1)
                act.activation(g_sb[:, k].rearrange("p a e -> p (a e)"), g_ps[:, k], ACT.Copy).then_inc(moved, 1)

            for k in range(2):
                weigh_hot(0, k)
            for k in range(2):
                move(0, k, True)
                weigh_hot(1, k)
            with act.Fori(1, T // (2 * TOKS) - 1) as i:
                for k in range(2):
                    move(i, k)
                    weigh_hot(i + 1, k)
            for k in range(2):
                move(T // (2 * TOKS) - 1, k)

            def cut_up(i, k, first=False):
                n = i * RAWS + k
                if not first:
                    act.wait_ge(out_sum, n - 1)
                cut_hi(act, h_hi[:, k % 2:k % 2 + 1], h[:, bass.ds(n, 1), :]).then_inc(hi_h, 1)
                act.wait_ge(up_in[k], i * 16 + 16)
                cut_hi(act, hi[:, k % 2], raw[:, k]).then_inc(hi_up, 1)

            act.wait_ge(weighted, T // TOKS)
            for k in range(RAWS):
                cut_up(0, k, k < 2)
            with act.Fori(1, BODIES) as i:
                for k in range(RAWS):
                    cut_up(i, k)

        @block.gpsimd
        def _(pool):
            def low_down(i, k):
                pool.wait_ge(hi_down, i * RAWS + k + 1)
                cut_lo(pool, lo[:, k % 2], raw[:, k], hi[:, k % 2]).then_inc(lo_down, 1)

            with pool.Fori(0, BODIES) as i:
                for k in range(RAWS):
                    low_down(i, k)
            pool.wait_ge(gelued, NK)

            def weigh(i, k):
                pool.wait_ge(moved, i * 2 + k + 1)
                hh = h[:, :, bass.ds((i * 2 + k) * TOKS, TOKS)]
                pool.tensor_tensor(hh, g_sb[:, k].rearrange("p a e -> p e a"), hh, ALU.mult).then_inc(weighted, 1)

            with pool.Fori(0, T // (2 * TOKS)) as i:
                for k in range(2):
                    weigh(i, k)
            with pool.Fori(0, BODIES) as i:
                for k in range(RAWS):
                    n = i * RAWS + k
                    pool.wait_ge(hi_h, n + 1)
                    cut_lo(pool, h_lo[:, k % 2:k % 2 + 1], h[:, bass.ds(n, 1), :], h_hi[:, k % 2:k % 2 + 1])\
                        .then_inc(lo_h, 1)

        @block.vector
        def _(dve):
            chain = Chain(dve, v_step)
            iota16 = K.iota[:, 0:PK].unsqueeze(1).unsqueeze(1).to_broadcast([P, PH, PK, PK])
            for t in range(TT):
                dve.wait_ge(s_in[t], 16)
                top16(dve, chain, s[:, t], HP, val, idx)
                chain(dve.tensor_copy(idxf, idx))
                v2 = val.rearrange("p (h s) k -> p h s k", s=2)
                chain(dve.tensor_tensor(
                    cand.rearrange("p h (a b) -> p h a b", a=PK),
                    v2[:, :, 0].unsqueeze(3).to_broadcast([P, PH, PK, PK]),
                    v2[:, :, 1].unsqueeze(2).to_broadcast([P, PH, PK, PK]), ALU.add))
                top16(dve, chain, cand, PH, top[:, t], pos)
                for n in range(2):
                    if n == 0:
                        chain(dve.tensor_scalar(half, pos, 4, None, ALU.logical_shift_right))
                    else:
                        chain(dve.tensor_scalar(half, pos, PK - 1, None, ALU.bitwise_and))
                    chain(dve.tensor_copy(halff, half))
                    chain(dve.tensor_tensor(match, halff.unsqueeze(3).to_broadcast([P, PH, PK, PK]), iota16,
                                            ALU.is_equal))
                    i2 = idxf.rearrange("p (h s) k -> p h s k", s=2)[:, :, n]
                    chain(dve.tensor_tensor(match, match, i2.unsqueeze(2).to_broadcast([P, PH, PK, PK]), ALU.mult))
                    chain(dve.tensor_reduce(pick[:, n, t].rearrange("p (h j) -> p h j", h=PH), match, AX_X, ALU.add))
            tops = choice[:, 2].rearrange("p (a j) -> p a j", j=PK)
            chain(dve.tensor_copy(den[:].unsqueeze(2), tops[:, :, 0:1]))
            dve.tensor_tensor(tops, tops, den[:].unsqueeze(2).to_broadcast([P, TT * PH, PK]), ALU.subtract)\
                .then_inc(shifted, 1)

            def mod_columns(tile, slots, loads, done, conditions):
                for k in range(slots):
                    dve.wait_ge(mod_in[k], loads)
                    for n in range(conditions):
                        dve.tensor_tensor_reduce(waste[:], wm[:, k], cond[:, n], 1.0, 0.0, ALU.mult,
                                                 ALU.add, sums[:, k, n:n + 1]).then_inc(mod_sum, 1)
                        dve.wait_ge(mod_sum, done + (k * conditions + n + 1))
                dve.tensor_copy(mod[:, bass.ds(tile, slots), 0:conditions], sums[:, 0:slots, 0:conditions])\
                    .then_inc(mod_done, 1)

            BOTH = CTX_MOD // A_PER

            def mod_batch(j, conditions):
                dve.wait_ge(mod_done, j)
                done = j * (A_PER * conditions) + (0 if conditions == NC else BOTH * A_PER * (NC - 1))
                mod_columns(j * A_PER, A_PER, j * 16 + 16, done, conditions)

            dve.wait_ge(silued, 1)
            mod_columns(0, A_PER, 16, 0, NC)
            with dve.Fori(1, EXP_AT - A_FROM) as j:
                mod_batch(j, NC)
            dve.wait_ge(exped, 1)
            chain(dve.tensor_reduce(den[:], tops, AX_X, ALU.add))
            chain(dve.reciprocal(rden[:], den[:]))
            dve.tensor_tensor(tops, tops, rden[:].unsqueeze(2).to_broadcast([P, TT * PH, PK]), ALU.mult)\
                .then_inc(chosen, 1)
            with dve.Fori(EXP_AT - A_FROM, BOTH) as j:
                mod_batch(j, NC)
            with dve.Fori(BOTH, A_MOD // A_PER) as j:
                mod_batch(j, 1)
            dve.wait_ge(copied, 1)

            def make_hots(i, k):
                t = (i * 2 + k) * TOKS
                for n, toks in ((0, ACT_TOKS), (1, TOKS)):
                    ins = dve.tensor_tensor(hots[:, n, k, 0:toks], K.iota[:].unsqueeze(1).to_broadcast([P, toks, P]),
                                            choice[:, n, bass.ds(t, toks)].unsqueeze(2).to_broadcast([P, toks, P]),
                                            ALU.is_equal)
                    if n == 0:
                        ins.then_inc(hot_a, 1)
                for a in range(ACT_TOKS, TOKS):
                    ins = dve.tensor_scalar(a_hot[:, k, a], K.iota[:], choice[:, 0, bass.ds(t + a, 1)],
                                            choice[:, 2, bass.ds(t + a, 1)], ALU.is_equal, ALU.mult)
                ins.then_inc(hot_b, 1)

            for k in range(2):
                make_hots(0, k)
            with dve.Fori(1, T // (2 * TOKS)) as i:
                for k in range(2):
                    dve.wait_ge(routed, i * 2 + k - 1)
                    make_hots(i, k)

            def low_up(i, k):
                dve.wait_ge(hi_up, i * RAWS + k + 1)
                cut_lo(dve, lo[:, k % 2], raw[:, k], hi[:, k % 2]).then_inc(lo_up, 1)

            for k in range(RAWS):
                low_up(0, k)
            with dve.Fori(1, C_MOD + 1) as i:
                for k in range(RAWS):
                    low_up(i, k)
                    if k == 1:
                        dve.wait_ge(mod_done, i + (A_MOD // A_PER - 1))
                        mod_columns(i + (A_MOD - 1), 1, i * 16 + A_MOD // A_PER * 16,
                                    i + (A_MOD + CTX_MOD * (NC - 1) - 1), 1)
            with dve.Fori(C_MOD + 1, BODIES) as i:
                for k in range(RAWS):
                    low_up(i, k)
            dve.wait_ge(out_sum, NK)
            for c in range(0, DC, 2):
                dve.tensor_tensor(K.x[:, c:c + 2], o_ps[:, c:c + 2], K.x[:, c:c + 2], ALU.add)


class Head:

    def __init__(self, qk, v, out, scale, sink=None):
        self.qk, self.v, self.out, self.scale, self.sink = qk, v, out, scale, sink


def attend(nc, K, name, heads, keys, chunks_of, mask, next_units=None):
    units = [(h, t) for h in heads for t in range(TT)]
    with stage(nc, name) as st:
        scored, masked, shifted, exped, normed = (
            st.sem(x) for x in ("scored", "masked", "shifted", "exped", "normed"))
        turned, copied, product, stored, v_step = (
            st.sem(x) for x in ("turned", "copied", "product", "stored", "v_step"))
        preloaded = [st.sem(f"preloaded{n}") for n in range(Units.RAWS)]
        nch = keys // P
        m = st.sb("m", [P, 2, keys])
        p = st.sb("p", [P, 2, keys])
        pn = st.sb("pn", [P, 2, keys])
        pt = st.sb("pt", [P, 2, nch, P])
        small = st.sb("small", [P, 2, 6])
        s_ps = st.ps("s", [P, 2, 512])
        t_ps = st.ps("t", [P, 2, 512])
        o_ps = st.ps("o", [P, 2, 512])
        block = st.ctx.enter_context(nc.Block())

        def width(h):
            return h.out.shape[0]

        @block.sync
        def _(sp):
            if next_units is not None:
                next_units.preload(sp, preloaded)

        @block.tensor
        def _(pe):
            def score(n):
                h, t = units[n]
                if n >= 2:
                    pe.wait_ge(masked, n - 1)
                for i, (q, k) in enumerate(h.qk):
                    mm = pe.matmul(s_ps[:, n % 2, 0:keys], q[:, t * P:(t + 1) * P], k,
                                   start=i == 0, stop=i == len(h.qk) - 1)
                mm.then_inc(scored, 1)

            def turn(n):
                t = units[n][1]
                pe.wait_ge(normed, n + 1)
                if n >= 2:
                    pe.wait_ge(copied, n - 1)
                for c in chunks_of[t]:
                    mm = pe.transpose(t_ps[:, n % 2, c * P:(c + 1) * P], pn[:, n % 2, c * P:(c + 1) * P], K.ident[:])
                mm.then_inc(turned, 1)

            def combine(n):
                h, t = units[n]
                pe.wait_ge(copied, n + 1)
                if n >= 2:
                    pe.wait_ge(stored, n - 1)
                at = h.out.base_partition() if callable(h.out.base_partition) else h.out.base_partition
                cs = chunks_of[t]
                for c in cs:
                    mm = pe.matmul(o_ps[at:at + width(h), n % 2, 0:P], h.v(c), pt[:, n % 2, c],
                                   start=c == cs[0], stop=c == cs[-1])
                mm.then_inc(product, 1)

            score(0)
            for n in range(len(units) + 2):
                if n + 1 < len(units):
                    score(n + 1)
                if 1 <= n <= len(units):
                    turn(n - 1)
                if n >= 2:
                    combine(n - 2)

        @block.vector
        def _(dve):
            chain = Chain(dve, v_step)

            def maximum(n):
                h, t = units[n]
                z = small[:, n % 2]
                dve.wait_ge(scored, n + 1)
                if n >= 2:
                    dve.wait_ge(exped, n - 1)
                dve.scalar_tensor_tensor(out=m[:, n % 2], in0=s_ps[:, n % 2, 0:keys], scalar=h.scale,
                                         in1=mask[:, t], op0=ALU.mult, op1=ALU.add).then_inc(masked, 1)
                dve.wait_ge(masked, n + 1)
                chain(dve.tensor_reduce(z[:, 0:1], m[:, n % 2], AX_X, ALU.max))
                bound = z[:, 0:1] if h.sink is None else h.sink
                dve.tensor_scalar(z[:, 1:2], z[:, 0:1], bound, -1.0, ALU.max, ALU.mult).then_inc(shifted, 1)

            def norm(n):
                h, t = units[n]
                z = small[:, n % 2]
                dve.wait_ge(exped, n + 1)
                total = z[:, 2:3]
                if h.sink is not None:
                    chain(dve.tensor_tensor(z[:, 4:5], z[:, 2:3], z[:, 3:4], ALU.add))
                    total = z[:, 4:5]
                chain(dve.reciprocal(z[:, 5:6], total))
                if n >= 2:
                    dve.wait_ge(turned, n - 1)
                dve.tensor_scalar(pn[:, n % 2], p[:, n % 2], z[:, 5:6], None, ALU.mult).then_inc(normed, 1)

            for n in range(len(units) + 1):
                if n < len(units):
                    maximum(n)
                if n >= 1:
                    norm(n - 1)

        @block.scalar
        def _(act):
            def exps(n):
                h, t = units[n]
                z = small[:, n % 2]
                act.wait_ge(shifted, n + 1)
                if n >= 2:
                    act.wait_ge(normed, n - 1)
                ins = act.activation(p[:, n % 2], m[:, n % 2], ACT.Exp, bias=z[:, 1:2], accum_out=z[:, 2:3])
                if h.sink is not None:
                    ins = act.activation(z[:, 3:4], h.sink, ACT.Exp, bias=z[:, 1:2])
                ins.then_inc(exped, 1)

            def copies(n):
                h, t = units[n]
                cs = chunks_of[t]
                act.wait_ge(turned, n + 1)
                if n >= 2:
                    act.wait_ge(product, n - 1)
                act.activation(pt[:, n % 2, cs[0]:cs[-1] + 1].rearrange("p c q -> p (c q)"),
                               t_ps[:, n % 2, cs[0] * P:(cs[-1] + 1) * P], ACT.Copy).then_inc(copied, 1)

            def store(n):
                h, t = units[n]
                at = h.out.base_partition() if callable(h.out.base_partition) else h.out.base_partition
                act.wait_ge(product, n + 1)
                act.activation(h.out[:, t * P:(t + 1) * P], o_ps[at:at + width(h), n % 2, 0:P], ACT.Copy)\
                    .then_inc(stored, 1)

            for n in range(len(units) + 2):
                if n < len(units):
                    exps(n)
                if 1 <= n <= len(units):
                    copies(n - 1)
                if n >= 2:
                    store(n - 2)


class Tok:

    def __init__(self, x, gain=None, rope=(), half=0):
        self.x, self.gain, self.rope, self.half = x, gain, rope, half


def token_norm_rope(nc, K, name, items, turns, beside=None):
    with stage(nc, name) as st:
        squared, summed, rooted, v_step = (st.sem(x) for x in ("squared", "summed", "rooted", "v_step"))
        done, turned, copied = (st.sem(x) for x in ("done", "turned", "copied"))
        normed = [x for x in items if x.gain is not None]
        most = max([x.x.shape[2] * x.x.shape[3] for x in normed], default=1)
        widest = max([x.x.shape[2] * x.half for x in items], default=1) or 1
        sq = st.sb("sq", [P, 2, TT * most])
        ss = st.sb("ss", [P, 2, 32])
        root = st.sb("root", [P, 2, 32])
        rstd = st.sb("rstd", [P, 32])
        tmp = [st.sb(f"tmp{i}", [P, TT * widest]) for i in range(4)]
        t_ps = st.ps("t", [P, 4, 512])
        beside = beside and beside(st)
        block = st.ctx.enter_context(nc.Block())

        @block.sync
        def _(sp):
            if beside:
                beside.sync(sp)

        @block.scalar
        def _(act):
            def square(n):
                heads, width = normed[n].x.shape[2], normed[n].x.shape[3]
                v = sq[:, n % 2, 0:TT * heads * width].rearrange("p (t h d) -> p t h d", t=TT, h=heads)
                if n >= 2:
                    act.wait_ge(summed, n - 1)
                act.activation(v, normed[n].x, ACT.Square).then_inc(squared, 1)

            if beside:
                beside.scalar(act)
            for n in range(min(2, len(normed))):
                square(n)
            for n, it in enumerate(normed):
                heads, width = it.x.shape[2], it.x.shape[3]
                act.wait_ge(summed, n + 1)
                act.activation(root[:, n % 2, 0:TT * heads], ss[:, n % 2, 0:TT * heads], ACT.Sqrt, bias=K.eps[:],
                               scale=1.0 / width).then_inc(rooted, 1)
                if n + 2 < len(normed):
                    square(n + 2)
            for n, (item, src, dst) in enumerate(turns):
                act.wait_ge(turned, n + 1)
                act.activation(dst, t_ps[0:dst.shape[0], n % 4, 0:T], ACT.Copy).then_inc(copied, 1)

        @block.vector
        def _(dve):
            chain = Chain(dve, v_step)

            def total(n):
                heads, width = normed[n].x.shape[2], normed[n].x.shape[3]
                v = sq[:, n % 2, 0:TT * heads * width].rearrange("p (n d) -> p n d", d=width)
                dve.wait_ge(squared, n + 1)
                dve.tensor_reduce(ss[:, n % 2, 0:TT * heads], v, AX_X, ALU.add).then_inc(summed, 1)

            if normed:
                total(0)
            for n, it in enumerate(items):
                heads, width = it.x.shape[2], it.x.shape[3]
                if it.gain is not None:
                    if n + 1 < len(normed):
                        total(n + 1)
                    dve.wait_ge(rooted, n + 1)
                    chain(dve.reciprocal(rstd[:, 0:TT * heads], root[:, n % 2, 0:TT * heads]))
                    r = rstd[:, 0:TT * heads].rearrange("p (t h) -> p t h", t=TT)
                    for t in range(TT):
                        ins = dve.tensor_tensor(it.x[:, t], it.x[:, t],
                                                r[:, t].unsqueeze(2).to_broadcast([P, heads, width]), ALU.mult)
                    chain(ins)
                    for t in range(TT):
                        ins = dve.tensor_tensor(it.x[:, t], it.x[:, t],
                                                it.gain.unsqueeze(1).to_broadcast([P, heads, width]), ALU.mult)
                    chain(ins)
                half = it.half
                for at, cos, sin in it.rope:
                    x1, x2 = it.x[:, :, :, at:at + half], it.x[:, :, :, at + half:at + 2 * half]
                    a, b, c, d = (x[:, 0:TT * heads * half].rearrange("p (t h e) -> p t h e", t=TT, h=heads)
                                  for x in tmp)
                    for t in range(TT):
                        cs = cos[:, t].unsqueeze(1).to_broadcast([P, heads, half])
                        sn = sin[:, t].unsqueeze(1).to_broadcast([P, heads, half])
                        dve.tensor_tensor(a[:, t], x1[:, t], cs, ALU.mult)
                        dve.tensor_tensor(b[:, t], x2[:, t], sn, ALU.mult)
                        dve.tensor_tensor(c[:, t], x2[:, t], cs, ALU.mult)
                        ins = dve.tensor_tensor(d[:, t], x1[:, t], sn, ALU.mult)
                    chain(ins)
                    for t in range(TT):
                        dve.tensor_tensor(x1[:, t], a[:, t], b[:, t], ALU.subtract)
                        ins = dve.tensor_tensor(x2[:, t], c[:, t], d[:, t], ALU.add)
                    chain(ins)
                dve.engine_nop().then_inc(done, 1)
            if beside:
                beside.vector(dve)

        @block.tensor
        def _(pe):
            if beside:
                beside.tensor(pe)
            for n, (item, src, dst) in enumerate(turns):
                pe.wait_ge(done, item + 1)
                if n >= 4:
                    pe.wait_ge(copied, n - 3)
                for t in range(TT):
                    mm = pe.transpose(t_ps[0:dst.shape[0], n % 4, t * P:(t + 1) * P], src[:, t], K.ident[:])
                mm.then_inc(turned, 1)


class Angles:

    def __init__(self, st, K, dram):
        self.K, self.dram = K, dram
        self.pos_in, self.v_step, self.reduced = (st.sem(f"angles_{x}") for x in ("pos_in", "v_step", "reduced"))
        self.pos, self.whole = st.sb("pos", [P, TT], I32), st.sb("whole", [P, TT, 32], I32)
        self.posf = st.sb("posf", [P, TT])
        self.ang, self.turn, self.wholef, self.tmp = (
            st.sb(x, [P, TT, 32]) for x in ("ang", "turn", "wholef", "angle_tmp"))
        self.rest = st.sb("rest", [P, 2, TT, 32])

    def sync(self, sp):
        sp.dma_start(self.pos[:], self.dram["positions"]).then_inc(self.pos_in, 16)

    def vector(self, dve):
        c1 = 6.28125
        c2 = float(np.float32(np.floor((2 * np.pi - c1) * 2.0 ** 19) / 2.0 ** 19))
        c3 = float(np.float32(2 * np.pi - c1 - c2))
        posf, ang, turn, whole, wholef, tmp, rest = (
            self.posf, self.ang, self.turn, self.whole, self.wholef, self.tmp, self.rest)
        chain = Chain(dve, self.v_step)
        dve.wait_ge(self.pos_in, 16)
        chain(dve.tensor_copy(posf[:], self.pos[:]))
        for t in range(TT):
            ins = dve.tensor_scalar(ang[:, t], self.K.inv_freq[:], posf[:, t:t + 1], None, ALU.mult)
        chain(ins)
        for n, ahead in ((0, float(np.pi / 2)), (1, 0.0)):
            chain(dve.tensor_scalar(turn[:], ang[:], ahead, float(1 / (2 * np.pi)), ALU.add, ALU.mult))
            chain(dve.tensor_copy(whole[:], turn[:]))
            chain(dve.tensor_copy(wholef[:], whole[:]))
            chain(dve.scalar_tensor_tensor(out=tmp[:], in0=wholef[:], scalar=-c1, in1=ang[:],
                                           op0=ALU.mult, op1=ALU.add))
            chain(dve.scalar_tensor_tensor(out=turn[:], in0=wholef[:], scalar=-c2, in1=tmp[:],
                                           op0=ALU.mult, op1=ALU.add))
            chain(dve.scalar_tensor_tensor(out=tmp[:], in0=wholef[:], scalar=-c3, in1=turn[:],
                                           op0=ALU.mult, op1=ALU.add))
            chain(dve.tensor_scalar(turn[:], tmp[:], ahead, float(np.float32(3.1415925)), ALU.add, ALU.min))
            chain(dve.tensor_scalar(rest[:, n], turn[:], -float(np.float32(3.1415925)), None, ALU.max))
        dve.engine_nop().then_inc(self.reduced, 1)

    def scalar(self, act):
        act.wait_ge(self.reduced, 1)
        act.activation(self.K.cos[:], self.rest[:, 0], ACT.Sin)
        act.activation(self.K.sin[:], self.rest[:, 1], ACT.Sin)


def mla_moba(nc, K, dram):
    with ExitStack() as keep:
        def sb(name, shape, dt=F32):
            return keep.enter_context(nc.sbuf_tensor(f"mla_{name}", shape, dt))

        cq, ckv, kpe = sb("cq", [P, 2, T]), sb("ckv", [P, 1, T]), sb("kpe", [P, TT, ROPE])
        qd, kd, vd = sb("qd", [P, TT, 512]), sb("kd", [P, TT, 512]), sb("vd", [P, TT, 512])
        cqn, ckvn = sb("cqn", [P, 2, 2, T], F32R), sb("ckvn", [P, 2, 1, T], F32R)
        qc, kc = sb("qc", [P, TT, CH, QK]), sb("kc", [P, TT, CH, QK])
        kv = sb("kv", [P, TT, CH, 2 * P])
        qt, kt = sb("qt", [P, 8, T]), sb("kt", [P, 8, T])
        qpt, kpt = sb("qpt", [ROPE, CH, T]), sb("kpt", [ROPE, CH, T])
        mix = sb("mix", [P, DC, T])
        causal = sb("causal", [P, TT, T])
        K.rows = sb("rows", [P, NROW])
        w, x = dram["l1_w_in"], K.xp[:]
        project(nc, "l1_in", [
            Proj(w, 0, 256, x, "f", cq[:]),
            Proj(w, 256, 128, x, "f", ckv[:]),
            Proj(w, 384, ROPE, x, "t", kpe[:]),
            Proj(w, 448, 512, x, "t", qd[:]),
            Proj(w, 960, 512, x, "t", kd[:]),
            Proj(w, 1472, 512, x, "t", vd[:]),
        ], lambda st: [Norm(st, K, "n", K.x, K.col("l1_norm_mix"), pair=K.xp)],
            [(K.rows[:], dram["rows"].partition_broadcast(P))])
        qcf, kvf = (a[:].rearrange("p t h d -> p t (h d)") for a in (qc, kv))
        project(nc, "uq", [
            Proj(dram["l1_mla_w_uq"], 0, 384, cqn[:], "t", qcf[:, :, 0:384]),
            Proj(dram["l1_mla_w_uq"], 384, 384, cqn[:], "t", qcf[:, :, 384:768]),
            Proj(dram["l1_mla_w_ukv"], 0, 512, ckvn[:], "t", kvf[:, :, 0:512], src=1),
            Proj(dram["l1_mla_w_ukv"], 512, 512, ckvn[:], "t", kvf[:, :, 512:1024], src=1),
        ], lambda st: [Norm(st, K, "q", cq, K.col("l1_mla_cq_norm"), width=256, pair=cqn),
                       Norm(st, K, "kv", ckv, K.col("l1_mla_ckv_norm"), width=128, pair=ckvn)])
        with stage(nc, "mla_keys") as st:
            cleared, half = st.sem("cleared"), st.sem("half")
            block = st.ctx.enter_context(nc.Block())

            @block.vector
            def _(dve):
                for t in range(TT):
                    dve.tensor_copy(kc[:, t, :, 0:NOPE], kv[:, t, :, 0:NOPE])
                    dve.tensor_copy(kc[:, t, :, NOPE:QK], kpe[:, t].unsqueeze(1).to_broadcast([P, CH, ROPE]))

            @block.gpsimd
            def _(pool):
                pool.memset(causal[:], 0.0).then_inc(cleared, 1)
                pool.wait_ge(cleared, 1)
                pool.affine_select(out=causal[:], in_=causal[:], compare_op=ALU.is_ge, fill=NEG, base=0,
                                   pattern=[[P, TT], [-1, T]], channel_multiplier=1)

        qd4, kd4, vd4 = (a[:].rearrange("p t (h d) -> p t h d", h=4) for a in (qd, kd, vd))
        rope = ((NOPE, K.cos, K.sin),)
        token_norm_rope(nc, K, "mla_qk", [
            Tok(qc[:], K.row("l1_mla_q_norm"), rope, ROPE // 2), Tok(kc[:], K.row("l1_mla_k_norm"), rope, ROPE // 2),
            Tok(qd4, K.row("l1_moba_q_norm")), Tok(kd4, K.row("l1_moba_k_norm")),
        ], [(n, src[:, :, h, at:at + width], dst[:, h])
            for n, src, at, width, dst in ((0, qc, 0, NOPE, qt), (0, qc, NOPE, ROPE, qpt), (1, kc, 0, NOPE, kt),
                                           (1, kc, NOPE, ROPE, kpt), (2, qd4, 0, P, qt[:, 4:8]), (3, kd4, 0, P, kt[:, 4:8]))
            for h in range(4)])

        def value(a, h, lo):
            return lambda c: a[:, c, h, lo:lo + P]

        seen = [[0], [0, 1]]
        out = residual_units(K, sb("l1_ring", [P, Units.RAWS, UNIT]), dram["l1_w_out"])
        heads = [Head([(qt[:, h], kt[:, h]), (qpt[:, h], kpt[:, h])], value(kv, h, NOPE), mix[:, h],
                      float(QK) ** -0.5) for h in range(4)]
        heads += [Head([(qt[:, 4 + h], kt[:, 4 + h])], value(vd4, h, 0), mix[:, 4 + h], float(P) ** -0.5)
                  for h in range(4)]
        attend(nc, K, "mla_moba", heads, T, seen, causal, out)
        project_residual(nc, K, "l1_out", out, mix)


class Modulation:

    def __init__(self, K, layer):
        self.K, self.layer, self.m = K, layer, K.mod[layer]

    def part(self, n, s):
        return self.m[:, n * DC:(n + 1) * DC, s]

    def shift(self, k, s=0):
        return self.part(3 * k, s)

    def gain(self, k, s=0):
        return self.part(3 * k + 1, s)

    def gate(self, k, s=0):
        return self.part(3 * k + 2, s)

    def __call__(self, st):
        self.biased = st.sem("biased")
        return self

    def sync(self, sp):
        pass

    def scalar(self, act):
        pass

    def vector(self, dve):
        K, layer, m = self.K, self.layer, self.m
        bias = K.col("b_mod_2")[:, layer * MT:(layer + 1) * MT]
        for s, count in ((0, MT), (1, 5 * DC))[:m.shape[2]]:
            dve.tensor_tensor(m[:, 0:count, s], m[:, 0:count, s], bias[:, 0:count], ALU.add)\
                .then_inc(self.biased, 1)
        dve.wait_ge(self.biased, m.shape[2])
        for k in range(3):
            g = K.col("norm_g_2")[:, (layer * 3 + k) * DC:(layer * 3 + k + 1) * DC]
            for s in range(m.shape[2] if k < 2 else 1):
                dve.scalar_tensor_tensor(out=self.gain(k, s), in0=self.gain(k, s), scalar=1.0, in1=g,
                                         op0=ALU.add, op1=ALU.mult)
        for k in (0, 2):
            for s in range(m.shape[2] if k == 0 else 1):
                dve.tensor_scalar(self.gate(k, s), self.gate(k, s), 0.5, None, ALU.mult)
        if layer == 1:
            dve.tensor_tensor(self.gate(1), self.gate(1), K.col("pool_scale_2"), ALU.mult)


class Stream:

    def __init__(self, x, gain, shift, gate, pair, load=None):
        self.x, self.gain, self.shift, self.gate, self.pair, self.load = x, gain, shift, gate, pair, load


def swiglu(nc, K, name, wi, wo, streams):
    n_s = len(streams)
    raws = 4
    with stage(nc, name) as st:
        w1_in = [st.sem(f"w1_in{s}") for s in range(raws)]
        w2_in = [st.sem(f"w2_in{s}") for s in range(raws)]
        stream_in = st.sem("stream_in")
        hi_1, lo_1, product, silued, gated, g_hi, g_lo = (
            st.sem(x) for x in ("hi_1", "lo_1", "product", "silued", "gated", "g_hi", "g_lo"))
        lo_0 = st.sem("lo_0")
        hi_2, lo_2, out_sum = (st.sem(x) for x in ("hi_2", "lo_2", "out_sum"))
        raw = st.sb("raw", [P, raws, D])
        hi, lo = st.sb("hi", [P, 2, D], F32R), st.sb("lo", [P, 2, D], F32R)
        g = st.sb("g", [P, 2, FT, n_s * T], F32R)
        gv = st.sb("gv", [P, 2, n_s * T])
        sl = st.sb("silu", [P, 2, n_s * T])
        acc = st.ps("acc", [P, 8, 512])
        au = lambda k, j: acc[:, 2 * k + j, 0:n_s * T]

        def out_ps(s, c):
            at = 4 * (s if n_s == 2 else 1) + c // 2
            return acc[:, at, (c % 2) * T:(c % 2 + 1) * T]

        norms = [Norm(st, K, f"n{n}", x.x, x.gain, x.shift, pair=x.pair, total=acc[:, 7 - n, 0:T])
                 for n, x in enumerate(streams)]
        block = st.ctx.enter_context(nc.Block())

        @block.sync
        def _(sp):
            for x in streams:
                if x.load is not None:
                    sp.dma_start(x.x[:], x.load).then_inc(stream_in, 16)
            for n in range(raws):
                sp.dma_start(raw[:, n], wi[n // 2, :, n % 2]).then_inc(w1_in[n], 16)
            def load_first(i, n):
                sp.dma_start(raw[:, n], wi[i * 2 + n // 2, :, n % 2]).then_inc(w1_in[n], 16)

            sp.wait_ge(lo_0, 1)
            load_first(1, 0)
            for n in range(1, raws):
                sp.wait_ge(lo_1, n)
                load_first(1, n)
            with sp.Fori(2, FT // 2) as i:
                for n in range(raws):
                    sp.wait_ge(lo_1, i * raws + n - raws)
                    load_first(i, n)

            def second(f, slot):
                sp.dma_start(raw[:, slot], wo[f]).then_inc(w2_in[slot], 16)

            for f in range(raws):
                sp.wait_ge(lo_1, 2 * FT - raws + f)
                second(f, f)
            for f in range(4, 6):
                sp.wait_ge(lo_2, f - (raws - 1))
                second(f, f % raws)
            with sp.Fori(1, (FT - 2) // 4) as i:
                for k in range(4):
                    sp.wait_ge(lo_2, i * 4 + k + 2 - (raws - 1))
                    second(i * 4 + k + 2, (k + 2) % raws)

        @block.tensor
        def _(pe):
            for n in norms:
                n.tensor(pe)

            def first(i, k, j, made=True):
                unit = i * 4 + 2 * k + j
                out = au(k, j)
                pe.wait_ge(hi_1, unit + 1)
                for c in range(DC):
                    w = hi[:, j, c * P:(c + 1) * P]
                    for s, x in enumerate(streams):
                        if not made:
                            norms[s].wait_chunk(pe, c)
                        at = out[:, s * T:(s + 1) * T]
                        pe.matmul(at, w, x.pair[:, 0, c], start=c == 0 and s == 0, stop=False, skip_group_check=True)
                        pe.matmul(at, w, x.pair[:, 1, c], start=False, stop=False, skip_group_check=True)
                if made:
                    pe.wait_ge(lo_1, unit)
                else:
                    pe.wait_ge(lo_0, 1)
                for c in range(DC):
                    w = lo[:, j, c * P:(c + 1) * P]
                    for s, x in enumerate(streams):
                        mm = pe.matmul(out[:, s * T:(s + 1) * T], w, x.pair[:, 0, c], start=False,
                                       stop=c == DC - 1, skip_group_check=True)
                mm.then_inc(product, 1)

            for k in range(2):
                for j in range(2):
                    first(0, k, j, k + j > 0)
            with pe.Fori(1, FT // 2) as i:
                for k in range(2):
                    pe.wait_ge(gated, i * 2 + k - 1)
                    for j in range(2):
                        first(i, k, j)

            def second(f, k, start=False):
                pe.wait_ge(g_lo, f + 1)
                pe.wait_ge(hi_2, f + 1)
                gs = lambda cut, s: g[:, cut, bass.ds(f, 1), s * T:(s + 1) * T]
                for c in range(DC):
                    w = hi[:, k, c * P:(c + 1) * P]
                    for s in range(n_s):
                        pe.matmul(out_ps(s, c), w, gs(0, s), start=start and c % 2 == 0, stop=False,
                                  skip_group_check=True)
                        pe.matmul(out_ps(s, c), w, gs(1, s), start=False, stop=False, skip_group_check=True)
                pe.wait_ge(lo_2, f + 1)
                for c in range(DC):
                    for s in range(n_s):
                        mm = pe.matmul(out_ps(s, c), lo[:, k, c * P:(c + 1) * P], gs(0, s), start=False,
                                       stop=False, skip_group_check=True)
                mm.then_inc(out_sum, 1)

            if n_s == 2:
                pe.wait_ge(gated, FT)
            for k in range(2):
                second(k, k, k == 0)
            with pe.Fori(0, (FT - 2) // 4) as i:
                for k in range(4):
                    second(i * 4 + k + 2, k % 2)

        @block.scalar
        def _(act):
            for n, x in zip(norms, streams):
                if x.load is not None:
                    act.wait_ge(stream_in, 16)
                n.scalar_squares(act)

            def cut_first(i, k, j, fresh=False):
                act.wait_ge(w1_in[2 * k + j], i * 16 + 16)
                if not fresh:
                    act.wait_ge(product, i * 4 + 2 * k + j - 1)
                cut_hi(act, hi[:, j], raw[:, 2 * k + j]).then_inc(hi_1, 1)

            def silu(f, k, fresh=False):
                act.wait_ge(product, f * 2 + 1)
                if not fresh:
                    act.wait_ge(gated, f - 1)
                act.activation(sl[:, k], au(k, 0), ACT.Silu).then_inc(silued, 1)

            def cut_g(f, k):
                act.wait_ge(gated, f + 1)
                cut_hi(act, g[:, 0, bass.ds(f, 1)], gv[:, k:k + 1]).then_inc(g_hi, 1)

            for k in range(2):
                for j in range(2):
                    cut_first(0, k, j, k == 0)
                    if k == j == 0:
                        for n in norms:
                            n.scalar_root(act)
                    for c in range(DC):
                        for n in norms:
                            n.scalar_to(act, c + 1)
            silu(0, 0, True)

            def first_body(i, fresh=False):
                for k in range(2):
                    for j in range(2):
                        cut_first(i, k, j)
                    silu(i * 2 + k - 1, 1 - k, fresh and k == 0)
                    cut_g(i * 2 + k - 2, k)

            first_body(1, True)
            with act.Fori(2, FT // 2) as i:
                first_body(i)
            silu(FT - 1, 1)
            for f in (FT - 2, FT - 1):
                cut_g(f, f % 2)

            def cut_second(f, slot, last_load):
                act.wait_ge(w2_in[slot], last_load)
                cut_hi(act, hi[:, slot % 2], raw[:, slot]).then_inc(hi_2, 1)

            for f in range(2):
                act.wait_ge(product, 2 * FT - 1 + f)
                cut_second(f, f, 16)
            with act.Fori(0, (FT - 2) // 4) as i:
                for k in range(4):
                    act.wait_ge(out_sum, i * 4 + k + 1)
                    cut_second(i * 4 + k + 2, (k + 2) % raws, i * 16 + (16 if k < 2 else 32))

        @block.gpsimd
        def _(pool):
            pool.wait_ge(hi_1, 1)
            cut_lo(pool, lo[:, 0], raw[:, 0], hi[:, 0]).then_inc(lo_0, 1)
            for n in norms:
                n.gpsimd(pool)

        @block.vector
        def _(dve):
            for n, x in zip(norms, streams):
                if x.load is not None:
                    dve.wait_ge(stream_in, 16)
                n.vector_squares(dve)
            for n in norms:
                n.vector_root(dve)

            def low_first(i, k, j):
                dve.wait_ge(hi_1, i * 4 + 2 * k + j + 1)
                cut_lo(dve, lo[:, j], raw[:, 2 * k + j], hi[:, j]).then_inc(lo_1, 1)

            def gate(f, k, fresh=False):
                dve.wait_ge(silued, f + 1)
                if not fresh:
                    dve.wait_ge(g_lo, f - 1)
                dve.wait_ge(product, f * 2 + 2)
                dve.tensor_tensor(gv[:, k], au(k, 1), sl[:, k], ALU.mult).then_inc(gated, 1)

            def low_g(f, k):
                dve.wait_ge(g_hi, f + 1)
                cut_lo(dve, g[:, 1, bass.ds(f, 1)], gv[:, k:k + 1], g[:, 0, bass.ds(f, 1)]).then_inc(g_lo, 1)

            for k in range(2):
                for j in range(2):
                    if k + j > 0:
                        low_first(0, k, j)
                    for c in range(DC):
                        for n in norms:
                            n.vector_to(dve, c + 1)
            gate(0, 0, True)

            def first_body(i, fresh=False):
                for k in range(2):
                    for j in range(2):
                        low_first(i, k, j)
                    gate(i * 2 + k - 1, 1 - k, fresh and k == 0)
                    low_g(i * 2 + k - 2, k)

            first_body(1, True)
            with dve.Fori(2, FT // 2) as i:
                first_body(i)
            gate(FT - 1, 1)
            for f in (FT - 2, FT - 1):
                low_g(f, f % 2)

            def low_second(f, slot):
                dve.wait_ge(hi_2, f + 1)
                cut_lo(dve, lo[:, slot % 2], raw[:, slot], hi[:, slot % 2]).then_inc(lo_2, 1)

            for f in range(2):
                low_second(f, f)
            with dve.Fori(0, (FT - 2) // 4) as i:
                for k in range(4):
                    low_second(i * 4 + k + 2, (k + 2) % raws)
            dve.wait_ge(out_sum, FT)
            for s, x in enumerate(streams):
                for c in range(DC):
                    dve.scalar_tensor_tensor(out=x.x[:, c], in0=out_ps(s, c), scalar=x.gate[:, c:c + 1],
                                             in1=x.x[:, c], op0=ALU.mult, op1=ALU.add)


def window_gla(nc, K, dram, M, ctx, ctx_pair, beside):
    with ExitStack() as keep:
        def sb(name, shape, dt=F32):
            return keep.enter_context(nc.sbuf_tensor(f"wg_{name}", shape, dt))

        mix = sb("mix", [P, DC, T])
        K.rows = sb("rows", [P, NROW])
        w, x, xc = dram["w_in"], K.xp[:], ctx_pair[:]
        gq, gk, gv = sb("gq", [P, 2, T]), sb("gk", [P, 2, 2, T]), sb("gv", [P, 2, TT, 512])
        gr, zg = sb("gr", [P, 4, T]), sb("zg", [16, 2, 2, T])
        la = sb("la", [P, 2, 2, 2, T])
        with ExitStack() as early:
            def eb(name, shape, dt=F32):
                return early.enter_context(nc.sbuf_tensor(f"wg_{name}", shape, dt))

            q = eb("q", [P, TT, 512])
            kv = eb("kv", [P, 2, TT, 256])
            qt, kt = eb("qt", [P, 4, T]), eb("kt", [P, WG, 2 * T])
            table, mask = eb("table", [P, TT, 4, 16]), eb("mask", [P, TT, 2 * T])
            full = eb("full", [P, TT, 2 * T])
            blocks = [
                Proj(w, 0, 512, x, "t", q[:]), Proj(w, 512, 256, x, "t", kv[:, 0]), Proj(w, 512, 256, xc, "t", kv[:, 1], src=1),
                Proj(w, 768, 256, x, "f", gq[:]), Proj(w, 1024, 256, x, "f", gk[:, 0]),
                Proj(w, 1024, 256, xc, "f", gk[:, 1], src=1), Proj(w, 1280, 512, x, "t", gv[:, 0]),
                Proj(w, 1280, 512, xc, "t", gv[:, 1], src=1),
            ]
            blocks += [Proj(w, 2304 + 16 * d, 16, y, "f", zg[:, d, s:s + 1], src=s) for d in range(2) for s, y in ((0, x), (1, xc))]
            blocks += [Proj(w, 1792, 512, x, "f", gr[:], ACT.Silu)]
            project(nc, "wg_in", blocks, lambda st: [
                Norm(st, K, "n", K.x, M.gain(1), M.shift(1), pair=K.xp),
                Norm(st, K, "nc", ctx, M.gain(1, 1), M.shift(1, 1), pair=ctx_pair),
            ], [(table[:], dram["rope_table"]), (K.rows[:], dram["rows"].partition_broadcast(P))])
            with stage(nc, "wg_mask") as st:
                step = st.sem("step")
                beside = beside(st)
                block = st.ctx.enter_context(nc.Block())

                @block.vector
                def _(dve):
                    beside.vector(dve)

                @block.gpsimd
                def _(pool):
                    pool.memset(full[:], 0.0).then_inc(step, 1)
                    pool.memset(mask[:, :, T:2 * T], 0.0)
                    pool.wait_ge(step, 1)
                    pool.affine_select(out=full[:, :, 0:T], in_=full[:, :, 0:T], compare_op=ALU.is_ge, fill=NEG,
                                       base=P, pattern=[[P, TT], [-1, T]], channel_multiplier=1).then_inc(step, 1)
                    pool.wait_ge(step, 2)
                    pool.affine_select(out=mask[:, :, 0:T], in_=full[:, :, 0:T], compare_op=ALU.is_ge, fill=NEG,
                                       base=P, pattern=[[-P, TT], [1, T]], channel_multiplier=-1)

            q4 = q[:].rearrange("p t (h d) -> p t h d", h=WH)
            k4 = kv[:, 0, :, 0:128].rearrange("p t (h d) -> p t h d", h=WG)
            rope = ((0, table[:, :, 0], table[:, :, 1]), (32, table[:, :, 2], table[:, :, 3]))
            turns = [(0, q[:, :, P * i:P * (i + 1)], qt[:, i]) for i in range(4)]
            for g in range(WG):
                for at in (0, WD):
                    turns.append((1, k4[:, :, g], kt[at:at + WD, g, 0:T]))
                    turns.append((1, kv[:, 1, :, g * WD:(g + 1) * WD], kt[at:at + WD, g, T:2 * T]))
            token_norm_rope(nc, K, "wg_rope", [Tok(q4, None, rope, 16), Tok(k4, None, rope, 16)], turns,
                            lambda st: LogDecays(st, K, dram, zg, la))
            heads = []
            for i in range(WH):
                at, g = WD * (i % 2), i // (WH // WG)

                def v(c, g=g):
                    return kv[:, c // TT, c % TT, 128 + g * WD:128 + (g + 1) * WD]

                heads.append(Head([(qt[at:at + WD, i // 2], kt[at:at + WD, g])], v, mix[at:at + WD, i // 2],
                                  WD ** -0.5, K.row("sink_2")[:, i:i + 1]))
            attend(nc, K, "window", heads, 2 * T, [[0, 1, 2, 3]] * 2, mask)
        out = residual_units(K, sb("ring", [P, Units.RAWS, UNIT]), dram["w_out"], M.gate(1))
        gla(nc, K, gq, gk, gv, gr, la, mix, out)
        project_residual(nc, K, "wg_out", out, mix)


class LogDecays:

    def __init__(self, st, K, dram, zg, la):
        self.K, self.dram, self.zg, self.la = K, dram, zg, la
        self.loaded, self.product, self.biased, self.absed, self.exped, self.logged, self.v_step = (
            st.sem(f"decays_{x}") for x in
            ("loaded", "product", "biased", "absed", "exped", "logged", "v_step"))
        self.w = st.sb("decays_w", [16, 2, 256])
        self.z, self.neg, self.ab = (st.sb(f"decays_{x}", [P, 4, 2 * T]) for x in ("z", "neg", "ab"))
        self.acc = st.ps("decays_acc", [P, 4, 2 * T])

    def sync(self, sp):
        sp.dma_start(self.w[:], self.dram["w_a2"]).then_inc(self.loaded, 16)

    def tensor(self, pe):
        pe.wait_ge(self.loaded, 16)
        for n in range(4):
            d, s = divmod(n, 2)
            for f in range(2):
                mm = pe.matmul(self.acc[:, n, f * T:(f + 1) * T], self.w[:, d, f * P:(f + 1) * P],
                               self.zg[:, d, s], start=True, stop=True)
        mm.then_inc(self.product, 1)

    def scalar(self, act):
        act.wait_ge(self.product, 1)
        for n in range(4):
            b = self.K.col("b_a_f_2" if n < 2 else "b_a_b_2")
            for f in range(2):
                ins = act.activation(self.z[:, n, f * T:(f + 1) * T], self.acc[:, n, f * T:(f + 1) * T],
                                     ACT.Identity, bias=b[:, f:f + 1])
        ins.then_inc(self.biased, 1)
        act.wait_ge(self.biased, 1)
        act.activation(self.ab[:], self.z[:], ACT.Abs).then_inc(self.absed, 1)
        act.wait_ge(self.absed, 1)
        act.activation(self.neg[:], self.ab[:], ACT.Exp, scale=-1.0).then_inc(self.exped, 1)
        act.wait_ge(self.exped, 1)
        act.activation(self.ab[:], self.neg[:], ACT.Ln, bias=self.K.ones[:, 0:1]).then_inc(self.logged, 1)

    def vector(self, dve):
        chain = Chain(dve, self.v_step)
        dve.wait_ge(self.logged, 1)
        chain(dve.scalar_tensor_tensor(out=self.neg[:], in0=self.z[:], scalar=0.0, in1=self.ab[:], op0=ALU.min,
                                       op1=ALU.subtract))
        dve.tensor_scalar(self.la[:].rearrange("p d s f t -> p (d s) (f t)"), self.neg[:], 1.0 / 16.0, None, ALU.mult)


def gla(nc, K, q, k, v, gr, la, mix, next_units):
    with stage(nc, "gla") as st:
        made, v_step, decayed, exped = (st.sem(x) for x in ("made", "v_step", "decayed", "exped"))
        keyed, turned, copied, summed = (st.sem(x) for x in ("keyed", "turned", "copied", "summed"))
        queried = st.sem("queried")
        preloaded = [st.sem(f"preloaded{n}") for n in range(Units.RAWS)]
        scored, selected, stated, out_sum = (st.sem(x) for x in ("scored", "selected", "stated", "out_sum"))
        squared = st.sem("squared")
        upto = st.sb("upto", [P, 2, P])
        pairs = st.sb("pairs", [P, 2, P], I32)
        carry_on = st.sb("carry_on", [P, 4 * T + BC])
        g2 = st.sb("g", [P, 2, 2, 2, T])
        e2 = st.sb("e", [P, 2, 3, 2, 2, T])
        qg2, kg2, ke2 = st.sb("qg", [P, 2, 2, T]), st.sb("kg", [P, 2, 2, T]), st.sb("ke", [P, 2, 2, 2, T])
        dec2 = st.sb("dec", [P, 2, 4, NBC])
        att2 = st.sb("att", [P, 2, 2, 2, TT, P])
        ket = st.sb("ket", [P, 2, 2, TT, P])
        carry = st.sb("carry", [P, 2, P])
        states2 = st.sb("states", [P, 2, NBC, 2, P])
        sq, gated = st.sb("sq", [P, 2, 2, T]), st.sb("gated", [P, 2, 2, T])
        t_ps = st.ps("t", [P, 2, 512])
        d_ps = st.ps("d", [P, 4, 512])
        o_ps = st.ps("o", [P, 2, 2, T])
        block = st.ctx.enter_context(nc.Block())
        head_norms = HeadNorms(st, K, sq[:].rearrange("p a b t -> p (a b t)"), d_ps[:, 0, 0:4 * TT],
                               t_ps[:].rearrange("p a t -> p (a t)"))
        sixteenth = lambda a: a.rearrange("p s f (n t) -> p (s f n) t", t=BC)
        flat = lambda a: a.rearrange("p s f t -> p (s f t)")
        add_of = lambda s, n, f: d_ps[:, 2 * s + n % 2, ((n // 2) * 2 + f) * P:((n // 2) * 2 + f + 1) * P]

        @block.sync
        def _(sp):
            next_units.preload(sp, preloaded)

        @block.gpsimd
        def _(pool):
            pool.memset(carry_on[:], 1.0).then_inc(made, 1)
            pool.memset(upto[:], 1.0).then_inc(made, 1)
            pool.wait_ge(made, 2)
            pool.memset(carry_on[:].rearrange("p (n t) -> p n t", t=BC)[:, :, 0:1], 0.0).then_inc(made, 1)
            pool.affine_select(out=upto[:, 0], in_=upto[:, 0], compare_op=ALU.is_ge, fill=0.0, base=0,
                               pattern=[[1, P]], channel_multiplier=-1).then_inc(made, 1)
            pool.affine_select(out=upto[:, 1], in_=upto[:, 1], compare_op=ALU.is_ge, fill=0.0, base=0,
                               pattern=[[-1, P]], channel_multiplier=1).then_inc(made, 1)
            pool.wait_ge(made, 5)
            pool.memset(upto[0:BC, 0, BC:P], 0.0).then_inc(made, 1)
            pool.memset(upto[BC:P, 1, 0:BC], 0.0).then_inc(made, 1)
            pool.wait_ge(made, 7)
            pool.memset(att2[:], 0.0).then_inc(made, 1)

        @block.vector
        def _(dve):
            chain = Chain(dve, v_step)
            dve.wait_ge(made, 3)
            for d in range(2):
                g, e = g2[:, d], e2[:, d]
                last = BC - 1 if d == 0 else 0
                if d == 0:
                    chain(dve.tensor_tensor_scan(flat(g), carry_on[:, 0:4 * T], flat(la[:, d]), 0.0,
                                                 ALU.mult, ALU.add))
                else:
                    chain(dve.tensor_tensor_scan(flat(g)[:, ::-1], carry_on[:, 1:4 * T + 1][:, ::-1],
                                                 flat(la[:, d])[:, ::-1], 0.0, ALU.mult, ALU.add))
                gl = sixteenth(g)[:, :, last:last + 1]
                dve.tensor_tensor(sixteenth(e[:, 2]), gl.to_broadcast([P, 16, BC]), sixteenth(g), ALU.subtract)\
                    .then_inc(decayed, 1)
            for d in range(2):
                e = e2[:, d]
                dve.wait_ge(exped, d + 1)
                dve.tensor_tensor(ke2[:, d], k[:], e[:, 2], ALU.mult).then_inc(keyed, 1)
                dve.scalar_tensor_tensor(out=qg2[:, d], in0=q[:], scalar=float(BC) ** -0.5, in1=e[:, 0, 0],
                                         op0=ALU.mult, op1=ALU.mult)
                dve.tensor_tensor(kg2[:, d], k[:, 0], e[:, 1, 0], ALU.mult).then_inc(queried, 1)
            dve.wait_ge(made, 8)
            chain(dve.tensor_copy(pairs[:], upto[:]))
            for d in range(2):
                att, states, dec = att2[:, d], states2[:, d], dec2[:, d]
                dve.wait_ge(scored, d + 1)
                dve.copy_predicated(att.rearrange("p a b t i -> p (a b t) i"),
                                    pairs[:, d].unsqueeze(1).to_broadcast([P, 8, P]),
                                    t_ps[:].rearrange("p a (b i) -> p (a b) i", i=P)).then_inc(selected, 1)
                chain(dve.memset(carry[:], 0.0))
                order = list(range(NBC)) if d == 0 else list(range(NBC))[::-1]
                for s in (1, 0):
                    for i, n in enumerate(order):
                        if s == 0 and i == 0:
                            chain(dve.tensor_copy(states[:, n], carry[:]))
                        if s == 0 and i == NBC - 1:
                            break
                        src = carry if s == 1 else states[:, n]
                        dst = carry if s == 1 else states[:, order[i + 1]]
                        for f in range(2):
                            ins = dve.scalar_tensor_tensor(out=dst[:, f], in0=src[:, f],
                                                           scalar=dec[:, 2 * s + f, n:n + 1],
                                                           in1=add_of(s, n, f), op0=ALU.mult, op1=ALU.add)
                        chain(ins)
                dve.engine_nop().then_inc(stated, 1)
            dve.wait_ge(squared, 1)
            for h in range(4):
                ins = dve.scalar_tensor_tensor(out=gated[:, h % 2, h // 2], in0=o_ps[:, h % 2, h // 2],
                                               scalar=K.col("gla_g_2"), in1=gr[:, h], op0=ALU.mult, op1=ALU.mult)
            chain(ins)
            head_norms.vector(dve)
            dve.wait_ge(head_norms.spread, 1)
            for par in range(2):
                dve.tensor_tensor(mix[:, 4 + par:8:2], t_ps[:, par].rearrange("p (f t) -> p f t", f=2), gated[:, par],
                                  ALU.mult)

        @block.scalar
        def _(act):
            for d in range(2):
                g, e = g2[:, d], e2[:, d]
                last = BC - 1 if d == 0 else 0
                act.wait_ge(decayed, d + 1)
                act.activation(e[:, 2], e[:, 2], ACT.Exp)
                act.activation(dec2[:, d], g.rearrange("p s f (n t) -> p (s f) n t", t=BC)[:, :, :, last], ACT.Exp)
                act.activation(e[:, 0, 0], g[:, 0], ACT.Exp)
                act.activation(e[:, 1, 0], g[:, 0], ACT.Exp, scale=-1.0).then_inc(exped, 1)
            for d in range(2):
                act.wait_ge(turned, d + 1)
                if d:
                    act.wait_ge(summed, d)
                act.activation(ket[:].rearrange("p s f t e -> p s (f t e)"), t_ps[:], ACT.Copy).then_inc(copied, 1)
            act.wait_ge(out_sum, 2)
            act.activation(sq[:], o_ps[:], ACT.Square).then_inc(squared, 1)
            head_norms.scalar(act)

        @block.tensor
        def _(pe):
            def turn(d):
                pe.wait_ge(keyed, d + 1)
                if d:
                    pe.wait_ge(selected, d)
                for s in range(2):
                    for f in range(2):
                        for t in range(TT):
                            mm = pe.transpose(t_ps[:, s, (2 * f + t) * P:(2 * f + t + 1) * P],
                                              ke2[:, d, s, f, t * P:(t + 1) * P], K.ident[:])
                mm.then_inc(turned, 1)

            def add(d):
                pe.wait_ge(copied, d + 1)
                if d:
                    pe.wait_ge(stated, d)
                for par in range(2):
                    for s in range(2):
                        for n in range(par, NBC, 2):
                            rows = slice(BC * par, BC * par + BC)
                            for h in range(4):
                                f, at = h // 2, BC * (h % 2)
                                mm = pe.matmul(add_of(s, n, f)[at:at + BC], ket[rows, s, f, n // 2, at:at + BC],
                                               v[rows, s, n // 2, h * P:(h + 1) * P], start=True, stop=True)
                mm.then_inc(summed, 1)

            def score(d):
                pe.wait_ge(queried, d + 1)
                for par in range(2):
                    rows = slice(BC * par, BC * par + BC)
                    for f in range(2):
                        for t in range(TT):
                            mm = pe.matmul(t_ps[:, par, (2 * f + t) * P:(2 * f + t + 1) * P],
                                           kg2[rows, d, f, t * P:(t + 1) * P], qg2[rows, d, f, t * P:(t + 1) * P],
                                           start=True, stop=True)
                mm.then_inc(scored, 1)

            def own(d):
                pe.wait_ge(selected, d + 1)
                for par in range(2):
                    for f in range(2):
                        for t in range(TT):
                            h = 2 * f + par
                            pe.matmul(o_ps[:, par, f, t * P:(t + 1) * P], v[:, 0, t, h * P:(h + 1) * P],
                                      att2[:, d, par, f, t], start=d == 0 and f == 0 and t == 0, stop=False,
                                      skip_group_check=True)

            def carried(d):
                pe.wait_ge(stated, d + 1)
                for par in range(2):
                    rows = slice(BC * par, BC * par + BC)
                    for f in range(2):
                        for n in range(NBC):
                            mm = pe.matmul(o_ps[:, par, f, n * BC:(n + 1) * BC], states2[rows, d, n, f],
                                           qg2[rows, d, f, n * BC:(n + 1) * BC], start=False, stop=d == 1,
                                           skip_group_check=True)
                mm.then_inc(out_sum, 1)

            turn(0)
            add(0)
            score(0)
            turn(1)
            own(0)
            add(1)
            carried(0)
            score(1)
            own(1)
            carried(1)
            pe.wait_ge(squared, 1)
            head_norms.tensor(pe)


def pool_mix(nc, K, dram, M):
    pad = 16
    wide = T + 2 * pad
    with stage(nc, "pool") as st:
        w_in, inv_in, cleared, v_step, product, ready = (
            st.sem(x) for x in ("w_in", "inv_in", "cleared", "v_step", "product", "ready"))
        w = st.sb("w", [P, 4, 2, T])
        inv = st.sb("inv", [P, 4, T])
        a, b, b2 = (st.sb(x, [P, DC, wide]) for x in ("a", "b", "b2"))
        pooled = st.sb("pooled", [P, DC, T])
        acc = st.ps("acc", [P, DC, T])
        h = a[:, :, pad:pad + T]
        norm = Norm(st, K, "n", K.x, M.gain(1), M.shift(1), raw=h)
        block = st.ctx.enter_context(nc.Block())

        @block.sync
        def _(sp):
            sp.dma_start(w[:], dram["w_pool"].rearrange("g (c p) e -> p g c e", p=P)).then_inc(w_in, 16)
            sp.dma_start(inv[:], dram["pool_inv"].partition_broadcast(P)).then_inc(inv_in, 16)

        @block.gpsimd
        def _(pool):
            for x in (a, b, b2):
                pool.memset(x[:, :, 0:pad], 0.0)
                pool.memset(x[:, :, pad + T:], 0.0).then_inc(cleared, 1)

        @block.vector
        def _(dve):
            chain = Chain(dve, v_step)
            norm.vector_squares(dve)
            dve.wait_ge(cleared, 3)
            norm.vector_root(dve)
            norm.vector_to(dve, DC)
            dve.wait_ge(norm.done_v, DC)
            dve.wait_ge(inv_in, 16)
            src, dst, other = a, b, b2
            for g, (back, ahead) in enumerate(((1, 0), (1, 1), (2, 2), (4, 4))):
                lo, hi = 8, wide - 8
                chain(dve.tensor_tensor(dst[:, 2 * g:, lo:hi], src[:, 2 * g:, lo - back:hi - back],
                                        src[:, 2 * g:, lo + ahead:hi + ahead], ALU.add))
                cs = slice(2 * g, 2 * g + 2)
                chain(dve.tensor_tensor(pooled[:, cs], dst[:, cs, pad:pad + T],
                                        inv[:, g:g + 1].to_broadcast([P, 2, T]), ALU.mult))
                dve.tensor_tensor(pooled[:, cs], pooled[:, cs], h[:, cs], ALU.subtract).then_inc(ready, 1)
                src, dst, other = dst, other, dst
            for g in range(4):
                dve.wait_ge(product, g + 1)
                for c in (2 * g, 2 * g + 1):
                    dve.scalar_tensor_tensor(out=K.x[:, c], in0=acc[:, c], scalar=M.gate(1)[:, c:c + 1], in1=K.x[:, c],
                                             op0=ALU.mult, op1=ALU.add)

        @block.tensor
        def _(pe):
            norm.tensor(pe)
            pe.wait_ge(w_in, 16)
            for g in range(4):
                pe.wait_ge(ready, g + 1)
                for j in range(2):
                    for c in range(2):
                        mm = pe.matmul(acc[:, 2 * g + j], w[:, g, c, j * P:(j + 1) * P], pooled[:, 2 * g + c],
                                       start=c == 0, stop=c == 1)
                mm.then_inc(product, 1)

        @block.scalar
        def _(act):
            norm.scalar_squares(act)
            norm.scalar_root(act)


def second_block(nc, K, dram, mods, out):
    for layer, M in enumerate(mods):
        first = Stream(K.x, M.gain(0), M.shift(0), M.gate(0), K.xp)
        weights = dram["ffn1_wi"][layer], dram["ffn1_wo"][layer]
        if layer == 0:
            with nc.sbuf_tensor("ctx_stream", [P, DC, T], F32) as ctx, \
                    nc.sbuf_tensor("ctx_normed", [P, 2, DC, T], F32R) as ctx_pair:
                swiglu(nc, K, "ffn1_0", *weights, [
                    first, Stream(ctx, M.gain(0, 1), M.shift(0, 1), M.gate(0, 1), ctx_pair, dram["ctx"])])
                window_gla(nc, K, dram, M, ctx, ctx_pair, mods[1])
        else:
            swiglu(nc, K, "ffn1_1", *weights, [first])
            pool_mix(nc, K, dram, M)
        swiglu(nc, K, f"ffn2_{layer}", dram["ffn2_wi"][layer], dram["ffn2_wo"][layer],
               [Stream(K.x, M.gain(2), M.shift(2), M.gate(2), K.xp)])
    finish(nc, K, out)


def finish(nc, K, out):
    with stage(nc, "finish") as st:
        stored = st.sem("stored")
        y = st.sb("y", [P, DC, T])
        norm = Norm(st, K, "n", K.x, K.col("final_g_2"), raw=y)
        block = st.ctx.enter_context(nc.Block())

        @block.sync
        def _(sp):
            for c in range(0, DC, 4):
                sp.wait_ge(norm.done_v, c + 4)
                sp.dma_start(out[:, c:c + 4], y[:, c:c + 4]).then_inc(stored, 16)
            sp.wait_ge(stored, 16 * 2)

        @block.tensor
        def _(pe):
            norm.tensor(pe)

        @block.scalar
        def _(act):
            norm.scalar_squares(act)
            norm.scalar_root(act)

        @block.vector
        def _(dve):
            norm.vector_squares(dve)
            norm.vector_root(dve)
            norm.vector_to(dve, DC)


def program(nc, dram, out):
    with ExitStack() as keep:
        K = Store()
        setup(nc, keep, dram, K)
        hgrn_gmlp(nc, K, dram)
        mods = [Modulation(K, layer) for layer in range(2)]
        peer(nc, K, dram, 0, lambda st: Angles(st, K, dram))
        mla_moba(nc, K, dram)
        peer(nc, K, dram, 1, mods[0])
        second_block(nc, K, dram, mods, out)


def by_column(a):
    return np.asarray(a).reshape(-1, P).T


def layouts(a):
    feature_major = lambda x: np.ascontiguousarray(x[0].T.reshape(DC, P, T).transpose(1, 0, 2))
    half = np.arange(ROPE // 2, dtype=np.float32) / (ROPE // 2)
    inv_freq = np.float32(10000.0) ** (-half)
    rows = [inv_freq if name == "inv_freq" else np.asarray(a[name]).reshape(-1) for name, _ in ROWS]
    freqs = np.float32(10000.0) ** (-np.arange(16, dtype=np.float32) / np.float32(16))
    t = np.arange(T, dtype=np.float32)
    at = [(np.floor(t / 64)[:, None] * freqs).astype(np.float32), ((t % 64)[:, None] * freqs).astype(np.float32)]
    table = np.stack([f(x) for x in at for f in (np.cos, np.sin)], 1).astype(np.float32)
    counts = [np.minimum(t + w // 2, T) - np.maximum(t - w // 2, 0) for w in (2, 4, 8, 16)]
    out = {
        "x": feature_major(a["x"]),
        "ctx": feature_major(a["ctx_2"]),
        "cols": np.concatenate([by_column(a[name]) for name, _ in COLS], 1),
        "rows": np.concatenate(rows),
        "positions": a["positions"].reshape(TT, P).T,
        "l0_w_in": a["l0_w_in"], "l0_w_out": a["l0_w_out"], "l1_w_in": a["l1_w_in"], "l1_w_out": a["l1_w_out"],
        "w_s": a["l0_gmlp_w_s"].transpose(2, 0, 1),
        "l1_mla_w_uq": a["l1_mla_w_uq"], "l1_mla_w_ukv": a["l1_mla_w_ukv"],
        "w_mod": a["w_mod_2"].transpose(0, 2, 1).reshape(2, MT, P, D),
        "cond": np.stack([a["c_2"].reshape(D), a["c_ctx_2"].reshape(D)]),
        "w_in": a["w_in_2"][0], "w_out": a["w_out_2"][0],
        "w_a2": np.stack([a["w_a2_f_2"][0], a["w_a2_b_2"][0]], 1),
        "rope_table": table.reshape(TT, P, 4, 16).transpose(1, 0, 2, 3),
        "w_pool": a["w_pool_2"][0],
        "pool_inv": np.stack([np.float32(1) / c for c in counts]).astype(np.float32),
    }
    for n in ("ffn1", "ffn2"):
        out[f"{n}_wi"] = a[f"{n}_wi_2"].reshape(2, DC, P, 2, FT, P).transpose(0, 4, 2, 3, 1, 5)\
            .reshape(2, FT, P, 2, DC * P)
        out[f"{n}_wo"] = a[f"{n}_wo_2"].reshape(2, FT, P, D)
    for n in ("l0", "l1"):
        out[f"{n}_peer_w_query"] = a[f"{n}_peer_w_query"]
        out[f"{n}_sub_keys"] = a[f"{n}_peer_sub_keys"].transpose(3, 0, 1, 2).reshape(P, HP, NK)
        out[f"{n}_down"] = a[f"{n}_peer_expert_down"].reshape(NK, NK, DC, P).transpose(1, 3, 2, 0)\
            .reshape(NK, P, DC * NK)
        out[f"{n}_up"] = a[f"{n}_peer_expert_up"].reshape(NK, NK, D)
    return {name: np.ascontiguousarray(x) for name, x in out.items()}


def kernel(**inputs):
    import concourse.bacc as bacc
    from concourse.bass_utils import run_bass_kernel_spmd as run

    arrays = layouts({name: np.asarray(x) for name, x in inputs.items()})
    nc = bacc.Bacc("TRN2", target_bir_lowering=False, num_devices=1)
    dram = {name: nc.dram_tensor(f"in_{name}", x.shape, mybir.dt.from_np(x.dtype), kind="ExternalInput").ap()
            for name, x in arrays.items()}
    out = nc.dram_tensor("out", [P, DC, T], F32, kind="ExternalOutput").ap()
    dram["scores"] = nc.dram_tensor("scores", [2, P, TT, HP, NK], F32, kind="Internal").ap()
    program(nc, dram, out)
    result = run(nc, [{f"in_{name}": x for name, x in arrays.items()}], core_ids=[0])
    y = np.asarray(result.results[0]["out"])
    return np.ascontiguousarray(y.transpose(1, 0, 2).reshape(D, T).T)[None]
```
